# Optimizing a Trainium2 kernel written in Bass

```python
import jax, jax.numpy as jnp
from jax import lax
import numpy as np

D_MODEL = 1024
BATCH = 1
SEQ = 512
DEPTH = 1
DEC_BATCH = 8
DEC_SEQ = 1
PAST_LEN = 2048
PAGE_SIZE = 128

N_META = 16
HA = 8
DK_A = 128
DV_A = 128
D_A = HA * DV_A
D_QKV_A = 3 * D_A
CONV_W = 4
CHUNK = 64
HB = 8
DH_B = 128
D_B = HB * DH_B
Q_BLOCK = 128
SB_SCALE = DH_B ** -0.5
D_FF = (((8 * D_MODEL + 2) // 3 + 255) // 256) * 256
D_IN = D_QKV_A + D_A + 2 * HA + 3 * D_B + 2 * D_MODEL
EPS = 1e-6
F32 = jnp.float32

kernel_name = 'hybrid_gdn_stickbreaking_decode_step'

def rmsnorm(x, w):
    xf = x.astype(F32)
    y = xf * lax.rsqrt(jnp.mean(xf * xf, axis=-1, keepdims=True) + EPS)
    return (y * w.astype(F32)).astype(x.dtype)

def l2norm(x):
    return x * lax.rsqrt(jnp.sum(x * x, axis=-1, keepdims=True) + EPS)

def mixer_inputs(h, norm_w, w_in):
    p = rmsnorm(h, norm_w) @ w_in
    bounds = np.cumsum([D_QKV_A, D_A, HA, HA, D_B, D_B, D_B, D_MODEL]).tolist()
    return jnp.split(p, bounds, axis=-1)

def causal_conv(buf, u, w):
    t_len = u.shape[1]
    up = jnp.concatenate([buf.astype(u.dtype), u], axis=1)
    y = sum(w[i] * up[:, i:i + t_len] for i in range(CONV_W))
    return jax.nn.silu(y), up[:, up.shape[1] - (CONV_W - 1):]

def gdn_prepare(buf, qkv, a, b, conv_w, a_log, dt_bias):
    qkv_c, new_buf = causal_conv(buf, qkv, conv_w)
    bn, t_len = qkv.shape[:2]

    def heads(t):
        return jnp.transpose(t.reshape(bn, t_len, HA, -1).astype(F32), (0, 2, 1, 3))

    q, k, v = (heads(t) for t in jnp.split(qkv_c, 3, axis=-1))
    q = l2norm(q) * (DK_A ** -0.5)
    k = l2norm(k)
    g = -jnp.exp(a_log.astype(F32)) * jax.nn.softplus(a.astype(F32) + dt_bias.astype(F32))
    beta = jax.nn.sigmoid(b.astype(F32))
    return q, k, v, jnp.transpose(g, (0, 2, 1)), jnp.transpose(beta, (0, 2, 1)), new_buf

def gdn_chunk(S, xs):
    q, k, v, g, beta = xs
    c = q.shape[2]
    incl = jnp.tril(jnp.ones((c, c), dtype=bool))
    strict = jnp.tril(jnp.ones((c, c), dtype=bool), -1)
    G = jnp.cumsum(g, axis=-1)
    decay = jnp.exp(jnp.where(incl, G[..., :, None] - G[..., None, :], -jnp.inf))
    a_mat = jnp.where(strict, beta[..., :, None] * jnp.einsum('bhid,bhjd->bhij', k, k) * decay, 0.0)
    lmat = a_mat + jnp.eye(c, dtype=F32)
    rhs = jnp.concatenate([beta[..., None] * v, (beta * jnp.exp(G))[..., None] * k], axis=-1)
    sol = lax.linalg.triangular_solve(lmat, rhs, left_side=True, lower=True, unit_diagonal=True)
    u, w = sol[..., :DV_A], sol[..., DV_A:]
    v_new = u - jnp.einsum('bhck,bhkv->bhcv', w, S)
    qk = jnp.einsum('bhid,bhjd->bhij', q, k) * decay
    o = jnp.einsum('bhck,bhkv->bhcv', q * jnp.exp(G)[..., None], S) + jnp.einsum('bhij,bhjv->bhiv', qk, v_new)
    g_last = G[..., -1]
    S_new = jnp.exp(g_last)[..., None, None] * S + jnp.einsum(
        'bhck,bhcv->bhkv', k * jnp.exp(g_last[..., None] - G)[..., None], v_new)
    return S_new, o

def gdn_scan(S0, q, k, v, g, beta, chunk):
    b, h, t_len = g.shape
    n = t_len // chunk

    def to_chunks(t):
        return jnp.moveaxis(t.reshape((b, h, n, chunk) + t.shape[3:]), 2, 0)

    S, o = lax.scan(gdn_chunk, S0, tuple(to_chunks(t) for t in (q, k, v, g, beta)))
    return S, jnp.moveaxis(o, 0, 2).reshape(b, h, t_len, DV_A)

def gdn_finish(o, z, norm_w):
    o = jnp.transpose(o, (0, 2, 1, 3))
    o = o * lax.rsqrt(jnp.mean(o * o, axis=-1, keepdims=True) + EPS) * norm_w.astype(F32)
    zf = z.reshape(o.shape).astype(F32)
    return (o * jax.nn.silu(zf)).reshape(o.shape[0], o.shape[1], D_A).astype(z.dtype)

def sb_weights(z, valid):
    log_stay = jnp.where(valid, jax.nn.log_sigmoid(-z), 0.0)
    log_after = lax.cumsum(log_stay, axis=z.ndim - 1, reverse=True) - log_stay
    return jnp.where(valid, jnp.exp(jax.nn.log_sigmoid(z) + log_after), 0.0)

def sb_logits(q, k, bias):
    return (jnp.einsum('bqhd,bkhd->bhqk', q, k).astype(F32) * SB_SCALE
            + bias.astype(F32)[None, :, None, None])

def sb_attend(qb, qpos, k, v, kpos, bias):
    z = sb_logits(qb, k, bias)
    a = sb_weights(z, kpos[None, :] < qpos[:, None])
    return jnp.einsum('bhqk,bkhd->bqhd', a.astype(v.dtype), v)

def sb_prompt(q, k, v, bias):
    b, l_len = q.shape[:2]
    seq = l_len - N_META
    kpos = jnp.arange(l_len)
    o_meta = sb_attend(q[:, :N_META], kpos[:N_META], k[:, :N_META], v[:, :N_META], kpos[:N_META], bias)
    n_blk = seq // Q_BLOCK
    qr = jnp.moveaxis(q[:, N_META:].reshape(b, n_blk, Q_BLOCK, HB, DH_B), 1, 0)
    qpos = (N_META + jnp.arange(seq)).reshape(n_blk, Q_BLOCK)
    o_real = lax.map(lambda xs: sb_attend(xs[0], xs[1], k, v, kpos, bias), (qr, qpos))
    o_real = jnp.moveaxis(o_real, 0, 1).reshape(b, seq, HB, DH_B)
    return jnp.concatenate([o_meta, o_real], axis=1)

def sb_sample(q, k_new, v_new, cache_k, cache_v, page_table, bias):
    b, t_len = q.shape[:2]
    past = page_table.shape[1] * PAGE_SIZE
    kp = cache_k[page_table].reshape(b, past, HB, DH_B).astype(q.dtype)
    vp = cache_v[page_table].reshape(b, past, HB, DH_B).astype(q.dtype)
    z = jnp.concatenate([sb_logits(q, kp, bias), sb_logits(q, k_new, bias)], axis=-1)
    qpos = past + jnp.arange(t_len)
    kpos = jnp.arange(past + t_len)
    a = sb_weights(z, kpos[None, :] < qpos[:, None]).astype(q.dtype)
    return (jnp.einsum('bhqk,bkhd->bqhd', a[..., :past], vp)
            + jnp.einsum('bhqk,bkhd->bqhd', a[..., past:], v_new))

def merge_out(o_a, o_b, gate_a, gate_b, w_pa, w_pb, w_o):
    m = jax.nn.sigmoid(gate_a) * (o_a @ w_pa) + jax.nn.sigmoid(gate_b) * (o_b @ w_pb)
    return m @ w_o

def ffn_block(h, norm_w, w_in, w_out):
    gt, up = jnp.split(rmsnorm(h, norm_w) @ w_in, 2, axis=-1)
    return h + (jax.nn.silu(gt) * up) @ w_out

def setup_inputs(seed: int = 0) -> dict:
    key = jax.random.key(seed)
    ks = jax.random.split(key, 24)
    n_pages = PAST_LEN // PAGE_SIZE
    n_phys = (DEC_BATCH * n_pages * 5 + 3) // 4

    def nrm(k, shape, s):
        return jax.random.normal(k, shape, F32) * s

    page_table = jax.random.permutation(ks[6], n_phys)[:DEC_BATCH * n_pages].reshape(
        DEC_BATCH, n_pages).astype(jnp.int32)
    return {
        'x_prompt': nrm(ks[0], (BATCH, SEQ, D_MODEL), 1.0),
        'x_sample': nrm(ks[1], (DEC_BATCH, DEC_SEQ, D_MODEL), 1.0),
        'cache_k': nrm(ks[2], (DEPTH, n_phys, PAGE_SIZE, HB, DH_B), 1.0),
        'cache_v': nrm(ks[3], (DEPTH, n_phys, PAGE_SIZE, HB, DH_B), 1.0),
        'state_rec': nrm(ks[4], (DEPTH, DEC_BATCH, HA, DK_A, DV_A), 0.1),
        'state_conv': nrm(ks[5], (DEPTH, DEC_BATCH, CONV_W - 1, D_QKV_A), 1.0),
        'page_table': page_table,
        'meta_tokens': nrm(ks[7], (N_META, D_MODEL), 1.0),
        'norm_mix': 1.0 + nrm(ks[8], (DEPTH, D_MODEL), 0.01),
        'w_in': nrm(ks[9], (DEPTH, D_MODEL, D_IN), D_MODEL ** -0.5),
        'conv_w': nrm(ks[10], (DEPTH, CONV_W, D_QKV_A), CONV_W ** -0.5),
        'a_log': jnp.log(jax.random.uniform(ks[11], (DEPTH, HA), F32, 1.0, 16.0)),
        'dt_bias': -4.0 + nrm(ks[12], (DEPTH, HA), 0.5),
        'gdn_norm': 1.0 + nrm(ks[13], (DEPTH, DV_A), 0.01),
        'sb_bias': -6.0 + nrm(ks[21], (DEPTH, HB), 0.5),
        'w_pa': nrm(ks[14], (DEPTH, D_A, D_MODEL), D_A ** -0.5),
        'w_pb': nrm(ks[15], (DEPTH, D_B, D_MODEL), D_B ** -0.5),
        'w_o': nrm(ks[16], (DEPTH, D_MODEL, D_MODEL), D_MODEL ** -0.5),
        'norm_ffn': 1.0 + nrm(ks[17], (DEPTH, D_MODEL), 0.01),
        'w_ffn_in': nrm(ks[18], (DEPTH, D_MODEL, 2 * D_FF), D_MODEL ** -0.5),
        'w_ffn_out': nrm(ks[19], (DEPTH, D_FF, D_MODEL), D_FF ** -0.5),
        'norm_final': 1.0 + nrm(ks[20], (D_MODEL,), 0.01),
    }

def reference(x_prompt, x_sample, cache_k, cache_v, state_rec, state_conv, page_table, meta_tokens,
              norm_mix, w_in, conv_w, a_log, dt_bias, gdn_norm, sb_bias, w_pa, w_pb, w_o,
              norm_ffn, w_ffn_in, w_ffn_out, norm_final):
    b, seq = x_prompt.shape[:2]
    bd, t_dec = x_sample.shape[:2]
    l_len = N_META + seq
    hp = jnp.concatenate([jnp.broadcast_to(meta_tokens.astype(x_prompt.dtype)[None], (b, N_META, D_MODEL)),
                          x_prompt], axis=1)
    hs = x_sample
    k_p, v_p, k_s, v_s, rec_p, rec_s, conv_p, conv_s = ([] for _ in range(8))
    for l in range(DEPTH):
        qkv_a, z_a, a_a, b_a, q_b, k_b, v_b, g_a, g_b = mixer_inputs(hp, norm_mix[l], w_in[l])
        q, k, v, g, beta, buf = gdn_prepare(jnp.zeros((b, CONV_W - 1, D_QKV_A), hp.dtype),
                                            qkv_a, a_a, b_a, conv_w[l], a_log[l], dt_bias[l])
        S, o_meta = gdn_scan(jnp.zeros((b, HA, DK_A, DV_A), F32),
                             *(t[:, :, :N_META] for t in (q, k, v, g, beta)), chunk=N_META)
        S, o_real = gdn_scan(S, *(t[:, :, N_META:] for t in (q, k, v, g, beta)), chunk=CHUNK)
        o_a = gdn_finish(jnp.concatenate([o_meta, o_real], axis=2), z_a, gdn_norm[l])
        qh, kh, vh = (t.reshape(b, l_len, HB, DH_B) for t in (q_b, k_b, v_b))
        o_b = sb_prompt(qh, kh, vh, sb_bias[l]).reshape(b, l_len, D_B)
        hp = hp + merge_out(o_a, o_b, g_a, g_b, w_pa[l], w_pb[l], w_o[l])
        hp = ffn_block(hp, norm_ffn[l], w_ffn_in[l], w_ffn_out[l])
        k_p.append(kh.astype(cache_k.dtype))
        v_p.append(vh.astype(cache_v.dtype))
        rec_p.append(S.astype(state_rec.dtype))
        conv_p.append(buf.astype(state_conv.dtype))

        qkv_a, z_a, a_a, b_a, q_b, k_b, v_b, g_a, g_b = mixer_inputs(hs, norm_mix[l], w_in[l])
        q, k, v, g, beta, buf = gdn_prepare(state_conv[l], qkv_a, a_a, b_a, conv_w[l], a_log[l], dt_bias[l])
        S, o_s = gdn_scan(state_rec[l].astype(F32), q, k, v, g, beta, chunk=t_dec)
        o_a = gdn_finish(o_s, z_a, gdn_norm[l])
        qh, kh, vh = (t.reshape(bd, t_dec, HB, DH_B) for t in (q_b, k_b, v_b))
        o_b = sb_sample(qh, kh, vh, cache_k[l], cache_v[l], page_table, sb_bias[l]).reshape(bd, t_dec, D_B)
        hs = hs + merge_out(o_a, o_b, g_a, g_b, w_pa[l], w_pb[l], w_o[l])
        hs = ffn_block(hs, norm_ffn[l], w_ffn_in[l], w_ffn_out[l])
        k_s.append(kh.astype(cache_k.dtype))
        v_s.append(vh.astype(cache_v.dtype))
        rec_s.append(S.astype(state_rec.dtype))
        conv_s.append(buf.astype(state_conv.dtype))

    y_prompt = rmsnorm(hp[:, N_META:], norm_final)
    y_sample = rmsnorm(hs, norm_final)
    return (y_prompt, y_sample, jnp.stack(k_p), jnp.stack(v_p), jnp.stack(k_s), jnp.stack(v_s),
            jnp.stack(rec_p), jnp.stack(rec_s), jnp.stack(conv_p), jnp.stack(conv_s))


_drawn_inputs = setup_inputs


def setup_inputs(seed=0):
    import zlib

    import numpy as np

    out = dict(_drawn_inputs(seed))
    spreads = {}
    factors = {'norm_mix': 3.907, 'gdn_norm': 8.0, 'sb_bias': 8.0, 'norm_ffn': 8.0, 'norm_final': 5.915}
    for name, (base, spread) in spreads.items():
        noise = np.random.default_rng([zlib.crc32(name.encode()), seed]).standard_normal(out[name].shape)
        drawn = base * np.exp(spread * noise) if base else spread * noise
        out[name] = __import__('jax').numpy.asarray(drawn.astype(out[name].dtype))
    for name, factor in factors.items():
        out[name] = (out[name] * factor).astype(out[name].dtype)
    return out
```

```python
from contextlib import ExitStack

import concourse.bass as bass
from concourse import mybir

F32 = mybir.dt.float32
I32 = mybir.dt.int32
ALU = mybir.AluOpType
ACT = mybir.ActivationFunctionType
AX = mybir.AxisListType

P = 128
D = 1024
KT = D // P
META, SEQ, DB = 16, 512, 8
LP = META + SEQ
TOKENS = LP + DB
HALF = TOKENS // 2
TT = 5
LAST = TOKENS - 4 * P
LASTP = LP - 4 * P
H = 8
PAGES, PAGE = 16, 128
CW = 4
D_FF = 2816
FT = D_FF // P
SCALE = float(P) ** -0.5
EPS = 1e-6
NQKV = 24
SEGS = 9
RING = 4
NEG = -1.0e30

C_QKV, C_Z, C_AB, C_Q, C_K, C_V, C_GA, C_GB = 0, 3072, 4096, 4112, 5136, 6160, 7184, 8208
SEG_W = [("w_in", C_K), ("w_in", C_V), ("w_in", C_QKV), ("w_in", C_QKV + D), ("w_in", C_QKV + 2 * D),
         ("w_in", C_Z), ("w_in", C_GA), ("w_pa", 0), ("w_in", C_GB)]

def weight_pieces():
    out = [("w_in", C_AB, 0, KT, 2 * H)]
    out += [("w_in", C_Q + P * n, 0, KT, P) for n in range(KT)]
    for name, col in SEG_W:
        out += [(name, col + P * n, 0, KT, P) for n in range(KT)]
    out += [("w_pb", P * n, 0, KT, P) for n in range(KT)]
    out += [("w_o", P * n, 0, KT, P) for n in range(KT)]
    for n in range(FT):
        out += [("w_ffn_in", P * n, 0, KT, P), ("w_ffn_in", D_FF + P * n, 0, KT, P)]
    for n in range(KT):
        out += [("w_ffn_out", P * n, 0, 8, P), ("w_ffn_out", P * n, 8, 16, P), ("w_ffn_out", P * n, 16, 22, P)]
    return out


T_AB, T_Q, T_SEG = 0, 1, 9
T_PB = T_SEG + SEGS * KT
T_O = T_PB + KT
T_FI = T_O + KT
T_FO = T_FI + 2 * FT
TILES = T_FO + KT


def reader(t):
    if T_SEG + 7 * KT <= t < T_SEG + 8 * KT or T_PB <= t < T_FI or t >= T_FO:
        return "dve"
    if T_FI <= t < T_FO:
        return "act" if (t - T_FI) % 2 == 0 else "dve"
    return "act"


READ_COUNT = []
for _t in range(TILES):
    READ_COUNT.append(sum(reader(u) == reader(_t) for u in range(_t + 1)))


def piece_of(t):
    return t if t < T_FO else T_FO + 3 * (t - T_FO)


SB_PIECES = [(0, 0, 512, 0, 0),
             (1, 128, 528, 1, 0), (0, 512, 528, 1, 400), (4, 512, 528, 1, 416),
             (2, 256, 528, 2, 0), (3, 384, 528, 2, 272)]
SB_WIDTH = [512, 432, 416]
SB_FLAT = [0, 512, 944]
SB_ALL = 1360


def sb_at(kt, q):
    for k, a, b, bank, col in SB_PIECES:
        if k == kt and a <= q < b:
            return bank, col + q - a, SB_FLAT[bank] + col + q - a


def build(nc, io):
    with ExitStack() as ctx:
        def sb(name, shape, dt=F32):
            return ctx.enter_context(nc.sbuf_tensor(name, shape, dt))

        def sem(name):
            return ctx.enter_context(nc.semaphore(name))

        ps = ctx.enter_context(nc.psum_tensor("ps", [P, 8, 512], F32))

        xn = sb("xn", [P, KT, TOKENS])
        obT = sb("obT", [P, H, TOKENS])
        wring = sb("wring", [P, RING, KT * P])
        kring = sb("kring", [P, RING, D])
        vring = sb("vring", [P, RING, D])
        qbc = sb("qbc", [P, 2, D])
        vacc = sb("vacc", [P, 2, D])
        rows = sb("rows", [P, D])
        qrow = rows[0:DB, :]
        dz = sb("dz", [P, 2, P])
        de = sb("de", [P, P])
        dsp = sb("dsp", [P, 2, P])
        dsuf = sb("dsuf", [P, 2, P])
        dw = sb("dw", [P, 2, P])
        ident = sb("ident", [P, P])
        ones = sb("ones", [P, P])
        tri_ge = sb("tri_ge", [P, P])
        tri_le = sb("tri_le", [P, P])
        tri_gt = sb("tri_gt", [P, P])
        lvl = sb("lvl", [P, 7, P])
        sel = sb("sel", [DB, DB, P])
        cols = sb("cols", [P, 32])
        convw = sb("convw", [P, CW, NQKV])
        alog = sb("alog", [P, H])
        dtb = sb("dtb", [P, H])
        sbb = sb("sbb", [P, H])
        ptab = sb("ptab", [1, DB * PAGES], I32)
        rawt = sb("rawt", [P, NQKV, 11])
        cbuf = sb("cbuf", [P, NQKV, 3 * DB])
        abT = rows[32:32 + 2 * H, 0:TOKENS]
        R = sb("R", [P, 21056])

        def at(o, *shape):
            n = 1
            for s in shape:
                n *= s
            v = R[:, o:o + n]
            if len(shape) == 2:
                v = v.rearrange("p (a b) -> p a b", a=shape[0])
            return v

        A8 = KT * TOKENS
        xs0 = at(0, TT, D)
        hT0 = at(5120, KT, TOKENS)
        cst = at(9408, 3 * D)
        sq = at(12480, 2, TOKENS)
        rstd = at(13552, TOKENS)
        prow = at(14088, P)
        crow = at(14216, P)
        qbT = at(0, H, TOKENS)
        kbT = at(A8, H, TOKENS)
        kbflat = R[:, A8:2 * A8 + P]
        vtok = at(2 * A8 + P, TT, D)
        SBT = 2 * A8 + P + TT * D
        vbT = at(SBT, H, TOKENS)
        ktok = at(SBT + A8, 2, D)
        zs = at(SBT, 2, SB_ALL)
        sps = at(SBT + 2 * SB_ALL, 2, SB_ALL)
        es = at(SBT + 4 * SB_ALL, SB_ALL)
        cT = at(0, NQKV, TOKENS)
        oaT = at(0, H, TOKENS)
        G0 = 3 * A8
        upad = at(G0, 2, 3 + TOKENS)
        krs, bvs, gm, DR, DC, Tm, Q1 = (at(G0 + i * 1024, H, P) for i in range(7))
        Um = vacc[:, 0, :].rearrange("p (h j) -> p h j", h=H)
        S = qbc[:, 0, :].rearrange("p (h j) -> p h j", h=H)
        cvt = at(G0 + 6 * 1024, NQKV, DB)
        Lm = [wring[:, 2 * i:2 * i + 1, :].rearrange("p a (h j) -> p (a h) j", h=H) for i in range(2)]
        rstg = at(G0, 2, TOKENS)
        sqg = wring[:, 0:2, 0:TOKENS]
        st = at(G0, 64, P)
        ksel = wring[64:P, 0:2, :].rearrange("p a (r j) -> p (a r) j", r=8)
        sgA = at(A8, KT, TOKENS)
        sgB = at(A8 + TT * D, KT, TOKENS)
        mT = at(2 * A8 + TT * D, KT, TOKENS)
        ztmp = at(3 * A8 + TT * D, 2, TOKENS)
        hT = at(0, KT, TOKENS)
        xs1 = at(A8, TT, D)
        hid = at(A8, FT, TOKENS)
        gtmp = at(A8 + FT * TOKENS, 2, TOKENS)
        sq1 = at(3 * A8 + TT * D, 2, TOKENS)
        rstd1 = at(3 * A8 + TT * D + 2 * TOKENS, TOKENS)
        ytok = at(A8, TT, D)
        small = sb("small", [P, 11, 40])
        gt, bt, gP, eG, eR, eL, nbG, tmp1, tmp2, eal = (small[:, i, :] for i in range(10))
        onr = small[:, 10, :]
        srow = sb("srow", [1, P])
        dsm = sb("dsm", [P, 10, 64])
        krow, vrow = rows[64:P, 0:P], rows[64:P, P:2 * P]

        zeros = sb("zeros", [P, 1])
        epsc = sb("epsc", [P, 1])
        ab5 = sb("ab5", [P, TT, 2 * H])
        convrow_sb = R[:, G0 + 2 * 1024:G0 + 5 * 1024]
        g_dve0, eps_ready, kpad = sem("g_dve0"), sem("eps_ready"), sem("kpad")

        def convrows(a, b):
            return convrow_sb[a:b, :]

        const_step, const_ready = sem("const_step"), sem("const_ready")
        x_in = [sem("x_in0"), sem("x_in1")]
        par_in, pt_in, cst_in = sem("par_in"), sem("pt_in"), sem("cst_in")
        w_in_slot = [sem(f"w_in_slot{i}") for i in range(RING)]
        k_in = [sem(f"k_in{i}") for i in range(RING)]
        v_in = [sem(f"v_in{i}") for i in range(RING)]
        w_used = sem("w_used")
        act_read = sem("act_read")
        dve_read = sem("dve_read")
        k_used, v_used = sem("k_used"), sem("v_used")
        xt_ready, xt_a, xt_d = sem("xt_ready"), sem("xt_a"), sem("xt_d")
        sq_ready, sq_used = sem("sq_ready"), sem("sq_used")
        ms_ready, rt_ready, rc_ready, xn_ready = sem("ms_ready"), sem("rt_ready"), sem("rc_ready"), sem("xn_ready")
        par_t, par_c, cb_c = sem("par_t"), sem("par_c"), sem("cb_c")
        qr_t, qr_c, qb_t, qb_c = sem("qr_t"), sem("qr_c"), sem("qb_t"), sem("qb_c")
        dz_raw, dz_ready = sem("dz_raw"), sem("dz_ready")
        d_abs, d_exp, d_ln, d_sp, d_suf = sem("d_abs"), sem("d_exp"), sem("d_ln"), sem("d_sp"), sem("d_suf")
        d_cum, d_arg, d_w = sem("d_cum"), sem("d_arg"), sem("d_w")
        v_sum, ob_s = sem("v_sum"), sem("ob_s")
        tok_t, tok_a, tok_d = sem("tok_t"), sem("tok_a"), sem("tok_d")
        k_out, v_out, c_out, r_out, y_out = [sem("k_out0"), sem("k_out1")], sem("v_out"), sem("c_out"), sem("r_out"), sem("y_out")
        s_s, s_z, s_abs, s_exp, s_ln, s_sp = (sem(n) for n in ("s_s", "s_z", "s_abs", "s_exp", "s_ln", "s_sp"))
        s_msp, s_c, s_arg, s_marg, s_w, s_av, s_o = (sem(n) for n in ("s_msp", "s_c", "s_arg", "s_marg", "s_w", "s_av", "s_o"))
        up_zero, cv_step, cs_done, raw_c = sem("up_zero"), sem("cv_step"), sem("cs_done"), sem("raw_c")
        sc_step = sem("sc_step")
        n_sq, n_ss, n_ms, n_rt, n_rc, n_done = (sem(n) for n in ("n_sq", "n_ss", "n_ms", "n_rt", "n_rc", "n_done"))
        co_t, co_c = sem("co_t"), sem("co_c")
        ab_t, ab_d, ab_a, ab_p, ab_row, ab_m = (sem(n) for n in ("ab_t", "ab_d", "ab_a", "ab_p", "ab_row", "ab_m"))
        g_pe, g_act, g_dve, g_pool = (sem(n) for n in ("g_pe", "g_act", "g_dve", "g_pool"))
        t_in = [sem(f"t_in{i}") for i in range(4)]
        t_pe, t_dve, t_act, t_pool = (sem(n) for n in ("t_pe", "t_dve", "t_act", "t_pool"))
        z_silu, z_done, gate_done, m_done = sem("z_silu"), sem("z_done"), sem("gate_done"), sem("m_done")
        h_ready, pb_t = sem("h_ready"), sem("pb_t")

        def slot_value(n):
            return 16 * (n // RING + 1)

        pieces = weight_pieces()

        def done(t):
            return piece_of(t) + (3 if t >= T_FO else 1)

        def wait_read(eng, t):
            eng.wait_ge(act_read if reader(t) == "act" else dve_read, READ_COUNT[t])

        def w_load(sp, p):
            name, col, k0, k1, n = pieces[p]
            if p >= RING:
                sp.wait_ge(w_used, p - RING + 1)
            dst = wring[:, p % RING, :].rearrange("p (k n) -> p k n", k=KT)[:, 0:k1 - k0, 0:n]
            src = io[name][k0 * P:k1 * P, col:col + n].rearrange("(k p) n -> p k n", p=P)
            sp.dma_start(dst, src).then_inc(w_in_slot[p % RING], 16)

        def w_block(p, k):
            return wring[:, p % RING, :].rearrange("p (k n) -> p k n", k=KT)[:, k, 0:pieces[p][4]]

        def pair(t, m=P):
            return ps[0:m, 2 * (t % 2):2 * (t % 2) + 2, 0:HALF]

        def halves(v):
            return v.rearrange("p (a b) -> p a b", a=2)

        def per_head(v, n):
            return v.unsqueeze(2).to_broadcast([v.shape[0], v.shape[1], n])

        def rows_of(t):
            return LAST if t == 4 else P

        def chunk(c):
            return LASTP if c == 4 else P

        LEVELS = {c: [s for s in (1, 2, 4, 8, 16, 32, 64) if s < chunk(c)] for c in range(TT)}
        G2 = (0, 1)

        def order(per_chunk):
            return {(c,) + k: i + 1 for i, (c, k) in
                    enumerate((c, k) for c in range(TT) for k in per_chunk(c))}

        PE_AT = order(lambda c: [(n, g) for n in ("tk", "tv", "dr", "dc", "kk", "kq", "lt") for g in G2]
                      + [(n, s, g) for s in LEVELS[c][1:] for n in ("q1", "up") for g in G2]
                      + [(n, g) for n in ("ks", "qs", "vn", "o2", "kv", "ot") for g in G2])
        ACT_AT = order(lambda c: [(n, g) for n in ("dr", "dc") for g in G2]
                       + [("q1", s, g) for s in LEVELS[c][1:] for g in G2]
                       + [("qs", 0), ("qs", 1), ("vn", 0), ("vn", 1), ("rt",), ("ot", 0), ("ot", 1)])
        DVE_AT = order(lambda c: [("kr", 0), ("kr", 1), ("bv", 0), ("bv", 1), ("A", 0), ("A", 1), ("qk", 0), ("qk", 1)]
                       + [(n, g) for g in G2 for n in ("U1", "T1")]
                       + [(n, s, g) for s in LEVELS[c][1:] for g in G2
                          for n in (("U", "T") if s != LEVELS[c][-1] else ("U",))]
                       + [("R", 0), ("R", 1), ("o", 0), ("o", 1), ("ss",), ("ms",), ("S", 0), ("S", 1), ("rc",), ("on",)])
        POOL_AT = order(lambda c: [("gm",), ("dr", 0), ("dr", 1), ("dc", 0), ("dc", 1)]
                        + [("L", s, g) for s in LEVELS[c] for g in G2] + [("sq",)])

        def even(v, s):
            return v.rearrange("p h (b two s) -> p h b two s", two=2, s=s)[:, :, :, 0, :]

        def odd(v, s):
            return v.rearrange("p h (b two s) -> p h b two s", two=2, s=s)[:, :, :, 1, :]

        block = ctx.enter_context(nc.Block())

        @block.sync
        def _(sp):
            def load_x(u, xs):
                sp.dma_start(xs[0:META, 0, :], io["meta_tokens"]).then_inc(x_in[u], 16)
                sp.dma_start(xs[META:P, 0, :], io["x_prompt"][0:P - META, :]).then_inc(x_in[u], 16)
                sp.dma_start(xs[:, 1:4, :], io["x_prompt"][P - META:4 * P - META, :]
                             .rearrange("(t p) d -> p t d", p=P)).then_inc(x_in[u], 16)
                sp.dma_start(xs[0:LASTP, 4, :], io["x_prompt"][4 * P - META:SEQ, :]).then_inc(x_in[u], 16)
                sp.dma_start(xs[LASTP:LAST, 4, :], io["x_sample"]).then_inc(x_in[u], 16)

            load_x(0, xs0)
            sp.dma_start(prow[0:KT, :], io["norm_mix"]).then_inc(par_in, 16)
            sp.dma_start(prow[KT:2 * KT, :], io["norm_ffn"]).then_inc(par_in, 16)
            sp.dma_start(prow[2 * KT:3 * KT, :], io["norm_final"]).then_inc(par_in, 16)
            sp.dma_start(prow[3 * KT:3 * KT + 1, :], io["gdn_norm"]).then_inc(par_in, 16)
            sp.dma_start(crow[0:CW * NQKV, :], io["conv_w"]).then_inc(par_in, 16)
            sp.dma_start(alog[:, :], io["a_log"].to_broadcast([P, H])).then_inc(par_in, 16)
            sp.dma_start(dtb[:, :], io["dt_bias"].to_broadcast([P, H])).then_inc(par_in, 16)
            sp.dma_start(sbb[:, :], io["sb_bias"].to_broadcast([P, H])).then_inc(par_in, 16)
            sp.dma_start(ptab[:, :], io["page_table"]).then_inc(pt_in, 16)
            sp.dma_start(cst[0:3 * DB, :], io["state_conv"]).then_inc(cst_in, 16)
            sp.dma_start(io["conv_sample"][:, 0:2, :], io["state_conv3"][:, 1:3, :]).then_inc(c_out, 16)
            for p in range(T_SEG):
                w_load(sp, p)
            sp.wait_ge(pt_in, 16)

            def page(ring, landed, used, cache, b, p):
                n = b * PAGES + p
                if n >= RING:
                    sp.wait_ge(used, n - RING + 1)
                row = sp.value_load(ptab[0:1, n:n + 1], min_val=0, max_val=NPHYS - 1)
                sp.dma_start(ring[:, n % RING:n % RING + 1, :],
                             cache[bass.ds(row, 1), :, :].rearrange("a p n -> p a n"))\
                  .then_inc(landed[n % RING], 16)

            def store_kv():
                for name, src, s_out in (("v", vtok, (v_out, v_out)), ("k", ktok, k_out)):
                    for t in range(TT):
                        i = t if name == "v" else TT + t
                        sp.wait_ge(tok_a, i + 1)
                        sp.wait_ge(tok_d, i + 1)
                        v = src[:, t if name == "v" else t % 2, :]
                        n = LASTP if t == 4 else P
                        sp.dma_start(io[name + "_prompt"][t * P:t * P + n, :], v[0:n, :]).then_inc(s_out[t % 2], 16)
                        if t == 4:
                            sp.dma_start(io[name + "_sample"], v[LASTP:LAST, :]).then_inc(s_out[0], 16)

            def gdn_dma():
                sp.wait_ge(ab_d, AB_G)
                sp.wait_ge(ab_a, AB_B)
                sp.dma_start(srow[0:1, 0:64],
                             gt[LASTP:LAST, 32:40]).then_inc(ab_row, 16)
                sp.dma_start(srow[0:1, 64:128],
                             bt[LASTP:LAST, 32:40]).then_inc(ab_row, 16)
                sp.wait_ge(co_c, 6)
                sp.dma_start(io["conv_prompt"], convrows(0, 3)).then_inc(c_out, 16)
                sp.dma_start(io["conv_sample"][:, 2, :], convrows(3, 11)).then_inc(c_out, 16)
                sp.wait_ge(g_dve, DVE_AT[4, "S", 1])
                sp.dma_start(io["rec_prompt"].rearrange("h k v -> k h v"), S).then_inc(r_out, 16)
                sp.wait_ge(r_out, 16)
                sp.wait_ge(g_act, ACT_AT[4, "ot", 1])
                for j in range(4):
                    sp.dma_start(st[:, 16 * j:16 * j + 16, :],
                                 io["state_rec"][2 * j:2 * j + 2].rearrange("b h k v -> k (b h) v"))\
                      .then_inc(t_in[j], 16)
                for j in range(4):
                    sp.wait_ge(t_dve, T_S0 + 4 * j + 4)
                    sp.dma_start(io["rec_sample"][2 * j:2 * j + 2].rearrange("b h k v -> k (b h) v"),
                                 st[:, 16 * j:16 * j + 16, :]).then_inc(r_out, 16)

            for s in range(SEGS):
                for q in range(4):
                    first = range(4) if (s in (0, 5) and q == 0) else range(2 * q + 2, 2 * q + 4)
                    for t in first:
                        if not (s == 4 and t >= KT) and T_SEG + s * KT + t < T_O:
                            w_load(sp, T_SEG + s * KT + t)
                    if s < DB:
                        for p in range(4 * q, 4 * q + 4):
                            page(kring, k_in, k_used, io["cache_k"], s, p)
                    if s >= 1:
                        for p in range(4 * q, 4 * q + 4):
                            page(vring, v_in, v_used, io["cache_v"], s - 1, p)
                if s == 1:
                    store_kv()
                if s == 4:
                    gdn_dma()
                    sp.wait_ge(t_pe, T_PE_END)
            for p in range(T_PB + 2, T_O):
                w_load(sp, p)
            sp.wait_ge(r_out, 16 * 5)
            wait_read(sp, T_SEG + 8 * KT - 1)
            load_x(1, xs1)
            for p in range(T_O, len(pieces)):
                w_load(sp, p)
            for t in range(TT):
                sp.wait_ge(tok_a, 2 * TT + t + 1)
                sp.wait_ge(tok_d, 2 * TT + t + 1)
                if t == 0:
                    sp.dma_start(io["y_prompt"][0:P - META, :], ytok[META:P, 0, :]).then_inc(y_out, 16)
                elif t < 4:
                    sp.dma_start(io["y_prompt"][t * P - META:(t + 1) * P - META, :], ytok[:, t, :]).then_inc(y_out, 16)
                else:
                    sp.dma_start(io["y_prompt"][4 * P - META:SEQ, :], ytok[0:LASTP, 4, :]).then_inc(y_out, 16)
                    sp.dma_start(io["y_sample"], ytok[LASTP:LAST, 4, :]).then_inc(y_out, 16)
            sp.wait_ge(y_out, 16 * 6)
            sp.wait_ge(k_out[0], 16 * 4)
            sp.wait_ge(k_out[1], 16 * 2)
            sp.wait_ge(v_out, 16 * 6)
            sp.wait_ge(c_out, 16 * 3)
            sp.wait_ge(r_out, 16 * 5)

        @block.tensor
        def _(pe):
            mm, tr = nc.tensor.matmul, nc.tensor.transpose

            def transpose_x(u, xs):
                pe.wait_ge(x_in[u], 80)
                for k in range(KT):
                    if k >= 2:
                        pe.wait_ge(xt_a, KT * u + k - 1)
                        pe.wait_ge(xt_d, KT * u + k - 1)
                    b = 2 * (k % 2)
                    for t in range(4):
                        tr(ps[:, b, t * P:t * P + P], xs[:, t, k * P:k * P + P], ident[:, :])
                    tr(ps[:, b + 1, 0:LAST], xs[0:LAST, 4, k * P:k * P + P], ident[0:LAST, 0:LAST])\
                        .then_inc(xt_ready, 1)

            def square_sums(u):
                for k in range(KT):
                    pe.wait_ge(sq_ready, KT * u + k + 1)
                    sq_u = sq if u == 0 else sq1
                    for i in range(2):
                        m = mm(ps[:, 4 + i, 0:HALF], ones[:, :], sq_u[:, k % 2, i * HALF:i * HALF + HALF],
                               start=(k == 0), stop=(k == KT - 1))
                    m.then_inc(sq_used, 1)

            def tile(t, src):
                if t >= 2:
                    wait_read(pe, t - 2)
                m, k, n_k = pieces[piece_of(t)][4], 0, FT if t >= T_FO else KT
                for p in range(piece_of(t), done(t)):
                    pe.wait_ge(w_in_slot[p % RING], slot_value(p))
                    for kk in range(pieces[p][3] - pieces[p][2]):
                        for i in range(2):
                            last = mm(ps[0:m, 2 * (t % 2) + i, 0:HALF], w_block(p, kk),
                                      src[:, k, i * HALF:i * HALF + HALF], start=(k == 0), stop=(k == n_k - 1))
                        k += 1
                    last.then_inc(w_used, 1)

            def spread_q(b):
                if b >= 1:
                    pe.wait_ge(qb_c, b)
                for i in range(2):
                    m = mm(ps[:, 6 + i, :], sel[:, b, :], qrow[:, 512 * i:512 * i + 512], start=True, stop=True)
                m.then_inc(qb_t, 1)

            def cumulate(b):
                pe.wait_ge(d_suf, 4 * (b + 1))
                if b >= 1:
                    pe.wait_ge(d_arg, b)
                mm(ps[:, 4, 0:P], tri_ge[:, :], dsp[:, b % 2, :], start=True, stop=False)
                mm(ps[:, 4, 0:P - H], ones[:, :], dsuf[:, 1, H:P], start=False, stop=True).then_inc(d_cum, 1)

            def sum_v(b):
                pe.wait_ge(v_used, PAGES * (b + 1))
                if b >= 1:
                    pe.wait_ge(ob_s, b)
                for h in range(H):
                    m = mm(ps[:, 5, h:h + 1], vacc[:, b % 2, h * P:h * P + P], ones[:, 0:1], start=True, stop=True)
                m.then_inc(v_sum, 1)

            def to_tokens(i, src, t):
                if i >= 2:
                    pe.wait_ge(tok_a, i - 1)
                    pe.wait_ge(tok_d, i - 1)
                n = rows_of(t)
                for h in range(H):
                    m = tr(ps[0:n, 2 * (i % 2) + h // 4, (h % 4) * P:(h % 4) * P + P],
                           src[:, h, t * P:t * P + n], ident[:, :])
                m.then_inc(tok_t, 1)

            def attend():
                def scores(h):
                    if h == 0:
                        pe.wait_ge(tok_a, 2 * TT)
                        pe.wait_ge(tok_d, 2 * TT)
                    else:
                        pe.wait_ge(s_z, h)
                    for kt, a, b, bank, col in SB_PIECES:
                        o = h * TOKENS + kt * P
                        m = mm(ps[:, bank, col:col + b - a], kbflat[:, o:o + P], qbT[:, h, a:b],
                               start=True, stop=True)
                    m.then_inc(s_s, 1)

                def later_sums(h):
                    pe.wait_ge(s_msp, h + 1)
                    if h >= 1:
                        pe.wait_ge(s_arg, h)
                    for kt, a, b, bank, col in SB_PIECES:
                        parts = [(tri_ge, kt, a)] + [(ones, k2, max(a, P * k2)) for k2 in range(kt + 1, TT)
                                                     if P * k2 < b]
                        for j, (lhs, k2, q) in enumerate(parts):
                            f = sb_at(k2, q)[2]
                            m = mm(ps[:, 3 + bank, col + q - a:col + b - a], lhs[:, :],
                                   sps[:, h % 2, f:f + b - q], start=(j == 0), stop=(j == len(parts) - 1))
                    m.then_inc(s_c, 1)

                def values(h):
                    pe.wait_ge(s_w, h + 1)
                    if h >= 1:
                        pe.wait_ge(s_o, h)
                    else:
                        pe.wait_ge(qb_c, 3)
                    for bank, a, b in ((6, 0, 512), (7, 512, LP)):
                        ks = [k for k in range(TT) if P * k < b]
                        for k in ks:
                            q, n = max(a, P * k), chunk(k)
                            f = sb_at(k, q)[2]
                            m = mm(ps[:, bank, q - a:b - a], vtok[0:n, k, h * P:h * P + P],
                                   zs[0:n, h % 2, f:f + b - q], start=(k == 0), stop=(k == ks[-1]))
                    m.then_inc(s_av, 1)

                scores(0)
                for h in range(H + 1):
                    if h + 1 < H:
                        scores(h + 1)
                    if h < H:
                        later_sums(h)
                    if h >= 1:
                        values(h - 1)
                pe.wait_ge(s_z, H)
                pe.wait_ge(s_arg, H)
                pe.wait_ge(s_o, H)

            def conv_rows():
                pe.wait_ge(raw_c, NQKV)
                for n in range(NQKV):
                    i = n // 4
                    if n % 4 == 0 and i >= 2:
                        pe.wait_ge(co_c, i - 1)
                    m = tr(ps[0:11, i % 2, (n % 4) * P:(n % 4) * P + P], rawt[:, n, :], ident[:, :])
                    if n % 4 == 3:
                        m.then_inc(co_t, 1)
                pe.wait_ge(co_c, 6)

            def norm_qk():
                for n in range(2 * H):
                    pe.wait_ge(n_sq, n + 1)
                    if n >= 2:
                        pe.wait_ge(n_ms, n - 1)
                    for i in range(2):
                        m = mm(ps[:, 2 * (n % 2) + i, 0:HALF], ones[:, :],
                               sqg[:, n % 2, i * HALF:i * HALF + HALF], start=True, stop=True)
                    m.then_inc(n_ss, 1)

            def decays():
                for t in range(TT):
                    n = rows_of(t)
                    m = tr(ps[0:n, 4, 16 * t:16 * t + 16], abT[:, t * P:t * P + n], ident[32:48, 32:48])
                m.then_inc(ab_t, 1)
                pe.wait_ge(ab_p, 2)
                mm(ps[:, 5, 0:40], tri_le[:, :], gP, start=True, stop=True)
                mm(ps[:, 5, 64:104], tri_gt[:, :], gP, start=True, stop=True)
                mm(ps[:, 5, 128:168], ones[:, :], gP, start=True, stop=True)
                pe.wait_ge(ab_row, 32)
                mm(ps[:, 5, 256:384], ones[0:1, :], srow[0:1, :], start=True, stop=True).then_inc(ab_m, 1)
                pe.wait_ge(ab_a, AB_END)
                pe.wait_ge(ab_d, AB_DEND)
                pe.wait_ge(n_done, 2 * H)

            def chunks():
                for c in range(TT):
                    n, t0 = chunk(c), P * c

                    def after(eng, *key):
                        s, at_ = {"act": (g_act, ACT_AT), "dve": (g_dve, DVE_AT), "pool": (g_pool, POOL_AT)}[eng]
                        if key[0] >= 0:
                            pe.wait_ge(s, at_[key])

                    def heads(g):
                        return range(4 * g, 4 * g + 4)

                    def col(h):
                        return (h % 4) * P

                    for g in G2:
                        after("act", c - 1, "vn", g)
                        for h in heads(g):
                            m = tr(ps[0:n, g, col(h):col(h) + P], cT[:, H + h, t0:t0 + n], ident[:, :])
                        m.then_inc(g_pe, 1)
                    for g in G2:
                        after("dve", c - 1, "o", g)
                        for h in heads(g):
                            m = tr(ps[0:n, 2 + g, col(h):col(h) + P], cT[:, 2 * H + h, t0:t0 + n], ident[:, :])
                        m.then_inc(g_pe, 1)
                    after("pool", c, "gm")
                    for g in G2:
                        after("dve", c - 1, "S", g)
                        mm(ps[0:n, 4 + g, 0:4 * n], tri_le[0:n, 0:n], gm[0:n, 4 * g:4 * g + 4, 0:n],
                           start=True, stop=True).then_inc(g_pe, 1)
                    for g in G2:
                        after("act", c - 1, "ot", g)
                        for h in heads(g):
                            m = mm(ps[0:n, 6 + g, (h % 4) * n:(h % 4) * n + n], gm[0:n, h, 0:n],
                                   tri_le[0:n, 0:n], start=True, stop=True)
                        m.then_inc(g_pe, 1)
                    for g in G2:
                        after("dve", c, "kr", g)
                        for h in heads(g):
                            m = mm(ps[0:n, g, (h % 4) * n:(h % 4) * n + n], cT[:, H + h, t0:t0 + n],
                                   cT[:, H + h, t0:t0 + n], start=True, stop=True)
                        m.then_inc(g_pe, 1)
                    for g in G2:
                        after("dve", c, "bv", g)
                        for h in heads(g):
                            m = mm(ps[0:n, 2 + g, (h % 4) * n:(h % 4) * n + n], cT[:, H + h, t0:t0 + n],
                                   cT[:, h, t0:t0 + n], start=True, stop=True)
                        m.then_inc(g_pe, 1)
                    for g in G2:
                        after("pool", c, "L", 1, g)
                        after("act", c, "dr", g)
                        for h in heads(g):
                            m = tr(ps[0:n, 4 + g, (h % 4) * n:(h % 4) * n + n], Lm[0][0:n, h, 0:n], ident[0:n, 0:n])
                        m.then_inc(g_pe, 1)
                    for j, s in enumerate(LEVELS[c][1:]):
                        w = n // 2
                        for g in G2:
                            after("pool", c, "L", s, g)
                            if j == 0:
                                after("dve", c, "U1", g)
                                after("dve", c, "A", g)
                            else:
                                after("dve", c, "U", s // 2, g)
                            for h in heads(g):
                                m = mm(ps[0:n, g, (h % 4) * n:(h % 4) * n + n], Lm[(j + 1) % 2][0:n, h, 0:n],
                                       Um[0:n, h, 0:n], start=True, stop=True)
                            m.then_inc(g_pe, 1)
                        for g in G2:
                            after("act", c, "q1", s, g)
                            if j == 0:
                                after("dve", c, "qk", g)
                                after("dve", c, "T1", g)
                            else:
                                after("dve", c, "T", s // 2, g)
                            for h in heads(g):
                                m = mm(ps[0:n, 2 + g, (h % 4) * w:(h % 4) * w + w], Tm[0:n, h, 0:n],
                                       odd(Q1[0:n, h:h + 1, 0:n], s)[:, 0], start=True, stop=True)
                            if 2 * s < n:
                                for h in heads(g):
                                    m = mm(ps[0:n, 2 + g, 256 + (h % 4) * w:256 + (h % 4) * w + w], Q1[0:n, h, 0:n],
                                           even(Tm[0:n, h:h + 1, 0:n], s)[:, 0], start=True, stop=True)
                            m.then_inc(g_pe, 1)
                    last = LEVELS[c][-1]
                    for g in G2:
                        if c:
                            after("dve", c - 1, "S", g)
                        else:
                            pe.wait_ge(g_dve0, 1)
                        after("dve", c, "U1", g)
                        for h in heads(g):
                            m = mm(ps[0:n, 4 + g, col(h):col(h) + P], cT[:, H + h, t0:t0 + n], S[:, h, :],
                                   start=True, stop=True)
                        m.then_inc(g_pe, 1)
                    for g in G2:
                        after("act", c, "dc", g)
                        for h in heads(g):
                            m = mm(ps[0:n, 6 + g, col(h):col(h) + P], cT[:, h, t0:t0 + n], S[:, h, :],
                                   start=True, stop=True)
                        m.then_inc(g_pe, 1)
                    for g in G2:
                        after("dve", c, "R", g)
                        after("dve", c, "U", last, g)
                        for h in heads(g):
                            m = mm(ps[0:n, g, col(h):col(h) + P], Um[0:n, h, 0:n], bvs[0:n, h, :],
                                   start=True, stop=True)
                        m.then_inc(g_pe, 1)
                    for g in G2:
                        after("act", c, "vn", g)
                        for h in heads(g):
                            m = mm(ps[0:n, 2 + g, col(h):col(h) + P], DC[0:n, h, 0:n], gm[0:n, h, :],
                                   start=True, stop=True)
                        m.then_inc(g_pe, 1)
                    for g in G2:
                        for h in heads(g):
                            m = mm(ps[:, 4 + g, col(h):col(h) + P], krs[0:n, h, :], gm[0:n, h, :],
                                   start=True, stop=True)
                        m.then_inc(g_pe, 1)
                    after("dve", c, "on")
                    for g in G2:
                        after("act", c, "qs", g)
                        for h in heads(g):
                            m = tr(ps[:, 6 + g, (h % 4) * n:(h % 4) * n + n], Q1[0:n, h, :], ident[0:n, 0:n])
                        m.then_inc(g_pe, 1)
                pe.wait_ge(g_act, ACT_AT[4, "ot", 1])
                pe.wait_ge(g_dve, DVE_AT[4, "on"])

            def sampled_delta():
                pe.wait_ge(t_dve, 1)
                for r in range(64):
                    b, h = r // H, r % H
                    if r % 16 == 0:
                        pe.wait_ge(t_in[r // 16], 16)
                    m = mm(ps[:, 0, 2 * r:2 * r + 2], st[:, r, :], cT[:, h:h + H + 1:H, LP + b],
                           start=True, stop=True)
                m.then_inc(t_pe, 1)
                mm(ps[:, 1, 0:64], ones[:, :], dsm[:, 0, :], start=True, stop=True).then_inc(t_pe, 1)
                pe.wait_ge(t_dve, T_VN)
                tr(ps[0:64, 2, 0:P], dsm[:, 3, :], ident[:, :])
                tr(ps[0:64, 2, P:2 * P], dsm[:, 1, :], ident[:, :]).then_inc(t_pe, 1)
                pe.wait_ge(t_dve, T_OSQ)
                mm(ps[:, 3, 0:64], ones[:, :], dsm[:, 6, :], start=True, stop=True).then_inc(t_pe, 1)
                for j in range(4):
                    pe.wait_ge(t_pool, j + 1)
                    pe.wait_ge(t_dve, T_ROWS)
                    for i in range(4):
                        if j:
                            pe.wait_ge(t_dve, T_S0 + 4 * (j - 1) + i + 1)
                        for r4 in range(4):
                            r = 4 * i + r4
                            m = mm(ps[:, 4 + i, r4 * P:r4 * P + P], ksel[:, r, :], vrow[:, :],
                                   start=True, stop=True)
                        m.then_inc(t_pe, 1)
                pe.wait_ge(t_dve, T_S0 + 16)
                pe.wait_ge(t_act, 3)

            pe.wait_ge(const_ready, NCONST)
            transpose_x(0, xs0)
            pe.wait_ge(par_in, 16 * 8)
            tr(ps[:, 6, 0:25], prow[0:25, :], ident[0:25, 0:25])
            tr(ps[:, 6, P:P + 96], crow[0:96, :], ident[0:96, 0:96]).then_inc(par_t, 1)
            square_sums(0)
            pe.wait_ge(par_c, 2)
            pe.wait_ge(cst_in, 16)
            for n in range(NQKV):
                m = tr(ps[:, 6 + n // 12, 24 * (n % 12):24 * (n % 12) + 24], cst[0:24, n * P:n * P + P],
                       ident[0:24, 0:24])
            m.then_inc(par_t, 1)
            pe.wait_ge(xn_ready, KT)
            for t in range(T_SEG):
                tile(t, xn)
            wait_read(pe, T_SEG - 1)
            pe.wait_ge(cb_c, 2)
            for h in range(H):
                m = tr(ps[0:DB, 6 + h // 4, (h % 4) * P:(h % 4) * P + P], qbT[:, h, LP:TOKENS], ident[:, :])
            m.then_inc(qr_t, 1)
            pe.wait_ge(qr_c, 1)
            spread_q(0)
            for s in range(SEGS):
                src = oaT if s == 7 else xn
                if s == 7:
                    pe.wait_ge(z_done, KT)
                for j in range(KT):
                    tile(T_SEG + s * KT + j, src)
                    if j == 0 and s >= 2:
                        sum_v(s - 2)
                    if j == 1 and s >= 1:
                        cumulate(s - 1)
                    if j == 4 and s + 1 < DB:
                        spread_q(s + 1)
                if s == 1:
                    wait_read(pe, T_SEG + 2 * KT - 2)
                    wait_read(pe, T_SEG + 2 * KT - 1)
                    for t in range(TT):
                        to_tokens(t, vbT, t)
                    for t in range(TT):
                        to_tokens(TT + t, kbT, t)
                    pe.wait_ge(d_arg, 1)
                    attend()
                if s == 4:
                    wait_read(pe, T_SEG + 5 * KT - 2)
                    wait_read(pe, T_SEG + 5 * KT - 1)
                    pe.wait_ge(d_arg, 4)
                    pe.wait_ge(ob_s, 3)
                    pe.wait_ge(qb_c, 6)
                    conv_rows()
                    norm_qk()
                    decays()
                    chunks()
                    sampled_delta()
            sum_v(DB - 1)
            pe.wait_ge(ob_s, DB)
            for n in range(KT):
                tile(T_PB + n, obT)
            wait_read(pe, T_PB + 6)
            wait_read(pe, T_PB + 7)
            transpose_x(1, xs1)
            pe.wait_ge(xt_a, 2 * KT)
            pe.wait_ge(xt_d, 2 * KT)
            pe.wait_ge(m_done, KT)
            for n in range(KT):
                tile(T_O + n, mT)
            square_sums(1)
            pe.wait_ge(xn_ready, 2 * KT)
            for n in range(2 * FT):
                tile(T_FI + n, xn)
            wait_read(pe, T_FO - 1)
            for n in range(KT):
                tile(T_FO + n, hid)
            square_sums(2)
            wait_read(pe, TILES - 2)
            wait_read(pe, TILES - 1)
            pe.wait_ge(xn_ready, 3 * KT)
            for t in range(TT):
                to_tokens(2 * TT + t, xn, t)

        @block.scalar
        def _(act):
            go = nc.scalar.activation

            def copy_x(u, dst):
                for k in range(KT):
                    act.wait_ge(xt_ready, KT * u + k + 1)
                    nc.scalar.copy(dst[:, k, 0:512], ps[:, 2 * (k % 2), :]).then_inc(xt_a, 1)

            def squares(u, src, dst, ready, value):
                for k in range(KT):
                    ready(k)
                    if KT * u + k >= 2:
                        act.wait_ge(sq_used, KT * u + k - 1)
                    go(dst[:, k % 2, :], src[:, k, :], ACT.Square).then_inc(sq_ready, 1)

            def root(u, buf):
                act.wait_ge(ms_ready, u + 1)
                go(buf, buf, ACT.Sqrt).then_inc(rt_ready, 1)

            def read_tile(t, dst, func=ACT.Copy, m=P):
                act.wait_ge(w_used, done(t))
                go(halves(dst), pair(t, m), func).then_inc(act_read, 1)

            def put_q(b):
                act.wait_ge(qb_t, b + 1)
                if b >= 2:
                    act.wait_ge(k_used, PAGES * (b - 1))
                nc.scalar.copy(qbc[:, b % 2, :].rearrange("p (a n) -> p a n", a=2), ps[:, 6:8, :]).then_inc(qb_c, 1)

            def softplus_part(b):
                act.wait_ge(dz_ready, b + 1)
                if b >= 1:
                    act.wait_ge(d_sp, b)
                go(de[:, :], dz[:, b % 2, :], ACT.Abs).then_inc(d_abs, 1)
                act.wait_ge(d_abs, b + 1)
                go(de[:, :], de[:, :], ACT.Exp, scale=-1.0).then_inc(d_exp, 1)
                act.wait_ge(d_exp, b + 1)
                go(de[:, :], de[:, :], ACT.Ln, bias=1.0).then_inc(d_ln, 1)

            def weights(b):
                act.wait_ge(d_arg, b + 1)
                if b >= 2:
                    act.wait_ge(v_used, PAGES * (b - 1))
                go(dw[:, b % 2, :], dz[:, b % 2, :], ACT.Exp).then_inc(d_w, 1)

            def put_o(b):
                act.wait_ge(v_sum, b + 1)
                nc.scalar.copy(obT[:, :, LP + b], ps[:, 5, 0:H]).then_inc(ob_s, 1)

            def token_bank(i, dst, t):
                act.wait_ge(tok_t, i + 1)
                n = rows_of(t)
                nc.scalar.copy(dst[0:n, 0:512], ps[0:n, 2 * (i % 2), :]).then_inc(tok_a, 1)

            def attend():
                def first(h):
                    act.wait_ge(s_s, h + 1)
                    if h == 0:
                        act.wait_ge(tok_d, 2 * TT)
                        act.wait_ge(k_out[0], 16 * 4)
                        act.wait_ge(k_out[1], 16 * 2)
                    if h >= 2:
                        act.wait_ge(s_av, h - 1)
                    for b in range(3):
                        w = SB_WIDTH[b]
                        m = go(zs[:, h % 2, SB_FLAT[b]:SB_FLAT[b] + w], ps[:, b, 0:w], ACT.Identity,
                               bias=sbb[:, h:h + 1], scale=SCALE)
                    m.then_inc(s_z, 1)
                    act.wait_ge(s_abs, h + 1)
                    go(es, es, ACT.Exp, scale=-1.0).then_inc(s_exp, 1)
                    act.wait_ge(s_exp, h + 1)
                    go(es, es, ACT.Ln, bias=1.0).then_inc(s_ln, 1)

                first(0)
                for h in range(H + 1):
                    if h + 1 < H:
                        first(h + 1)
                    if h < H:
                        act.wait_ge(s_marg, h + 1)
                        go(zs[:, h % 2, :], zs[:, h % 2, :], ACT.Exp).then_inc(s_w, 1)
                    if h >= 1:
                        act.wait_ge(s_av, h)
                        nc.scalar.copy(obT[:, h - 1, 0:512], ps[:, 6, :])
                        nc.scalar.copy(obT[:, h - 1, 512:LP], ps[:, 7, 0:LP - 512]).then_inc(s_o, 1)

            def silu_conv(n):
                act.wait_ge(cv_step, CW * (n + 1))
                go(cT[:, n, 0:LP], cT[:, n, 0:LP], ACT.Silu).then_inc(cs_done, 1)

            def norm_qk():
                act.wait_ge(sc_step, 7)
                go(cT[:, :, LP:TOKENS], cT[:, :, LP:TOKENS], ACT.Silu).then_inc(cs_done, 1)
                act.wait_ge(cs_done, NQKV + 1)
                for n in range(2 * H + 1):
                    if n < 2 * H:
                        if n >= 2:
                            act.wait_ge(n_ss, n - 1)
                        go(sqg[:, n % 2, :], cT[:, n, :], ACT.Square).then_inc(n_sq, 1)
                    if n >= 1:
                        act.wait_ge(n_ms, n)
                        go(rstg[:, (n - 1) % 2, :], rstg[:, (n - 1) % 2, :], ACT.Sqrt).then_inc(n_rt, 1)

            def decays():
                act.wait_ge(par_in, 16 * 8)
                go(eal[:, 0:H], alog[:, :], ACT.Exp).then_inc(ab_a, 1)
                act.wait_ge(ab_d, AB_X)
                go(tmp2, tmp1, ACT.Abs).then_inc(ab_a, 1)
                act.wait_ge(ab_a, 2)
                go(tmp2, tmp2, ACT.Exp, scale=-1.0).then_inc(ab_a, 1)
                act.wait_ge(ab_a, 3)
                go(tmp2, tmp2, ACT.Ln, bias=1.0).then_inc(ab_a, 1)
                go(bt.rearrange("p (t h) -> p t h", h=H), ab5[:, :, H:2 * H], ACT.Sigmoid).then_inc(ab_a, 1)
                act.wait_ge(ab_m, 1)
                go(eG, ps[:, 5, 0:40], ACT.Exp).then_inc(ab_a, 1)
                go(eR, ps[:, 5, 64:104], ACT.Exp).then_inc(ab_a, 1)
                go(eL, ps[:, 5, 128:168], ACT.Exp).then_inc(ab_a, 1)
                go(dsm[:, 8, :], ps[:, 5, 256:320], ACT.Exp).then_inc(ab_a, 1)
                nc.scalar.copy(dsm[:, 9, :], ps[:, 5, 320:384]).then_inc(ab_a, 1)

            def chunks():
                for c in range(TT):
                    n, t0 = chunk(c), P * c

                    def after(eng, *key):
                        s, at_ = {"pe": (g_pe, PE_AT), "dve": (g_dve, DVE_AT), "pool": (g_pool, POOL_AT)}[eng]
                        if key[0] >= 0:
                            act.wait_ge(s, at_[key])

                    for name, dst, bank, user in (("dr", DR, 4, "L"), ("dc", DC, 6, "o2")):
                        for g in G2:
                            if name == "dr" and c:
                                after("pool", c - 1, "L", LEVELS[c - 1][-1], g)
                            after("pe", c, name, g)
                            go(dst[0:n, 4 * g:4 * g + 4, 0:n],
                               ps[0:n, bank + g, 0:4 * n].rearrange("p (h j) -> p h j", h=4), ACT.Exp)\
                                .then_inc(g_act, 1)
                    for s in LEVELS[c][1:]:
                        for g in G2:
                            after("pe", c, "q1", s, g)
                            nc.scalar.copy(Q1[0:n, 4 * g:4 * g + 4, 0:n],
                                           ps[0:n, g, 0:4 * n].rearrange("p (h j) -> p h j", h=4)).then_inc(g_act, 1)
                    for g in G2:
                        after("pe", c, "qs", g)
                        for h in range(4 * g, 4 * g + 4):
                            i = (h % 4) * P
                            m = go(Q1[0:n, h, :], ps[0:n, 6 + g, i:i + P], ACT.Copy, scale=eG[0:n, H * c + h:H * c + h + 1])
                        m.then_inc(g_act, 1)
                    for g in G2:
                        after("pe", c, "vn", g)
                        nc.scalar.copy(gm[0:n, 4 * g:4 * g + 4, :],
                                       ps[0:n, g, :].rearrange("p (h j) -> p h j", h=4)).then_inc(g_act, 1)
                    after("dve", c, "ms")
                    go(onr[0:n, H:2 * H], onr[0:n, 0:H], ACT.Sqrt).then_inc(g_act, 1)
                    for g in G2:
                        after("pe", c, "ot", g)
                        go(oaT[:, 4 * g:4 * g + 4, t0:t0 + n],
                           ps[:, 6 + g, 0:4 * n].rearrange("p (h j) -> p h j", h=4), ACT.Copy,
                           scale=cols[:, 24:25]).then_inc(g_act, 1)

            def sampled_delta():
                act.wait_ge(t_pe, 4)
                go(dsm[:, 7, :], ps[:, 3, 0:64], ACT.Identity, scale=1.0 / P, bias=epsc[:, :]).then_inc(t_act, 1)
                act.wait_ge(t_act, 1)
                go(dsm[:, 7, :], dsm[:, 7, :], ACT.Sqrt).then_inc(t_act, 1)
                act.wait_ge(t_dve, T_ON)
                go(oaT[:, :, LP:TOKENS].rearrange("p h b -> p b h"),
                   dsm[:, 5, :].rearrange("p (b h) -> p b h", h=H), ACT.Copy, scale=cols[:, 24:25]).then_inc(t_act, 1)

            act.wait_ge(const_ready, NCONST)
            copy_x(0, hT0)

            def x_there(k):
                act.wait_ge(xt_a, k + 1)
                act.wait_ge(xt_d, k + 1)
            squares(0, hT0, sq, x_there, 0)
            root(0, rstd)
            read_tile(T_AB, abT[:, :], m=2 * H)
            for n in range(KT):
                read_tile(T_Q + n, qbT[:, n, :])
            put_q(0)
            for s in range(SEGS):
                if s == 5:
                    act.wait_ge(r_out, 16 * 5)
                for j in range(KT):
                    t, n = T_SEG + s * KT + j, (s - 2) * KT + j
                    if j == 0 and s >= 1:
                        softplus_part(s - 1)
                    if j == 2 and s >= 1:
                        weights(s - 1)
                    if s in (0, 1):
                        read_tile(t, (kbT, vbT)[s][:, j, :])
                    elif s in (2, 3, 4):
                        if n == 0:
                            act.wait_ge(v_out, 16 * 6)
                            act.wait_ge(up_zero, 1)
                        if n >= 2:
                            act.wait_ge(cv_step, CW * (n - 1))
                            act.wait_ge(raw_c, n - 1)
                        read_tile(t, upad[:, n % 2, CW - 1:CW - 1 + TOKENS])
                        if n % 2 and n >= 3:
                            silu_conv(n - 3)
                            silu_conv(n - 2)
                    elif s == 5:
                        if j >= 2:
                            act.wait_ge(z_done, j - 1)
                        act.wait_ge(w_used, done(t))
                        go(halves(ztmp[:, j % 2, :]), pair(t), ACT.Silu).then_inc(act_read, 1)
                    elif s in (6, 8):
                        read_tile(t, (sgA if s == 6 else sgB)[:, j, :], ACT.Sigmoid)
                    if j == 1 and s >= 2:
                        put_o(s - 2)
                    if j == 5 and s + 1 < DB:
                        put_q(s + 1)
                if s == 1:
                    for t in range(TT):
                        token_bank(t, vtok[:, t, :], t)
                    for t in range(TT):
                        if t >= 2:
                            act.wait_ge(k_out[t % 2], 16 * (t // 2))
                        token_bank(TT + t, ktok[:, t % 2, :], t)
                    attend()
                if s == 4:
                    silu_conv(NQKV - 2)
                    silu_conv(NQKV - 1)
                    norm_qk()
                    decays()
                    chunks()
                    sampled_delta()
            put_o(DB - 1)
            copy_x(1, hT)

            def h_there(base):
                def wait(k):
                    act.wait_ge(dve_read, base + k + 1)
                return wait
            squares(1, hT, sq1, h_there(READ_COUNT[T_O] - 1), 0)
            root(1, rstd1)
            for n in range(FT):
                if n >= 2:
                    act.wait_ge(dve_read, READ_COUNT[T_FI + 2 * (n - 2) + 1])
                read_tile(T_FI + 2 * n, gtmp[:, n % 2, :], ACT.Silu)
            squares(2, hT, sq1, h_there(READ_COUNT[T_FO] - 1), 0)
            root(2, rstd1)
            for t in range(TT):
                token_bank(2 * TT + t, ytok[:, t, :], t)

        @block.vector
        def _(dve):
            v = nc.vector

            def copy_x(u, dst):
                for k in range(KT):
                    dve.wait_ge(xt_ready, KT * u + k + 1)
                    v.tensor_copy(dst[:, k, 512:TOKENS], ps[:, 2 * (k % 2) + 1, 0:LAST]).then_inc(xt_d, 1)

            def normalise(u, src, w0, rs):
                dve.wait_ge(sq_used, KT * (u + 1))
                v.tensor_scalar(halves(rs), ps[:, 4:6, 0:HALF], 1.0 / D, EPS, ALU.mult, ALU.add).then_inc(ms_ready, 1)
                dve.wait_ge(rt_ready, u + 1)
                v.reciprocal(rs, rs).then_inc(rc_ready, 1)
                dve.wait_ge(rc_ready, u + 1)
                for k in range(KT):
                    v.scalar_tensor_tensor(xn[:, k, :], src[:, k, :], cols[:, w0 + k:w0 + k + 1], rs,
                                           ALU.mult, ALU.mult).then_inc(xn_ready, 1)

            def k_page(b, p):
                n = b * PAGES + p
                dve.wait_ge(k_in[n % RING], slot_value(n))
                if p == 0:
                    dve.wait_ge(qb_c, b + 1)
                    if b >= 2:
                        dve.wait_ge(d_w, b - 1)
                for h in range(H):
                    kh = kring[:, n % RING, h * P:h * P + P]
                    m = v.tensor_tensor_reduce(kh, kh, qbc[:, b % 2, h * P:h * P + P], 1.0, 0.0, ALU.mult,
                                               ALU.add, dz[:, b % 2, p * H + h:p * H + h + 1])
                m.then_inc(k_used, 1)

            def scale_scores(b):
                dve.wait_ge(k_used, PAGES * (b + 1))
                z = dz[:, b % 2, :].rearrange("p (a h) -> p a h", h=H)
                v.scalar_tensor_tensor(z, z, SCALE, sbb[:, :].unsqueeze(1).to_broadcast([P, PAGES, H]),
                                       ALU.mult, ALU.add).then_inc(dz_ready, 1)

            def chain_sp(b):
                dve.wait_ge(d_ln, b + 1)
                if b >= 1:
                    dve.wait_ge(d_cum, b)
                v.scalar_tensor_tensor(dsp[:, b % 2, :], dz[:, b % 2, :], 0.0, de[:, :], ALU.max, ALU.add)\
                    .then_inc(d_sp, 1)
                dve.wait_ge(d_sp, b + 1)
                src = dsp[:, b % 2, :]
                for i, step in enumerate((H, 2 * H, 4 * H, 8 * H)):
                    dst = dsuf[:, i % 2, :]
                    v.tensor_copy(dst[:, P - step:P], src[:, P - step:P])
                    v.tensor_tensor(dst[:, 0:P - step], src[:, 0:P - step], src[:, step:P], ALU.add).then_inc(d_suf, 1)
                    dve.wait_ge(d_suf, 4 * b + i + 1)
                    src = dst

            def chain_arg(b):
                dve.wait_ge(d_cum, b + 1)
                v.tensor_tensor(dz[:, b % 2, :], dz[:, b % 2, :], ps[:, 4, 0:P], ALU.subtract).then_inc(d_arg, 1)

            def v_page(b, p):
                n = b * PAGES + p
                dve.wait_ge(v_in[n % RING], slot_value(n))
                if p == 0:
                    dve.wait_ge(d_w, b + 1)
                    if b >= 2:
                        dve.wait_ge(v_sum, b - 1)
                else:
                    dve.wait_ge(v_used, n)
                for h in range(H):
                    vh, a = vring[:, n % RING, h * P:h * P + P], vacc[:, b % 2, h * P:h * P + P]
                    w = dw[:, b % 2, p * H + h:p * H + h + 1]
                    if p == 0:
                        m = v.tensor_scalar(a, vh, w, None, ALU.mult)
                    else:
                        m = v.scalar_tensor_tensor(a, vh, w, a, ALU.mult, ALU.add)
                m.then_inc(v_used, 1)

            def token_bank(i, dst, t):
                dve.wait_ge(tok_t, i + 1)
                n = rows_of(t)
                v.tensor_copy(dst[0:n, 512:D], ps[0:n, 2 * (i % 2) + 1, :]).then_inc(tok_d, 1)

            def attend():
                def first(h):
                    dve.wait_ge(s_z, h + 1)
                    if h >= 1:
                        dve.wait_ge(s_sp, h)
                    v.scalar_tensor_tensor(es, zs[:, h % 2, :], -1.0, zs[:, h % 2, :], ALU.mult, ALU.max).then_inc(s_abs, 1)
                    dve.wait_ge(s_ln, h + 1)
                    if h >= 2:
                        dve.wait_ge(s_c, h - 1)
                    v.scalar_tensor_tensor(sps[:, h % 2, :], zs[:, h % 2, :], 0.0, es, ALU.max, ALU.add)\
                        .then_inc(s_sp, 1)

                first(0)
                for h in range(H):
                    if h + 1 < H:
                        first(h + 1)
                    dve.wait_ge(s_c, h + 1)
                    for b in range(3):
                        w = SB_WIDTH[b]
                        zb = zs[:, h % 2, SB_FLAT[b]:SB_FLAT[b] + w]
                        m = v.tensor_tensor(zb, zb, ps[:, 3 + b, 0:w], ALU.subtract)
                    m.then_inc(s_arg, 1)

            def conv(n):
                y = cT[:, n, 0:LP]
                dve.wait_ge(act_read, READ_COUNT[T_SEG + 2 * KT + n])
                for i in range(CW):
                    u, w = upad[:, n % 2, i:i + LP], convw[:, i, n:n + 1]
                    if i == 0:
                        v.tensor_scalar(y, u, w, None, ALU.mult).then_inc(cv_step, 1)
                    else:
                        dve.wait_ge(cv_step, CW * n + i)
                        v.scalar_tensor_tensor(y, u, w, y, ALU.mult, ALU.add).then_inc(cv_step, 1)

            def conv_sampled():
                y = cT[:, :, LP:TOKENS]
                dve.wait_ge(raw_c, NQKV)

                def w(i):
                    return per_head(convw[:, i, :], DB)
                v.tensor_tensor(y, rawt[:, :, 3:11], w(CW - 1), ALU.mult).then_inc(sc_step, 1)
                cb = cbuf[:, :, :].rearrange("p n (b i) -> p n b i", i=3)
                for i in range(3):
                    dve.wait_ge(sc_step, 1 + 2 * i)
                    v.tensor_tensor(cvt, cb[:, :, :, i], w(i), ALU.mult).then_inc(sc_step, 1)
                    dve.wait_ge(sc_step, 2 + 2 * i)
                    v.tensor_tensor(y, y, cvt, ALU.add).then_inc(sc_step, 1)

            def norm_qk():
                def first(n):
                    dve.wait_ge(n_ss, n + 1)
                    if n >= 2:
                        dve.wait_ge(n_done, n - 1)
                    v.tensor_scalar(halves(rstg[:, n % 2, :]), ps[:, 2 * (n % 2):2 * (n % 2) + 2, 0:HALF], 1.0, EPS,
                                    ALU.mult, ALU.add).then_inc(n_ms, 1)

                first(0)
                for n in range(2 * H):
                    if n + 1 < 2 * H:
                        first(n + 1)
                    r = rstg[:, n % 2, :]
                    dve.wait_ge(n_rt, n + 1)
                    v.reciprocal(r, r).then_inc(n_rc, 1)
                    dve.wait_ge(n_rc, n + 1)
                    v.scalar_tensor_tensor(cT[:, n, :], cT[:, n, :], SCALE if n < H else 1.0, r, ALU.mult, ALU.mult)\
                        .then_inc(n_done, 1)

            def decays():
                def t5(x):
                    return x.rearrange("p (t h) -> p t h", h=H)
                v.memset(ab5[:, :, :], 0.0).then_inc(ab_d, 1)
                dve.wait_ge(ab_d, 1)
                dve.wait_ge(ab_t, 1)
                v.tensor_copy(ab5[:, 0:4, :], ps[:, 4, 0:64].rearrange("p (t h) -> p t h", t=4)).then_inc(ab_d, 1)
                v.tensor_copy(ab5[0:LAST, 4, :], ps[0:LAST, 4, 64:80]).then_inc(ab_d, 1)
                dve.wait_ge(ab_d, 3)
                v.tensor_tensor(t5(tmp1), ab5[:, :, 0:H], dtb[:, :].unsqueeze(1).to_broadcast([P, TT, H]), ALU.add)\
                    .then_inc(ab_d, 1)
                dve.wait_ge(ab_a, 4)
                dve.wait_ge(ab_d, 4)
                v.scalar_tensor_tensor(tmp1, tmp1, 0.0, tmp2, ALU.max, ALU.add).then_inc(ab_d, 1)
                dve.wait_ge(ab_d, 5)
                v.scalar_tensor_tensor(t5(gt), t5(tmp1), -1.0, eal[:, 0:H].unsqueeze(1).to_broadcast([P, TT, H]),
                                       ALU.mult, ALU.mult).then_inc(ab_d, 1)
                dve.wait_ge(ab_a, AB_END)
                v.scalar_tensor_tensor(nbG, bt, -1.0, eG, ALU.mult, ALU.mult).then_inc(ab_d, 1)

            def chunks():
                v.memset(S, 0.0).then_inc(g_dve0, 1)
                for c in range(TT):
                    n = chunk(c)

                    def after(eng, *key):
                        s, at_ = {"act": (g_act, ACT_AT), "pe": (g_pe, PE_AT), "pool": (g_pool, POOL_AT),
                                  "dve": (g_dve, DVE_AT)}[eng]
                        if key[0] >= 0:
                            dve.wait_ge(s, at_[key])

                    def hs(g):
                        return slice(4 * g, 4 * g + 4)

                    def bank(i, w, m=n):
                        return ps[0:m, i, 0:4 * w].rearrange("p (h j) -> p h j", h=4)

                    def one(x, h):
                        return x[0:n, H * c + h:H * c + h + 1]

                    for g in G2:
                        after("pe", c - 1, "kv", g)
                        after("pe", c, "tk", g)
                        v.tensor_tensor(krs[0:n, hs(g), :], bank(g, P),
                                        per_head(eR[0:n, H * c + 4 * g:H * c + 4 * g + 4], P), ALU.mult).then_inc(g_dve, 1)
                    for g in G2:
                        after("pe", c, "tv", g)
                        v.tensor_tensor(bvs[0:n, hs(g), :], bank(2 + g, P),
                                        per_head(bt[0:n, H * c + 4 * g:H * c + 4 * g + 4], P), ALU.mult).then_inc(g_dve, 1)
                    for g in G2:
                        after("pe", c, "kk", g)
                        after("pool", c, "dr", g)
                        for h in range(4 * g, 4 * g + 4):
                            i = (h % 4) * n
                            m = v.scalar_tensor_tensor(DR[0:n, h, 0:n], ps[0:n, g, i:i + n], one(bt, h), DR[0:n, h, 0:n],
                                                       ALU.mult, ALU.mult)
                        m.then_inc(g_dve, 1)
                    for g in G2:
                        after("pe", c, "kq", g)
                        after("pool", c, "dc", g)
                        v.tensor_tensor(DC[0:n, hs(g), 0:n], bank(2 + g, n), DC[0:n, hs(g), 0:n], ALU.mult).then_inc(g_dve, 1)
                    idb = ident[0:n, 0:n].unsqueeze(1).to_broadcast([n, 4, n])
                    for g in G2:
                        after("pe", c, "lt", g)
                        v.tensor_tensor(Um[0:n, hs(g), 0:n], idb, bank(4 + g, n), ALU.subtract).then_inc(g_dve, 1)
                        v.tensor_tensor(Tm[0:n, hs(g), 0:n], idb, Lm[0][0:n, hs(g), 0:n], ALU.subtract).then_inc(g_dve, 1)
                    for s in LEVELS[c][1:]:
                        w = n // 2
                        for g in G2:
                            after("pe", c, "up", s, g)
                            ue, te = odd(Um[0:n, hs(g), 0:n], s), even(Tm[0:n, hs(g), 0:n], s)

                            def upd(o):
                                return ps[0:n, 2 + g, o:o + 4 * w].rearrange("p (h b s) -> p h b s", h=4, s=s)
                            v.tensor_tensor(ue, ue, upd(0), ALU.subtract).then_inc(g_dve, 1)
                            if 2 * s < n:
                                v.tensor_tensor(te, te, upd(256), ALU.subtract).then_inc(g_dve, 1)
                    for g in G2:
                        after("pe", c, "ks", g)
                        for h in range(4 * g, 4 * g + 4):
                            i = (h % 4) * P
                            m = v.scalar_tensor_tensor(bvs[0:n, h, :], ps[0:n, 4 + g, i:i + P], one(nbG, h), bvs[0:n, h, :],
                                                       ALU.mult, ALU.add)
                        m.then_inc(g_dve, 1)
                    for g in G2:
                        after("pe", c, "o2", g)
                        after("act", c, "qs", g)
                        v.tensor_tensor(Q1[0:n, hs(g), :], Q1[0:n, hs(g), :], bank(2 + g, P), ALU.add).then_inc(g_dve, 1)
                    after("pool", c, "sq")
                    v.tensor_reduce(onr[0:n, 0:H], Lm[0][0:n, :, :], AX.X, ALU.add).then_inc(g_dve, 1)
                    after("dve", c, "ss")
                    v.tensor_scalar(onr[0:n, 0:H], onr[0:n, 0:H], 1.0 / P, EPS, ALU.mult, ALU.add).then_inc(g_dve, 1)
                    for g in G2:
                        after("pe", c, "kv", g)
                        for h in range(4 * g, 4 * g + 4):
                            i = (h % 4) * P
                            m = v.scalar_tensor_tensor(S[:, h, :], S[:, h, :], eL[:, H * c + h:H * c + h + 1],
                                                       ps[:, 4 + g, i:i + P], ALU.mult, ALU.add)
                        m.then_inc(g_dve, 1)
                    after("act", c, "rt")
                    v.reciprocal(onr[0:n, 2 * H:3 * H], onr[0:n, H:2 * H]).then_inc(g_dve, 1)
                    after("dve", c, "rc")
                    v.tensor_tensor(Q1[0:n, :, :], Q1[0:n, :, :], per_head(onr[0:n, 2 * H:3 * H], P), ALU.mult)\
                        .then_inc(g_dve, 1)

            def sampled_delta():
                count = [0]

                def step(ins):
                    ins.then_inc(t_dve, 1)
                    count[0] += 1
                    dve.wait_ge(t_dve, count[0])

                def bh(x):
                    return x.rearrange("p (b h) -> p b h", h=H)

                def of(i):
                    return cT[:, H * i:H * i + H, LP:TOKENS].rearrange("p h b -> p b h")
                qk, kk, t1, vn, t2, o, osq, rs, eg, be = (dsm[:, i, :] for i in range(10))
                dve.wait_ge(n_done, 2 * H)
                step(v.tensor_tensor(bh(qk), of(0), of(1), ALU.mult))
                step(v.tensor_copy(bh(kk), of(1)))
                dve.wait_ge(t_pe, 2)
                sqk = ps[:, 0, 0:P].rearrange("p (r two) -> p r two", two=2)
                step(v.tensor_tensor(t1, sqk[:, :, 1], eg, ALU.mult))
                step(v.tensor_tensor(bh(t1), of(2), bh(t1), ALU.subtract))
                step(v.tensor_tensor(vn, t1, be, ALU.mult))
                step(v.tensor_tensor(t2, sqk[:, :, 0], eg, ALU.mult))
                step(v.tensor_tensor(o, vn, ps[:, 1, 0:64], ALU.mult))
                step(v.tensor_tensor(o, o, t2, ALU.add))
                step(v.tensor_tensor(osq, o, o, ALU.mult))
                dve.wait_ge(t_pe, 3)
                step(v.tensor_copy(vrow[:, :], ps[0:64, 2, 0:P]))
                step(v.tensor_copy(krow[:, :], ps[0:64, 2, P:2 * P]))
                dve.wait_ge(t_act, 2)
                step(v.reciprocal(rs, rs))
                step(v.tensor_tensor(o, o, rs, ALU.mult))
                for j in range(4):
                    for i in range(4):
                        dve.wait_ge(t_pe, 5 + 4 * j + i)
                        for r4 in range(4):
                            r = 16 * j + 4 * i + r4
                            m = v.scalar_tensor_tensor(st[:, r, :], st[:, r, :], eg[:, r:r + 1],
                                                       ps[:, 4 + i, r4 * P:r4 * P + P], ALU.mult, ALU.add)
                        m.then_inc(t_dve, 1)

            v.memset(epsc[:, :], EPS).then_inc(eps_ready, 1)
            copy_x(0, hT0)
            dve.wait_ge(par_t, 1)
            v.tensor_copy(cols[:, 0:25], ps[:, 6, 0:25]).then_inc(par_c, 1)
            v.tensor_copy(convw[:, :, :], ps[:, 6, P:P + 96].rearrange("p (i n) -> p i n", i=CW)).then_inc(par_c, 1)
            dve.wait_ge(par_c, 2)
            dve.wait_ge(xt_a, KT)
            dve.wait_ge(xt_d, KT)
            normalise(0, hT0, 0, rstd)
            dve.wait_ge(par_t, 2)
            for i in range(2):
                v.tensor_copy(cbuf[:, 12 * i:12 * i + 12, :],
                              ps[:, 6 + i, 0:288].rearrange("p (n c) -> p n c", n=12)).then_inc(cb_c, 1)
            dve.wait_ge(xn_ready, KT)
            v.memset(R[:, 2 * A8:2 * A8 + P], 0.0).then_inc(kpad, 1)
            dve.wait_ge(qr_t, 1)
            v.tensor_copy(qrow[:, :].rearrange("p (a n) -> p a n", a=2), ps[0:DB, 6:8, :]).then_inc(qr_c, 1)
            for s in range(SEGS):
                if s >= 1:
                    chain_sp(s - 1)
                if s == 2:
                    v.memset(upad[:, :, 0:CW - 1], 0.0).then_inc(up_zero, 1)
                for q in range(4):
                    if s in (2, 3, 4) and (s - 2) * KT + 2 * q >= 2:
                        conv((s - 2) * KT + 2 * q - 2)
                        conv((s - 2) * KT + 2 * q - 1)
                    if s == 7:
                        for j in (2 * q, 2 * q + 1):
                            dve.wait_ge(act_read, READ_COUNT[T_SEG + 6 * KT + j])
                            dve.wait_ge(w_used, done(T_SEG + s * KT + j))
                            v.tensor_tensor(halves(mT[:, j, :]), halves(sgA[:, j, :]), pair(T_SEG + s * KT + j), ALU.mult)\
                                .then_inc(dve_read, 1)
                    if s < DB:
                        for p in range(4 * q, 4 * q + 4):
                            k_page(s, p)
                    if s >= 1 and q == 0:
                        chain_arg(s - 1)
                    if s >= 1:
                        for p in range(4 * q, 4 * q + 4):
                            v_page(s - 1, p)
                if s < DB:
                    scale_scores(s)
                if s == 1:
                    for t in range(TT):
                        token_bank(t, vtok[:, t, :], t)
                    for t in range(TT):
                        if t >= 2:
                            dve.wait_ge(k_out[t % 2], 16 * (t // 2))
                        token_bank(TT + t, ktok[:, t % 2, :], t)
                    attend()
                    dve.wait_ge(s_av, H)
                    dve.wait_ge(v_out, 16 * 6)
                if s == 4:
                    conv(NQKV - 2)
                    conv(NQKV - 1)
                    conv_sampled()
                    for i in range(6):
                        dve.wait_ge(co_t, i + 1)
                        v.tensor_copy(convrow_sb[0:11, i * 512:i * 512 + 512], ps[0:11, i % 2, :]).then_inc(co_c, 1)
                    norm_qk()
                    decays()
                    chunks()
                    sampled_delta()
            for n in range(KT):
                dve.wait_ge(act_read, READ_COUNT[T_SEG + 8 * KT + n])
                dve.wait_ge(w_used, done(T_PB + n))
                v.tensor_tensor(halves(sgB[:, n, :]), halves(sgB[:, n, :]), pair(T_PB + n), ALU.mult).then_inc(dve_read, 1)
                dve.wait_ge(dve_read, READ_COUNT[T_PB + n])
                v.tensor_tensor(mT[:, n, :], mT[:, n, :], sgB[:, n, :], ALU.add).then_inc(m_done, 1)
            copy_x(1, hT)
            dve.wait_ge(xt_a, 2 * KT)
            dve.wait_ge(xt_d, 2 * KT)
            for n in range(KT):
                dve.wait_ge(w_used, done(T_O + n))
                v.tensor_tensor(halves(hT[:, n, :]), halves(hT[:, n, :]), pair(T_O + n), ALU.add).then_inc(dve_read, 1)
            dve.wait_ge(dve_read, READ_COUNT[T_O + KT - 1])
            normalise(1, hT, KT, rstd1)
            for n in range(FT):
                dve.wait_ge(act_read, READ_COUNT[T_FI + 2 * n])
                dve.wait_ge(w_used, done(T_FI + 2 * n + 1))
                v.tensor_tensor(halves(hid[:, n, :]), halves(gtmp[:, n % 2, :]), pair(T_FI + 2 * n + 1), ALU.mult)\
                    .then_inc(dve_read, 1)
            for n in range(KT):
                dve.wait_ge(w_used, done(T_FO + n))
                v.tensor_tensor(halves(hT[:, n, :]), halves(hT[:, n, :]), pair(T_FO + n), ALU.add).then_inc(dve_read, 1)
            dve.wait_ge(dve_read, READ_COUNT[T_FO + KT - 1])
            normalise(2, hT, 2 * KT, rstd1)
            for t in range(TT):
                token_bank(2 * TT + t, ytok[:, t, :], t)

        @block.gpsimd
        def _(pool):
            g_ = nc.gpsimd

            def keep(out, in_, pattern, base, cm, op=ALU.is_ge, fill=0.0):
                return g_.affine_select(out=out, in_=in_, pattern=pattern, compare_op=op, fill=fill,
                                        base=base, channel_multiplier=cm)
            for m in (ident, zeros):
                g_.memset(m[:, :], 0.0).then_inc(const_step, 1)
            for m in (ones, tri_ge, tri_le, tri_gt):
                g_.memset(m[:, :], 1.0).then_inc(const_step, 1)
            g_.memset(lvl[:, :, :], 1.0).then_inc(const_step, 1)
            g_.memset(sel[:, :, :], 1.0).then_inc(const_step, 1)
            pool.wait_ge(const_step, 8)
            keep(ident[:, :], ident[:, :], [[-1, P]], 0, 1, ALU.not_equal, 1.0).then_inc(const_ready, 1)
            keep(tri_ge[:, :], tri_ge[:, :], [[-1, P]], 0, 1).then_inc(const_ready, 1)
            keep(tri_le[:, :], tri_le[:, :], [[1, P]], 0, -1).then_inc(const_ready, 1)
            keep(tri_gt[:, :], tri_gt[:, :], [[-1, P]], 0, 1, ALU.is_gt).then_inc(const_ready, 1)
            keep(sel[:, :, :], sel[:, :, :], [[-1, DB], [0, P]], 0, 1, ALU.is_equal).then_inc(const_ready, 1)
            for i in range(7):
                s = 1 << i
                v = lvl[:, i, :].rearrange("p (b two s) -> p b two s", two=2, s=s)
                nb = P // (2 * s)
                g_.memset(v[:, :, 1, :], 0.0).then_inc(const_step, 1)
                keep(v[:, :, 0, :], v[:, :, 0, :], [[-2 * s, nb], [0, s]], -s, 1).then_inc(const_step, 1)
            pool.wait_ge(const_step, 8 + 14)
            for i in range(7):
                s = 1 << i
                v = lvl[:, i, :].rearrange("p (b two s) -> p b two s", two=2, s=s)
                keep(v[:, :, 0, :], v[:, :, 0, :], [[2 * s, P // (2 * s)], [0, s]], 2 * s - 1, -1).then_inc(const_ready, 1)

            def causal(buf, fill, sig):
                for kt in range(TT):
                    n = chunk(kt)
                    f = sb_at(kt, P * kt)[2]
                    m = keep(buf[:, f:f + n], buf[:, f:f + n], [[1, n]], 0, -1, ALU.is_gt, fill)
                m.then_inc(sig, 1)

            pool.wait_ge(s_sp, 1)
            causal(sps[:, 0, :], 0.0, s_msp)
            for h in range(H):
                if h + 1 < H:
                    pool.wait_ge(s_sp, h + 2)
                    causal(sps[:, (h + 1) % 2, :], 0.0, s_msp)
                pool.wait_ge(s_arg, h + 1)
                causal(zs[:, h % 2, :], NEG, s_marg)
            for n in range(NQKV):
                pool.wait_ge(act_read, READ_COUNT[T_SEG + 2 * KT + n])
                g_.tensor_copy(rawt[:, n, :], upad[:, n % 2, CW - 1 + LP - 3:CW - 1 + TOKENS]).then_inc(raw_c, 1)
            pool.wait_ge(ab_d, AB_G)
            g_.tensor_copy(gP[:, 0:32], gt[:, 0:32]).then_inc(ab_p, 1)
            keep(gP[:, 32:40], gt[:, 32:40], [[0, H]], LASTP - 1, -1).then_inc(ab_p, 1)
            pool.wait_ge(ab_p, 2)
            for c in range(TT):
                n = chunk(c)

                def after(eng, *key):
                    s, at_ = {"act": (g_act, ACT_AT), "pe": (g_pe, PE_AT), "dve": (g_dve, DVE_AT)}[eng]
                    if key[0] >= 0:
                        pool.wait_ge(s, at_[key])

                def hs(g):
                    return slice(4 * g, 4 * g + 4)
                after("pe", c - 1, "kv", 1)
                if c == 0:
                    pool.wait_ge(c_out, 16 * 3)
                    pool.wait_ge(n_done, 2 * H)
                g_.tensor_tensor(gm[0:n, :, 0:n], tri_gt[0:n, 0:n].unsqueeze(1).to_broadcast([n, H, n]),
                                 per_head(gP[0:n, H * c:H * c + H], n), ALU.mult).then_inc(g_pool, 1)
                for g in G2:
                    after("act", c, "dr", g)
                    keep(DR[0:n, hs(g), 0:n], DR[0:n, hs(g), 0:n], [[0, 4], [-1, n]], 0, 1, ALU.is_gt).then_inc(g_pool, 1)
                for g in G2:
                    after("act", c, "dc", g)
                    keep(DC[0:n, hs(g), 0:n], DC[0:n, hs(g), 0:n], [[0, 4], [1, n]], 0, -1).then_inc(g_pool, 1)
                for j, s in enumerate(LEVELS[c]):
                    for g in G2:
                        if j == 0:
                            after("dve", c, "A", g)
                            if c:
                                after("dve", c - 1, "ss")
                        elif j == 2:
                            after("dve", c, "T1", g)
                            after("pe", c, "lt", g)
                        elif j >= 3:
                            after("pe", c, "q1", LEVELS[c][j - 2], g)
                        elif j == 1 and c:
                            after("pe", c - 1, "q1", LEVELS[c - 1][-1], g)
                        g_.tensor_tensor(Lm[j % 2][0:n, hs(g), 0:n], DR[0:n, hs(g), 0:n],
                                         lvl[0:n, j, 0:n].unsqueeze(1).to_broadcast([n, 4, n]), ALU.mult)\
                            .then_inc(g_pool, 1)
                after("dve", c, "o", 0)
                after("dve", c, "o", 1)
                g_.tensor_tensor(Lm[0][0:n, :, :], Q1[0:n, :, :], Q1[0:n, :, :], ALU.mult).then_inc(g_pool, 1)
            pool.wait_ge(t_dve, T_ROWS)
            for j in range(4):
                if j:
                    pool.wait_ge(t_pe, 4 + 4 * j)
                g_.tensor_tensor(ksel[:, :, :], krow[:, :].unsqueeze(1).to_broadcast([64, 16, P]),
                                 per_head(ident[64:P, 64 + 16 * j:64 + 16 * j + 16], P), ALU.mult).then_inc(t_pool, 1)
            pool.wait_ge(t_act, 3)
            for j in range(KT):
                pool.wait_ge(act_read, READ_COUNT[T_SEG + 5 * KT + j])
                g_.tensor_tensor(oaT[:, j, :], oaT[:, j, :], ztmp[:, j % 2, :], ALU.mult).then_inc(z_done, 1)


NPHYS = 160
NCONST = 12
AB_X, AB_G, AB_B, AB_END, AB_DEND = 4, 6, 5, 10, 7
T_VN, T_OSQ, T_ROWS, T_ON, T_S0 = 5, 9, 11, 13, 13
T_PE_END = 20
_VIEWS = {
    "x_prompt": (SEQ, D), "x_sample": (DB, D), "cache_k": (NPHYS, PAGE, D), "cache_v": (NPHYS, PAGE, D),
    "state_rec": (DB, H, P, P), "state_conv": (DB * 3, 3 * D), "page_table": (1, DB * PAGES),
    "meta_tokens": (META, D), "norm_mix": (KT, P), "w_in": (D, 9232), "conv_w": (CW * NQKV, P),
    "a_log": (1, H), "dt_bias": (1, H), "gdn_norm": (1, P), "sb_bias": (1, H), "w_pa": (D, D), "w_pb": (D, D),
    "w_o": (D, D), "norm_ffn": (KT, P), "w_ffn_in": (D, 2 * D_FF), "w_ffn_out": (D_FF, D), "norm_final": (KT, P),
}
_OUTS = [("y_prompt", (SEQ, D), (1, SEQ, D)), ("y_sample", (DB, D), (DB, 1, D)),
         ("k_prompt", (LP, D), (1, 1, LP, H, P)), ("v_prompt", (LP, D), (1, 1, LP, H, P)),
         ("k_sample", (DB, D), (1, DB, 1, H, P)), ("v_sample", (DB, D), (1, DB, 1, H, P)),
         ("rec_prompt", (H, P, P), (1, 1, H, P, P)), ("rec_sample", (DB, H, P, P), (1, DB, H, P, P)),
         ("conv_prompt", (3, 3 * D), (1, 1, 3, 3 * D)), ("conv_sample", (DB, 3, 3 * D), (1, DB, 3, 3 * D))]


def kernel(**inputs):
    import numpy as _np
    import concourse.bacc as _bacc
    from concourse.bass_utils import run_bass_kernel_spmd as _run

    nc = _bacc.Bacc("TRN2", target_bir_lowering=False, num_devices=1)
    arrays, io = {}, {}
    for name, shape in _VIEWS.items():
        a = _np.ascontiguousarray(inputs[name]).reshape(shape)
        arrays[f"in_{name}"] = a
        io[name] = nc.dram_tensor(f"in_{name}", shape, mybir.dt.from_np(a.dtype), kind="ExternalInput").ap()
    io["state_conv3"] = io["state_conv"].rearrange("(b i) n -> b i n", i=3)
    for name, shape, _ in _OUTS:
        io[name] = nc.dram_tensor(f"out_{name}", shape, F32, kind="ExternalOutput").ap()
    build(nc, io)
    r = _run(nc, [arrays], core_ids=[0])
    return tuple(r.results[0][f"out_{name}"].reshape(whole) for name, _, whole in _OUTS)
```

```python
from contextlib import ExitStack

import concourse.bass as bass
from concourse import mybir

F32 = mybir.dt.float32
F32R = mybir.dt.float32r
I32 = mybir.dt.int32
ALU = mybir.AluOpType
ACT = mybir.ActivationFunctionType
AX = mybir.AxisListType

P = 128
D = 1024
KT = D // P
META, SEQ, DB = 16, 512, 8
LP = META + SEQ
TOKENS = LP + DB
HALF = TOKENS // 2
TT = 5
LAST = TOKENS - 4 * P
LASTP = LP - 4 * P
H = 8
PAGES, PAGE = 16, 128
CW = 4
D_FF = 2816
FT = D_FF // P
SCALE = float(P) ** -0.5
EPS = 1e-6
NQKV = 24
SEGS = 9
RING = 4
NEG = -1.0e30

C_QKV, C_Z, C_AB, C_Q, C_K, C_V, C_GA, C_GB = 0, 3072, 4096, 4112, 5136, 6160, 7184, 8208
SEG_W = [("w_in", C_K), ("w_in", C_V), ("w_in", C_QKV), ("w_in", C_QKV + D), ("w_in", C_QKV + 2 * D),
         ("w_in", C_Z), ("w_in", C_GA), ("w_pa", 0), ("w_in", C_GB)]

def weight_pieces():
    out = [("w_in", C_AB, 0, KT, 2 * H)]
    out += [("w_in", C_Q + P * n, 0, KT, P) for n in range(KT)]
    for name, col in SEG_W:
        out += [(name, col + P * n, 0, KT, P) for n in range(KT)]
    out += [("w_pb", P * n, 0, KT, P) for n in range(KT)]
    out += [("w_o", P * n, 0, KT, P) for n in range(KT)]
    for n in range(FT):
        out += [("w_ffn_in", P * n, 0, KT, P), ("w_ffn_in", D_FF + P * n, 0, KT, P)]
    for n in range(KT):
        out += [("w_ffn_out", P * n, 0, 8, P), ("w_ffn_out", P * n, 8, 16, P), ("w_ffn_out", P * n, 16, 22, P)]
    return out


T_AB, T_Q, T_SEG = 0, 1, 9
T_PB = T_SEG + SEGS * KT
T_O = T_PB + KT
T_FI = T_O + KT
T_FO = T_FI + 2 * FT
TILES = T_FO + KT


def reader(t):
    if T_SEG + 7 * KT <= t < T_SEG + 8 * KT or T_PB <= t < T_FI or t >= T_FO:
        return "dve"
    if T_FI <= t < T_FO:
        return "act" if (t - T_FI) % 2 == 0 else "dve"
    return "act"


READ_COUNT = []
for _t in range(TILES):
    READ_COUNT.append(sum(reader(u) == reader(_t) for u in range(_t + 1)))


def piece_of(t):
    return t if t < T_FO else T_FO + 3 * (t - T_FO)


SB_PIECES = [(0, 0, 512, 0, 0),
             (1, 128, 528, 1, 0), (0, 512, 528, 1, 400), (4, 512, 528, 1, 416),
             (2, 256, 528, 2, 0), (3, 384, 528, 2, 272)]
SB_WIDTH = [512, 432, 416]
SB_FLAT = [0, 512, 944]
SB_ALL = 1360


def sb_at(kt, q):
    for k, a, b, bank, col in SB_PIECES:
        if k == kt and a <= q < b:
            return bank, col + q - a, SB_FLAT[bank] + col + q - a


K_IN = {0: (0,), 1: (1,), 3: (3,), 5: (4, 5), 6: (6,), 7: (7,)}
V_IN = {1: (0,), 2: (2,), 4: (3,), 6: (4,), 7: (5,), 8: (6, 7)}
K_ATT, V_ATT = 2, 1
CHAIN_IN = {1: 0, 2: 2, 4: 3, 6: 4, 7: 5, 8: 6}
SUM_IN = {2: 1, 3: 2, 7: 4, 8: 5}


def pages_of(seqs, part, parts):
    every = [(b, p) for b in seqs for p in range(PAGES)]
    n = len(every) // parts
    return every[n * part:n * part + n]


def fr(v):
    return v.bitcast(F32R)


def build(nc, io):
    with ExitStack() as ctx:
        def sb(name, shape, dt=F32):
            return ctx.enter_context(nc.sbuf_tensor(name, shape, dt))

        def twins(name, shape):
            with nc.sbuf_tensor(name + "_split", shape, F32) as split:
                pass
            return sb(name, shape), split

        def sem(name):
            return ctx.enter_context(nc.semaphore(name))

        ps = ctx.enter_context(nc.psum_tensor("ps", [P, 8, 512], F32))

        xn, xn2 = twins("xn", [P, KT, TOKENS])
        obT, obT2 = twins("obT", [P, H, TOKENS])
        wring, wring2 = twins("wring", [P, RING, KT * P])
        kring, kring2 = twins("kring", [P, RING, D])
        vring, vring2 = twins("vring", [P, RING, D])
        qbc, qbc2 = twins("qbc", [P, 2, D])
        vacc, vacc2 = twins("vacc", [P, 2, D])
        rows, rows2 = twins("rows", [P, D])
        qrow = rows[0:DB, :]
        dz = sb("dz", [P, 3, P])
        de = sb("de", [P, P])
        dsp = sb("dsp", [P, P])
        dsuf = sb("dsuf", [P, 2, P])
        dw = sb("dw", [P, 2, P])
        ident = sb("ident", [P, P])
        ones = sb("ones", [P, P])
        tri_ge = sb("tri_ge", [P, P])
        tri_le = sb("tri_le", [P, P])
        tri_gt = sb("tri_gt", [P, P])
        lvl, lvl2 = twins("lvl", [P, 7, P])
        sel = sb("sel", [DB, DB, P])
        cols = sb("cols", [P, 32])
        convw = sb("convw", [P, CW, NQKV])
        alog = sb("alog", [P, H])
        dtb = sb("dtb", [P, H])
        sbb = sb("sbb", [P, H])
        ptab = sb("ptab", [1, DB * PAGES], I32)
        rawt = sb("rawt", [P, NQKV, 11])
        cbuf = sb("cbuf", [P, NQKV, 3 * DB])
        abT = rows[32:32 + 2 * H, 0:TOKENS]
        R, R2 = twins("R", [P, 21056])

        def at(o, *shape):
            n = 1
            for s in shape:
                n *= s
            v = R[:, o:o + n]
            if len(shape) == 2:
                v = v.rearrange("p (a b) -> p a b", a=shape[0])
            return v

        A8 = KT * TOKENS
        xs0 = at(0, TT, D)
        hT0 = at(5120, KT, TOKENS)
        cst = at(9408, 3 * D)
        sq = at(12480, 2, TOKENS)
        rstd = at(13552, TOKENS)
        prow = at(14088, P)
        crow = at(14216, P)
        qbT = at(0, H, TOKENS)
        kbT = at(A8, H, TOKENS)
        kbflat = R[:, A8:2 * A8 + P]
        vtok = at(2 * A8 + P, TT, D)
        SBT = 2 * A8 + P + TT * D
        vbT = at(SBT, H, TOKENS)
        ktok = at(SBT + A8, 2, D)
        zs = at(SBT, 2, SB_ALL)
        sps = at(SBT + 2 * SB_ALL, 2, SB_ALL)
        es = at(SBT + 4 * SB_ALL, SB_ALL)
        cT = at(0, NQKV, TOKENS)
        oaT = at(0, H, TOKENS)
        G0 = 3 * A8
        upad = at(G0, 2, 3 + TOKENS)
        krs, bvs, gmA, DR, DC, Tm, Q1 = (at(G0 + i * 1024, H, P) for i in range(7))
        gms = [gmA, kring[:, 0, :].rearrange("p (h j) -> p h j", h=H)]
        vnb = kring[:, 1, :].rearrange("p (h j) -> p h j", h=H)
        Lm = [kring[:, 2 + i, :].rearrange("p (h j) -> p h j", h=H) for i in range(2)]
        vflat = vring[:, 2:4, :].rearrange("p a n -> p (a n)")
        SQB = 7
        sqg = kring[:, :, :].rearrange("p a n -> p (a n)")[:, 0:SQB * TOKENS].rearrange("p (a t) -> p a t", a=SQB)
        dg = vflat[:, 0:D].rearrange("p (h j) -> p h j", h=H)
        nrm = vflat[:, 1088:1088 + 11 * 80].rearrange("p (a t) -> p a t", a=11)
        Um = vacc[:, 0, :].rearrange("p (h j) -> p h j", h=H)
        S = vacc[:, 1, :].rearrange("p (h j) -> p h j", h=H)
        cvt = at(G0 + 6 * 1024, NQKV, DB)
        st = at(G0, 64, P)
        ksel = vring[64:P, 0:2, :].rearrange("p a (r j) -> p (a r) j", r=8)
        sgA = at(A8, KT, TOKENS)
        sgB = at(A8 + TT * D, KT, TOKENS)
        mT = at(2 * A8 + TT * D, KT, TOKENS)
        ztmp = at(3 * A8 + TT * D, 2, TOKENS)
        hT = at(0, KT, TOKENS)
        xs1 = at(A8, TT, D)
        hid = at(A8, FT, TOKENS)
        gtmp = at(A8 + FT * TOKENS, 2, TOKENS)
        sq1 = at(3 * A8 + TT * D, 2, TOKENS)
        rstd1 = at(3 * A8 + TT * D + 2 * TOKENS, TOKENS)
        ytok = at(A8, TT, D)
        whi, wlo = vring2, wring2

        def flat(buf):
            return buf[:, :, :].rearrange("p a n -> p (a n)")

        def cut(buf, n, o=0):
            return [buf[:, o + i * TOKENS:o + (i + 1) * TOKENS] for i in range(n)]

        def low_parts(ob, r, k, q, va, lv, ro):
            return (cut(r, KT, 2 * A8 + TT * D), cut(flat(ob), KT),
                    cut(flat(k), 7) + cut(r, 7, A8 + (FT + 2) * TOKENS) + cut(flat(q), 3) + cut(flat(va), 3)
                    + cut(flat(lv), 1) + cut(ro, 1))
        m_full, x_full, h_full = low_parts(obT, R, kring, qbc, vacc, lvl, rows)
        m_lo, x_lo, h_lo = low_parts(obT2, R2, kring2, qbc2, vacc2, lvl2, rows2)
        m_hi = cut(flat(kring2), 7) + cut(flat(qbc2), 1)
        x_hi = cut(flat(xn2), KT)
        h_hi = cut(R2, FT, A8)
        sq2, rstd2 = obT[:, 0:2, :], obT[:, 2, :]
        small = sb("small", [P, 11, 40])
        gt, bt, gP, eG, eR, eL, nbG, tmp1, tmp2, eal = (small[:, i, :] for i in range(10))
        onr = small[:, 10, :]
        srow = sb("srow", [1, P])
        dsm = sb("dsm", [P, 10, 64])
        krow, vrow = rows[64:P, 0:P], rows[64:P, P:2 * P]

        zeros = sb("zeros", [P, 1])
        nr_q, nr_t, nr_r = (nrm[:, i, :] for i in range(3))
        rq, rq2, lnk, btk = (nrm[:, 3 + i // 2, 40 * (i % 2):40 * (i % 2) + 40] for i in range(4))
        nr_s = vflat[:, 1088 + 400:1088 + 400 + P]
        epsc = sb("epsc", [P, 1])
        ab5 = sb("ab5", [P, TT, 2 * H])
        convrow_sb = R[:, G0 + 2 * 1024:G0 + 5 * 1024]
        g_dve0, eps_ready, kpad = sem("g_dve0"), sem("eps_ready"), sem("kpad")

        def convrows(a, b):
            return convrow_sb[a:b, :]

        const_step, const_ready = sem("const_step"), sem("const_ready")
        x_in = [sem("x_in0"), sem("x_in1")]
        par_in, pt_in, cst_in = sem("par_in"), sem("pt_in"), sem("cst_in")
        w_in_slot = [sem(f"w_in_slot{i}") for i in range(RING)]
        k_in = [sem(f"k_in{i}") for i in range(RING)]
        v_in = [sem(f"v_in{i}") for i in range(RING)]
        w_used = sem("w_used")
        act_read = sem("act_read")
        dve_read = sem("dve_read")
        k_used, v_used = sem("k_used"), sem("v_used")
        xt_ready, xt_a, xt_d = sem("xt_ready"), sem("xt_a"), sem("xt_d")
        sq_ready, sq_used = sem("sq_ready"), sem("sq_used")
        ms_ready, rt_ready, rc_ready, xn_ready = sem("ms_ready"), sem("rt_ready"), sem("rc_ready"), sem("xn_ready")
        par_t, par_c, cb_c = sem("par_t"), sem("par_c"), sem("cb_c")
        qr_t, qr_c, qb_t, qb_c = sem("qr_t"), sem("qr_c"), sem("qb_t"), sem("qb_c")
        dz_raw, dz_ready = sem("dz_raw"), sem("dz_ready")
        d_abs, d_exp, d_ln, d_sp, d_suf = sem("d_abs"), sem("d_exp"), sem("d_ln"), sem("d_sp"), sem("d_suf")
        d_cum, d_arg, d_w = sem("d_cum"), sem("d_arg"), sem("d_w")
        v_sum, ob_s = sem("v_sum"), sem("ob_s")
        tok_t, tok_a, tok_d = sem("tok_t"), sem("tok_a"), sem("tok_d")
        k_out, v_out, c_out, r_out, y_out = [sem("k_out0"), sem("k_out1")], sem("v_out"), sem("c_out"), sem("r_out"), sem("y_out")
        s_s, s_z, s_abs, s_exp, s_ln, s_sp = (sem(n) for n in ("s_s", "s_z", "s_abs", "s_exp", "s_ln", "s_sp"))
        s_msp, s_c, s_arg, s_marg, s_w, s_av, s_o = (sem(n) for n in ("s_msp", "s_c", "s_arg", "s_marg", "s_w", "s_av", "s_o"))
        up_zero, cv_step, cs_done, raw_c = sem("up_zero"), sem("cv_step"), sem("cs_done"), sem("raw_c")
        sc_step = sem("sc_step")
        n_sq, n_ss, n_act, n_dve = (sem(n) for n in ("n_sq", "n_ss", "n_act", "n_dve"))
        co_t, co_c = sem("co_t"), sem("co_c")
        ab_t, ab_d, ab_a, ab_p, ab_row, ab_m = (sem(n) for n in ("ab_t", "ab_d", "ab_a", "ab_p", "ab_row", "ab_m"))
        g_pe, g_act, g_dve, g_pool = (sem(n) for n in ("g_pe", "g_act", "g_dve", "g_pool"))
        t_in = [sem(f"t_in{i}") for i in range(4)]
        t_pe, t_dve, t_act, t_pool = (sem(n) for n in ("t_pe", "t_dve", "t_act", "t_pool"))
        z_done = sem("z_done")
        w_hi, w_lo = sem("w_hi"), sem("w_lo")
        a_full, a_hi, a_lo = sem("a_full"), sem("a_hi"), sem("a_lo")

        def slot_value(n):
            return 16 * (n // RING + 1)

        pieces = weight_pieces()

        def done(t):
            return piece_of(t) + (3 if t >= T_FO else 1)

        def wait_read(eng, t):
            eng.wait_ge(act_read if reader(t) == "act" else dve_read, READ_COUNT[t])

        def w_load(sp, p):
            name, col, k0, k1, n = pieces[p]
            if p >= RING:
                sp.wait_ge(w_used, p - RING + 1)
            dst = wring[:, p % RING, :].rearrange("p (k n) -> p k n", k=KT)[:, 0:k1 - k0, 0:n]
            src = io[name][k0 * P:k1 * P, col:col + n].rearrange("(k p) n -> p k n", p=P)
            sp.dma_start(dst, src).then_inc(w_in_slot[p % RING], 16)

        def split_hi(act, t):
            for p in range(piece_of(t), done(t)):
                n = (pieces[p][3] - pieces[p][2]) * P
                act.wait_ge(w_in_slot[p % RING], slot_value(p))
                nc.scalar.activation(fr(whi[:, p % RING, 0:n]), wring[:, p % RING, 0:n], ACT.Copy).then_inc(w_hi, 1)

        def split_lo(dve, t):
            for p in range(piece_of(t), done(t)):
                n = (pieces[p][3] - pieces[p][2]) * P
                dve.wait_ge(w_hi, p - piece_of(T_O) + 1)
                nc.vector.tensor_tensor(fr(wlo[:, p % RING, 0:n]), wring[:, p % RING, 0:n], whi[:, p % RING, 0:n],
                                        ALU.subtract).then_inc(w_lo, 1)

        def act_hi(act, i, dst, src):
            if i < 2 * KT:
                act.wait_ge(a_full, i + 1)
            else:
                act.wait_ge(dve_read, READ_COUNT[T_FI + 2 * (i - 2 * KT) + 1])
            nc.scalar.activation(fr(dst), src, ACT.Copy).then_inc(a_hi, 1)

        def act_lo(dve, i, hi, full, lo):
            dve.wait_ge(a_hi, i + 1)
            nc.vector.tensor_tensor(fr(lo), full, hi, ALU.subtract).then_inc(a_lo, 1)

        def w_block(p, k):
            return wring[:, p % RING, :].rearrange("p (k n) -> p k n", k=KT)[:, k, 0:pieces[p][4]]

        def pair(t, m=P):
            return ps[0:m, 2 * (t % 2):2 * (t % 2) + 2, 0:HALF]

        def halves(v):
            return v.rearrange("p (a b) -> p a b", a=2)

        def per_head(v, n):
            return v.unsqueeze(2).to_broadcast([v.shape[0], v.shape[1], n])

        def rows_of(t):
            return LAST if t == 4 else P

        def chunk(c):
            return LASTP if c == 4 else P

        LEVELS = {c: [s for s in (1, 2, 4, 8, 16, 32, 64) if s < chunk(c)] for c in range(TT)}
        G2 = (0, 1)

        def order(per_chunk):
            return {(c,) + k: i + 1 for i, (c, k) in
                    enumerate((c, k) for c in range(TT) for k in per_chunk(c))}

        PE_AT = order(lambda c: [(n, g) for n in ("tk", "tv", "dr", "dc", "kk", "kq", "lt") for g in G2]
                      + [(n, s, g) for s in LEVELS[c][1:] for n in ("q1", "up") for g in G2]
                      + [(n, g) for n in ("ks", "qs", "vn", "o2", "kv", "ot") for g in G2])
        ACT_AT = order(lambda c: [(n, g) for n in ("dr", "dc") for g in G2]
                       + [("q1", s, g) for s in LEVELS[c][1:] for g in G2]
                       + [("qs", 0), ("qs", 1), ("vn", 0), ("vn", 1), ("rt",), ("ot", 0), ("ot", 1)])
        DVE_AT = order(lambda c: [("kr", 0), ("kr", 1), ("bv", 0), ("bv", 1), ("A", 0), ("A", 1), ("qk", 0), ("qk", 1)]
                       + [(n, g) for g in G2 for n in ("U1", "T1")]
                       + [(n, s, g) for s in LEVELS[c][1:] for g in G2
                          for n in (("U", "T") if s != LEVELS[c][-1] else ("U",))]
                       + [("R", 0), ("R", 1), ("o", 0), ("o", 1), ("ss",), ("ms",), ("S", 0), ("S", 1), ("rc",), ("rq",),
                          ("on",)])
        pool_steps = [(0, n) for n in ("gt", "gd", "gm")]
        for c in range(TT):
            pool_steps += [(c, n, g) for n in ("dr", "dc") for g in G2]
            pool_steps += [(c, "L", s, g) for s in LEVELS[c] for g in G2]
            if c + 1 < TT:
                pool_steps += [(c + 1, n) for n in ("gt", "gd", "gm")]
            pool_steps.append((c, "sq"))
        POOL_AT = {key: i + 1 for i, key in enumerate(pool_steps)}

        def even(v, s):
            return v.rearrange("p h (b two s) -> p h b two s", two=2, s=s)[:, :, :, 0, :]

        def odd(v, s):
            return v.rearrange("p h (b two s) -> p h b two s", two=2, s=s)[:, :, :, 1, :]

        block = ctx.enter_context(nc.Block())

        @block.sync
        def _(sp):
            def load_x(u, xs):
                sp.dma_start(xs[0:META, 0, :], io["meta_tokens"]).then_inc(x_in[u], 16)
                sp.dma_start(xs[META:P, 0, :], io["x_prompt"][0:P - META, :]).then_inc(x_in[u], 16)
                sp.dma_start(xs[:, 1:4, :], io["x_prompt"][P - META:4 * P - META, :]
                             .rearrange("(t p) d -> p t d", p=P)).then_inc(x_in[u], 16)
                sp.dma_start(xs[0:LASTP, 4, :], io["x_prompt"][4 * P - META:SEQ, :]).then_inc(x_in[u], 16)
                sp.dma_start(xs[LASTP:LAST, 4, :], io["x_sample"]).then_inc(x_in[u], 16)

            load_x(0, xs0)
            sp.dma_start(prow[0:KT, :], io["norm_mix"]).then_inc(par_in, 16)
            sp.dma_start(prow[KT:2 * KT, :], io["norm_ffn"]).then_inc(par_in, 16)
            sp.dma_start(prow[2 * KT:3 * KT, :], io["norm_final"]).then_inc(par_in, 16)
            sp.dma_start(prow[3 * KT:3 * KT + 1, :], io["gdn_norm"]).then_inc(par_in, 16)
            sp.dma_start(crow[0:CW * NQKV, :], io["conv_w"]).then_inc(par_in, 16)
            sp.dma_start(alog[:, :], io["a_log"].to_broadcast([P, H])).then_inc(par_in, 16)
            sp.dma_start(dtb[:, :], io["dt_bias"].to_broadcast([P, H])).then_inc(par_in, 16)
            sp.dma_start(sbb[:, :], io["sb_bias"].to_broadcast([P, H])).then_inc(par_in, 16)
            sp.dma_start(ptab[:, :], io["page_table"]).then_inc(pt_in, 16)
            sp.dma_start(cst[0:3 * DB, :], io["state_conv"]).then_inc(cst_in, 16)
            sp.dma_start(io["conv_sample"][:, 0:2, :], io["state_conv3"][:, 1:3, :]).then_inc(c_out, 16)
            for p in range(T_SEG):
                w_load(sp, p)
            sp.wait_ge(pt_in, 16)

            def page(ring, landed, used, cache, b, p):
                n = b * PAGES + p
                if n >= RING:
                    sp.wait_ge(used, n - RING + 1)
                row = sp.value_load(ptab[0:1, n:n + 1], min_val=0, max_val=NPHYS - 1)
                sp.dma_start(ring[:, n % RING:n % RING + 1, :],
                             cache[bass.ds(row, 1), :, :].rearrange("a p n -> p a n"))\
                  .then_inc(landed[n % RING], 16)

            def store_kv():
                for name, src, s_out in (("v", vtok, (v_out, v_out)), ("k", ktok, k_out)):
                    for t in range(TT):
                        i = t if name == "v" else TT + t
                        sp.wait_ge(tok_a, i + 1)
                        sp.wait_ge(tok_d, i + 1)
                        v = src[:, t if name == "v" else t % 2, :]
                        n = LASTP if t == 4 else P
                        sp.dma_start(io[name + "_prompt"][t * P:t * P + n, :], v[0:n, :]).then_inc(s_out[t % 2], 16)
                        if t == 4:
                            sp.dma_start(io[name + "_sample"], v[LASTP:LAST, :]).then_inc(s_out[0], 16)

            def gdn_dma():
                sp.wait_ge(ab_d, AB_G)
                sp.wait_ge(ab_a, AB_B)
                sp.dma_start(srow[0:1, 0:64],
                             gt[LASTP:LAST, 32:40]).then_inc(ab_row, 16)
                sp.dma_start(srow[0:1, 64:128],
                             bt[LASTP:LAST, 32:40]).then_inc(ab_row, 16)
                sp.wait_ge(co_c, 6)
                sp.dma_start(io["conv_prompt"], convrows(0, 3)).then_inc(c_out, 16)
                sp.dma_start(io["conv_sample"][:, 2, :], convrows(3, 11)).then_inc(c_out, 16)
                sp.wait_ge(g_dve, DVE_AT[4, "S", 1])
                sp.dma_start(io["rec_prompt"].rearrange("h k v -> k h v"), S).then_inc(r_out, 16)
                sp.wait_ge(r_out, 16)
                sp.wait_ge(g_act, ACT_AT[4, "ot", 1])
                for j in range(4):
                    sp.dma_start(st[:, 16 * j:16 * j + 16, :],
                                 io["state_rec"][2 * j:2 * j + 2].rearrange("b h k v -> k (b h) v"))\
                      .then_inc(t_in[j], 16)
                for j in range(4):
                    sp.wait_ge(t_dve, T_S0 + 4 * j + 4)
                    sp.dma_start(io["rec_sample"][2 * j:2 * j + 2].rearrange("b h k v -> k (b h) v"),
                                 st[:, 16 * j:16 * j + 16, :]).then_inc(r_out, 16)

            for s in range(SEGS):
                for q in range(4):
                    for t in range(4) if s == 0 and q == 0 else range(2 * q + 2, 2 * q + 4):
                        w_load(sp, T_SEG + s * KT + t)
                    for b, p in pages_of(K_IN.get(s, ()), q, 4):
                        page(kring, k_in, k_used, io["cache_k"], b, p)
                    for b, p in pages_of(V_IN.get(s, ()), q, 4):
                        page(vring, v_in, v_used, io["cache_v"], b, p)
                if s == 1:
                    for i in range(8):
                        for p in (2 * i, 2 * i + 1):
                            page(kring, k_in, k_used, io["cache_k"], K_ATT, p)
                            page(vring, v_in, v_used, io["cache_v"], V_ATT, p)
                        if i == 1:
                            store_kv()
                if s == 4:
                    gdn_dma()
                    sp.wait_ge(t_pe, T_PE_END)
            for p in range(T_PB + 2, T_O):
                w_load(sp, p)
            sp.wait_ge(r_out, 16 * 5)
            wait_read(sp, T_SEG + 8 * KT - 1)
            load_x(1, xs1)
            for p in range(T_O, len(pieces)):
                w_load(sp, p)
            for t in range(TT):
                sp.wait_ge(tok_a, 2 * TT + t + 1)
                sp.wait_ge(tok_d, 2 * TT + t + 1)
                if t == 0:
                    sp.dma_start(io["y_prompt"][0:P - META, :], ytok[META:P, 0, :]).then_inc(y_out, 16)
                elif t < 4:
                    sp.dma_start(io["y_prompt"][t * P - META:(t + 1) * P - META, :], ytok[:, t, :]).then_inc(y_out, 16)
                else:
                    sp.dma_start(io["y_prompt"][4 * P - META:SEQ, :], ytok[0:LASTP, 4, :]).then_inc(y_out, 16)
                    sp.dma_start(io["y_sample"], ytok[LASTP:LAST, 4, :]).then_inc(y_out, 16)
            sp.wait_ge(y_out, 16 * 6)
            sp.wait_ge(k_out[0], 16 * 4)
            sp.wait_ge(k_out[1], 16 * 2)
            sp.wait_ge(v_out, 16 * 6)
            sp.wait_ge(c_out, 16 * 3)
            sp.wait_ge(r_out, 16 * 5)

        @block.tensor
        def _(pe):
            mm, tr = nc.tensor.matmul, nc.tensor.transpose

            def transpose_x(u, xs):
                pe.wait_ge(x_in[u], 80)
                for k in range(KT):
                    if k >= 2:
                        pe.wait_ge(xt_a, KT * u + k - 1)
                        pe.wait_ge(xt_d, KT * u + k - 1)
                    b = 2 * (k % 2)
                    for t in range(4):
                        tr(ps[:, b, t * P:t * P + P], xs[:, t, k * P:k * P + P], ident[:, :])
                    tr(ps[:, b + 1, 0:LAST], xs[0:LAST, 4, k * P:k * P + P], ident[0:LAST, 0:LAST])\
                        .then_inc(xt_ready, 1)

            def square_sums(u):
                for k in range(KT):
                    pe.wait_ge(sq_ready, KT * u + k + 1)
                    sq_u = (sq, sq1, sq2)[u]
                    for i in range(2):
                        m = mm(ps[:, 4 + i, 0:HALF], ones[:, :], sq_u[:, k % 2, i * HALF:i * HALF + HALF],
                               start=(k == 0), stop=(k == KT - 1))
                    m.then_inc(sq_used, 1)

            def tile(t, src):
                if t >= 2:
                    wait_read(pe, t - 2)
                m, k, n_k = pieces[piece_of(t)][4], 0, FT if t >= T_FO else KT
                for p in range(piece_of(t), done(t)):
                    pe.wait_ge(w_in_slot[p % RING], slot_value(p))
                    for kk in range(pieces[p][3] - pieces[p][2]):
                        for i in range(2):
                            last = mm(ps[0:m, 2 * (t % 2) + i, 0:HALF], w_block(p, kk),
                                      src[:, k, i * HALF:i * HALF + HALF], start=(k == 0), stop=(k == n_k - 1))
                        k += 1
                    last.then_inc(w_used, 1)

            def tile_split(t, hi, lo):
                if t >= 2:
                    wait_read(pe, t - 2)
                k, n_k = 0, FT if t >= T_FO else KT
                for p in range(piece_of(t), done(t)):
                    pe.wait_ge(w_lo, p - piece_of(T_O) + 1)
                    for kk in range(pieces[p][3] - pieces[p][2]):
                        w_h, w_l = (b[:, p % RING, kk * P:kk * P + P] for b in (whi, wlo))
                        for w, x in ((w_h, hi), (w_h, lo), (w_l, hi)):
                            for i in range(2):
                                last = mm(ps[:, 2 * (t % 2) + i, 0:HALF], fr(w),
                                          fr(x[k][:, i * HALF:i * HALF + HALF]),
                                          start=(k == 0 and w is w_h and x is hi),
                                          stop=(k == n_k - 1 and w is w_l))
                        k += 1
                    last.then_inc(w_used, 1)

            def spread_q(b):
                if b >= 1:
                    pe.wait_ge(qb_c, b)
                for i in range(2):
                    m = mm(ps[:, 6 + i, :], sel[:, b, :], qrow[:, 512 * i:512 * i + 512], start=True, stop=True)
                m.then_inc(qb_t, 1)

            def cumulate(b):
                pe.wait_ge(d_suf, 4 * (b + 1))
                if b >= 1:
                    pe.wait_ge(d_arg, b)
                mm(ps[:, 4, 0:P], tri_ge[:, :], dsp[:, :], start=True, stop=False)
                mm(ps[:, 4, 0:P - H], ones[:, :], dsuf[:, 1, H:P], start=False, stop=True).then_inc(d_cum, 1)

            def sum_v(b):
                pe.wait_ge(v_used, PAGES * (b + 1))
                if b >= 1:
                    pe.wait_ge(ob_s, b)
                for h in range(H):
                    m = mm(ps[:, 5, h:h + 1], vacc[:, b % 2, h * P:h * P + P], ones[:, 0:1], start=True, stop=True)
                m.then_inc(v_sum, 1)

            def to_tokens(i, src, t):
                if i >= 2:
                    pe.wait_ge(tok_a, i - 1)
                    pe.wait_ge(tok_d, i - 1)
                n = rows_of(t)
                for h in range(H):
                    m = tr(ps[0:n, 2 * (i % 2) + h // 4, (h % 4) * P:(h % 4) * P + P],
                           src[:, h, t * P:t * P + n], ident[:, :])
                m.then_inc(tok_t, 1)

            def attend():
                def scores(h):
                    if h == 0:
                        pe.wait_ge(tok_a, 2 * TT)
                        pe.wait_ge(tok_d, 2 * TT)
                    else:
                        pe.wait_ge(s_z, h)
                    for kt, a, b, bank, col in SB_PIECES:
                        o = h * TOKENS + kt * P
                        m = mm(ps[:, bank, col:col + b - a], kbflat[:, o:o + P], qbT[:, h, a:b],
                               start=True, stop=True)
                    m.then_inc(s_s, 1)

                def later_sums(h):
                    pe.wait_ge(s_msp, h + 1)
                    if h >= 1:
                        pe.wait_ge(s_arg, h)
                    for kt, a, b, bank, col in SB_PIECES:
                        parts = [(tri_ge, kt, a)] + [(ones, k2, max(a, P * k2)) for k2 in range(kt + 1, TT)
                                                     if P * k2 < b]
                        for j, (lhs, k2, q) in enumerate(parts):
                            f = sb_at(k2, q)[2]
                            m = mm(ps[:, 3 + bank, col + q - a:col + b - a], lhs[:, :],
                                   sps[:, h % 2, f:f + b - q], start=(j == 0), stop=(j == len(parts) - 1))
                    m.then_inc(s_c, 1)

                def values(h):
                    pe.wait_ge(s_w, h + 1)
                    if h >= 1:
                        pe.wait_ge(s_o, h)
                    else:
                        pe.wait_ge(qb_c, 3)
                    for bank, a, b in ((6, 0, 512), (7, 512, LP)):
                        ks = [k for k in range(TT) if P * k < b]
                        for k in ks:
                            q, n = max(a, P * k), chunk(k)
                            f = sb_at(k, q)[2]
                            m = mm(ps[:, bank, q - a:b - a], vtok[0:n, k, h * P:h * P + P],
                                   zs[0:n, h % 2, f:f + b - q], start=(k == 0), stop=(k == ks[-1]))
                    m.then_inc(s_av, 1)

                scores(0)
                for h in range(H + 1):
                    if h + 1 < H:
                        scores(h + 1)
                    if h < H:
                        later_sums(h)
                    if h >= 1:
                        values(h - 1)
                pe.wait_ge(s_z, H)
                pe.wait_ge(s_arg, H)
                pe.wait_ge(s_o, H)

            def conv_rows():
                pe.wait_ge(raw_c, NQKV)
                for n in range(NQKV):
                    i = n // 4
                    if n % 4 == 0 and i >= 2:
                        pe.wait_ge(co_c, i - 1)
                    m = tr(ps[0:11, i % 2, (n % 4) * P:(n % 4) * P + P], rawt[:, n, :], ident[:, :])
                    if n % 4 == 3:
                        m.then_inc(co_t, 1)
                pe.wait_ge(co_c, 6)

            def norm_qk():
                for n in range(2 * H):
                    pe.wait_ge(n_sq, n + 1)
                    for t in range(TT):
                        m_rows = rows_of(t)
                        mm(ps[0:m_rows, 3, 16 * t + n:16 * t + n + 1], sqg[:, n % SQB, t * P:t * P + m_rows], ones[:, 0:1],
                           start=True, stop=True)
                    mm(ps[:, 2, DB * n:DB * n + DB], ones[:, :], sqg[:, n % SQB, LP:TOKENS], start=True, stop=True)\
                        .then_inc(n_ss, 1)

            def decay_rows():
                for t in range(TT):
                    n = rows_of(t)
                    m = tr(ps[0:n, 4, 16 * t:16 * t + 16], abT[:, t * P:t * P + n], ident[32:48, 32:48])
                m.then_inc(ab_t, 1)

            def decays():
                pe.wait_ge(ab_p, 2)
                mm(ps[:, 5, 0:40], tri_le[:, :], gP, start=True, stop=True)
                mm(ps[:, 5, 64:104], tri_gt[:, :], gP, start=True, stop=True)
                mm(ps[:, 5, 128:168], ones[:, :], gP, start=True, stop=True)
                pe.wait_ge(ab_row, 32)
                mm(ps[:, 5, 256:384], ones[0:1, :], srow[0:1, :], start=True, stop=True).then_inc(ab_m, 1)

            def chunks():
                pe.wait_ge(ab_a, AB_END)
                pe.wait_ge(ab_d, AB_DEND)
                pe.wait_ge(n_dve, N_END)
                for c in range(TT):
                    n, t0 = chunk(c), P * c
                    gm = gms[c % 2]

                    def after(eng, *key):
                        s, at_ = {"act": (g_act, ACT_AT), "dve": (g_dve, DVE_AT), "pool": (g_pool, POOL_AT)}[eng]
                        if key[0] >= 0:
                            pe.wait_ge(s, at_[key])

                    def heads(g):
                        return range(4 * g, 4 * g + 4)

                    def col(h):
                        return (h % 4) * P

                    for g in G2:
                        after("act", c - 1, "vn", g)
                        for h in heads(g):
                            m = tr(ps[0:n, g, col(h):col(h) + P], cT[:, H + h, t0:t0 + n], ident[:, :])
                        m.then_inc(g_pe, 1)
                    for g in G2:
                        after("dve", c - 1, "o", g)
                        for h in heads(g):
                            m = tr(ps[0:n, 2 + g, col(h):col(h) + P], cT[:, 2 * H + h, t0:t0 + n], ident[:, :])
                        m.then_inc(g_pe, 1)
                    after("pool", c, "gm")
                    for g in G2:
                        after("dve", c - 1, "S", g)
                        mm(ps[0:n, 4 + g, 0:4 * n], tri_le[0:n, 0:n], gm[0:n, 4 * g:4 * g + 4, 0:n],
                           start=True, stop=True).then_inc(g_pe, 1)
                    for g in G2:
                        after("act", c - 1, "ot", g)
                        for h in heads(g):
                            m = mm(ps[0:n, 6 + g, (h % 4) * n:(h % 4) * n + n], gm[0:n, h, 0:n],
                                   tri_le[0:n, 0:n], start=True, stop=True)
                        m.then_inc(g_pe, 1)
                    for g in G2:
                        after("dve", c, "kr", g)
                        for h in heads(g):
                            m = mm(ps[0:n, g, (h % 4) * n:(h % 4) * n + n], cT[:, H + h, t0:t0 + n],
                                   cT[:, H + h, t0:t0 + n], start=True, stop=True)
                        m.then_inc(g_pe, 1)
                    for g in G2:
                        after("dve", c, "bv", g)
                        for h in heads(g):
                            m = mm(ps[0:n, 2 + g, (h % 4) * n:(h % 4) * n + n], cT[:, H + h, t0:t0 + n],
                                   cT[:, h, t0:t0 + n], start=True, stop=True)
                        m.then_inc(g_pe, 1)
                    for g in G2:
                        after("pool", c, "L", 1, g)
                        after("act", c, "dr", g)
                        for h in heads(g):
                            m = tr(ps[0:n, 4 + g, (h % 4) * n:(h % 4) * n + n], Lm[0][0:n, h, 0:n], ident[0:n, 0:n])
                        m.then_inc(g_pe, 1)
                    for j, s in enumerate(LEVELS[c][1:]):
                        w = n // 2
                        for g in G2:
                            after("pool", c, "L", s, g)
                            if j == 0:
                                after("dve", c, "U1", g)
                                after("dve", c, "A", g)
                            else:
                                after("dve", c, "U", s // 2, g)
                            for h in heads(g):
                                m = mm(ps[0:n, g, (h % 4) * n:(h % 4) * n + n], Lm[(j + 1) % 2][0:n, h, 0:n],
                                       Um[0:n, h, 0:n], start=True, stop=True)
                            m.then_inc(g_pe, 1)
                        for g in G2:
                            after("act", c, "q1", s, g)
                            if j == 0:
                                after("dve", c, "qk", g)
                                after("dve", c, "T1", g)
                            else:
                                after("dve", c, "T", s // 2, g)
                            for h in heads(g):
                                m = mm(ps[0:n, 2 + g, (h % 4) * w:(h % 4) * w + w], Tm[0:n, h, 0:n],
                                       odd(Q1[0:n, h:h + 1, 0:n], s)[:, 0], start=True, stop=True)
                            if 2 * s < n:
                                for h in heads(g):
                                    m = mm(ps[0:n, 2 + g, 256 + (h % 4) * w:256 + (h % 4) * w + w], Q1[0:n, h, 0:n],
                                           even(Tm[0:n, h:h + 1, 0:n], s)[:, 0], start=True, stop=True)
                            m.then_inc(g_pe, 1)
                    last = LEVELS[c][-1]
                    for g in G2:
                        if c:
                            after("dve", c - 1, "S", g)
                        else:
                            pe.wait_ge(g_dve0, 1)
                        after("dve", c, "U1", g)
                        for h in heads(g):
                            m = mm(ps[0:n, 4 + g, col(h):col(h) + P], cT[:, H + h, t0:t0 + n], S[:, h, :],
                                   start=True, stop=True)
                        m.then_inc(g_pe, 1)
                    for g in G2:
                        after("act", c, "dc", g)
                        for h in heads(g):
                            m = mm(ps[0:n, 6 + g, col(h):col(h) + P], cT[:, h, t0:t0 + n], S[:, h, :],
                                   start=True, stop=True)
                        m.then_inc(g_pe, 1)
                    for g in G2:
                        after("dve", c, "R", g)
                        after("dve", c, "U", last, g)
                        for h in heads(g):
                            m = mm(ps[0:n, g, col(h):col(h) + P], Um[0:n, h, 0:n], bvs[0:n, h, :],
                                   start=True, stop=True)
                        m.then_inc(g_pe, 1)
                    for g in G2:
                        after("act", c, "vn", g)
                        for h in heads(g):
                            m = mm(ps[0:n, 2 + g, col(h):col(h) + P], DC[0:n, h, 0:n], vnb[0:n, h, :],
                                   start=True, stop=True)
                        m.then_inc(g_pe, 1)
                    for g in G2:
                        for h in heads(g):
                            m = mm(ps[:, 4 + g, col(h):col(h) + P], krs[0:n, h, :], vnb[0:n, h, :],
                                   start=True, stop=True)
                        m.then_inc(g_pe, 1)
                    after("dve", c, "on")
                    for g in G2:
                        after("act", c, "qs", g)
                        for h in heads(g):
                            m = tr(ps[:, 6 + g, (h % 4) * n:(h % 4) * n + n], Q1[0:n, h, :], ident[0:n, 0:n])
                        m.then_inc(g_pe, 1)
                pe.wait_ge(g_act, ACT_AT[4, "ot", 1])
                pe.wait_ge(g_dve, DVE_AT[4, "on"])

            def sampled_delta():
                pe.wait_ge(t_dve, 1)
                for r in range(64):
                    b, h = r // H, r % H
                    if r % 16 == 0:
                        pe.wait_ge(t_in[r // 16], 16)
                    m = mm(ps[:, 0, 2 * r:2 * r + 2], st[:, r, :], cT[:, h:h + H + 1:H, LP + b],
                           start=True, stop=True)
                m.then_inc(t_pe, 1)
                mm(ps[:, 1, 0:64], ones[:, :], dsm[:, 0, :], start=True, stop=True).then_inc(t_pe, 1)
                pe.wait_ge(t_dve, T_VN)
                tr(ps[0:64, 2, 0:P], dsm[:, 3, :], ident[:, :])
                tr(ps[0:64, 2, P:2 * P], dsm[:, 1, :], ident[:, :]).then_inc(t_pe, 1)
                pe.wait_ge(t_dve, T_OSQ)
                mm(ps[:, 3, 0:64], ones[:, :], dsm[:, 6, :], start=True, stop=True).then_inc(t_pe, 1)
                for j in range(4):
                    pe.wait_ge(t_pool, j + 1)
                    pe.wait_ge(t_dve, T_ROWS)
                    for i in range(4):
                        if j:
                            pe.wait_ge(t_dve, T_S0 + 4 * (j - 1) + i + 1)
                        for r4 in range(4):
                            r = 4 * i + r4
                            m = mm(ps[:, 4 + i, r4 * P:r4 * P + P], ksel[:, r, :], vrow[:, :],
                                   start=True, stop=True)
                        m.then_inc(t_pe, 1)
                pe.wait_ge(t_dve, T_S0 + 16)
                pe.wait_ge(t_act, 3)

            pe.wait_ge(const_ready, NCONST)
            transpose_x(0, xs0)
            pe.wait_ge(par_in, 16 * 8)
            tr(ps[:, 6, 0:25], prow[0:25, :], ident[0:25, 0:25])
            tr(ps[:, 6, P:P + 96], crow[0:96, :], ident[0:96, 0:96]).then_inc(par_t, 1)
            square_sums(0)
            pe.wait_ge(par_c, 2)
            pe.wait_ge(cst_in, 16)
            for n in range(NQKV):
                m = tr(ps[:, 6 + n // 12, 24 * (n % 12):24 * (n % 12) + 24], cst[0:24, n * P:n * P + P],
                       ident[0:24, 0:24])
            m.then_inc(par_t, 1)
            pe.wait_ge(xn_ready, KT)
            for t in range(T_SEG):
                tile(t, xn)
            wait_read(pe, T_SEG - 1)
            pe.wait_ge(cb_c, 2)
            for h in range(H):
                m = tr(ps[0:DB, 6 + h // 4, (h % 4) * P:(h % 4) * P + P], qbT[:, h, LP:TOKENS], ident[:, :])
            m.then_inc(qr_t, 1)
            pe.wait_ge(qr_c, 1)
            spread_q(0)
            for s in range(SEGS):
                src = oaT if s == 7 else xn
                if s == 7:
                    pe.wait_ge(z_done, KT)
                for j in range(KT):
                    tile(T_SEG + s * KT + j, src)
                    if j == 0 and s in SUM_IN:
                        sum_v(SUM_IN[s])
                    if j == 1 and s in CHAIN_IN:
                        cumulate(CHAIN_IN[s])
                    if j == 4 and s == 8:
                        cumulate(DB - 1)
                    if j == 4 and s + 1 < DB:
                        spread_q(s + 1)
                if s == 1:
                    wait_read(pe, T_SEG + 2 * KT - 2)
                    wait_read(pe, T_SEG + 2 * KT - 1)
                    for t in range(TT):
                        to_tokens(t, vbT, t)
                    cumulate(V_ATT)
                    sum_v(0)
                    for t in range(TT):
                        to_tokens(TT + t, kbT, t)
                    pe.wait_ge(d_arg, 2)
                    pe.wait_ge(ob_s, 1)
                    attend()
                if s == 4:
                    wait_read(pe, T_SEG + 5 * KT - 2)
                    wait_read(pe, T_SEG + 5 * KT - 1)
                    pe.wait_ge(d_arg, 4)
                    sum_v(3)
                    pe.wait_ge(qb_c, 6)
                    decay_rows()
                    conv_rows()
                    pe.wait_ge(ob_s, 4)
                    norm_qk()
                    decays()
                    chunks()
                    sampled_delta()
            sum_v(DB - 2)
            sum_v(DB - 1)
            pe.wait_ge(ob_s, DB)
            for n in range(KT):
                tile(T_PB + n, obT)
            wait_read(pe, T_PB + 6)
            wait_read(pe, T_PB + 7)
            transpose_x(1, xs1)
            pe.wait_ge(xt_a, 2 * KT)
            pe.wait_ge(xt_d, 2 * KT)
            pe.wait_ge(a_lo, KT)
            for n in range(KT):
                tile_split(T_O + n, m_hi, m_lo)
            square_sums(1)
            pe.wait_ge(a_lo, 2 * KT)
            for n in range(2 * FT):
                tile_split(T_FI + n, x_hi, x_lo)
            pe.wait_ge(a_lo, 2 * KT + FT)
            for n in range(KT):
                tile_split(T_FO + n, h_hi, h_lo)
            square_sums(2)
            wait_read(pe, TILES - 2)
            wait_read(pe, TILES - 1)
            pe.wait_ge(xn_ready, 2 * KT)
            for t in range(TT):
                to_tokens(2 * TT + t, xn, t)

        @block.scalar
        def _(act):
            go = nc.scalar.activation

            def copy_x(u, dst):
                for k in range(KT):
                    act.wait_ge(xt_ready, KT * u + k + 1)
                    nc.scalar.copy(dst[:, k, 0:512], ps[:, 2 * (k % 2), :]).then_inc(xt_a, 1)

            def squares(u, src, dst, ready, value):
                for k in range(KT):
                    ready(k)
                    if KT * u + k >= 2:
                        act.wait_ge(sq_used, KT * u + k - 1)
                    go(dst[:, k % 2, :], src[:, k, :], ACT.Square).then_inc(sq_ready, 1)

            def root(u, buf):
                act.wait_ge(ms_ready, u + 1)
                go(buf, buf, ACT.Sqrt).then_inc(rt_ready, 1)

            def read_tile(t, dst, func=ACT.Copy, m=P):
                act.wait_ge(w_used, done(t))
                go(halves(dst), pair(t, m), func).then_inc(act_read, 1)

            def put_q(b):
                act.wait_ge(qb_t, b + 1)
                if b >= 2:
                    act.wait_ge(k_used, PAGES * (b - 1))
                nc.scalar.copy(qbc[:, b % 2, :].rearrange("p (a n) -> p a n", a=2), ps[:, 6:8, :]).then_inc(qb_c, 1)

            def softplus_part(b):
                act.wait_ge(dz_ready, b + 1)
                if b >= 1:
                    act.wait_ge(d_sp, b)
                go(de[:, :], dz[:, b % 3, :], ACT.Abs).then_inc(d_abs, 1)
                act.wait_ge(d_abs, b + 1)
                go(de[:, :], de[:, :], ACT.Exp, scale=-1.0).then_inc(d_exp, 1)
                act.wait_ge(d_exp, b + 1)
                go(de[:, :], de[:, :], ACT.Ln, bias=1.0).then_inc(d_ln, 1)

            def weights(b):
                act.wait_ge(d_arg, b + 1)
                if b >= 2:
                    act.wait_ge(v_used, PAGES * (b - 1))
                go(dw[:, b % 2, :], dz[:, b % 3, :], ACT.Exp).then_inc(d_w, 1)

            def put_o(b):
                act.wait_ge(v_sum, b + 1)
                nc.scalar.copy(obT[:, :, LP + b], ps[:, 5, 0:H]).then_inc(ob_s, 1)

            def token_bank(i, dst, t):
                act.wait_ge(tok_t, i + 1)
                n = rows_of(t)
                nc.scalar.copy(dst[0:n, 0:512], ps[0:n, 2 * (i % 2), :]).then_inc(tok_a, 1)

            def attend():
                def first(h):
                    act.wait_ge(s_s, h + 1)
                    if h == 0:
                        act.wait_ge(tok_d, 2 * TT)
                        act.wait_ge(k_out[0], 16 * 4)
                        act.wait_ge(k_out[1], 16 * 2)
                    if h >= 2:
                        act.wait_ge(s_av, h - 1)
                    for b in range(3):
                        w = SB_WIDTH[b]
                        m = go(zs[:, h % 2, SB_FLAT[b]:SB_FLAT[b] + w], ps[:, b, 0:w], ACT.Identity,
                               bias=sbb[:, h:h + 1], scale=SCALE)
                    m.then_inc(s_z, 1)
                    act.wait_ge(s_abs, h + 1)
                    go(es, es, ACT.Exp, scale=-1.0).then_inc(s_exp, 1)
                    act.wait_ge(s_exp, h + 1)
                    go(es, es, ACT.Ln, bias=1.0).then_inc(s_ln, 1)

                first(0)
                for h in range(H + 1):
                    if h + 1 < H:
                        first(h + 1)
                    if h < H:
                        act.wait_ge(s_marg, h + 1)
                        go(zs[:, h % 2, :], zs[:, h % 2, :], ACT.Exp).then_inc(s_w, 1)
                    if h >= 1:
                        act.wait_ge(s_av, h)
                        nc.scalar.copy(obT[:, h - 1, 0:512], ps[:, 6, :])
                        nc.scalar.copy(obT[:, h - 1, 512:LP], ps[:, 7, 0:LP - 512]).then_inc(s_o, 1)

            def silu_conv(n):
                act.wait_ge(cv_step, CW * (n + 1))
                go(cT[:, n, 0:LP], cT[:, n, 0:LP], ACT.Silu).then_inc(cs_done, 1)

            def norm_qk():
                act.wait_ge(sc_step, 7)
                go(cT[:, :, LP:TOKENS], cT[:, :, LP:TOKENS], ACT.Silu).then_inc(cs_done, 1)
                act.wait_ge(cs_done, NQKV + 1)
                act.wait_ge(k_used, PAGES * 4)
                for n in range(2 * H):
                    if n >= SQB:
                        act.wait_ge(n_ss, n - SQB + 1)
                    go(sqg[:, n % SQB, :], cT[:, n, :], ACT.Square).then_inc(n_sq, 1)

            def norm_roots():
                act.wait_ge(n_ss, 2 * H)
                go(nr_s, ps[:, 2, 0:P], ACT.Sqrt, bias=epsc[:, :]).then_inc(n_act, 1)
                act.wait_ge(n_dve, N_ROWS)
                go(nr_t, nr_q, ACT.Sqrt, bias=epsc[:, :]).then_inc(n_act, 1)
                go(lnk.rearrange("p (t h) -> p t h", h=H), nr_q.rearrange("p (t n) -> p t n", t=TT)[:, :, H:2 * H],
                   ACT.Ln, bias=epsc[:, :]).then_inc(n_act, 1)

            def decays():
                act.wait_ge(par_in, 16 * 8)
                go(eal[:, 0:H], alog[:, :], ACT.Exp).then_inc(ab_a, 1)
                act.wait_ge(ab_d, AB_X)
                go(tmp2, tmp1, ACT.Abs).then_inc(ab_a, 1)
                act.wait_ge(ab_a, 2)
                go(tmp2, tmp2, ACT.Exp, scale=-1.0).then_inc(ab_a, 1)
                act.wait_ge(ab_a, 3)
                go(tmp2, tmp2, ACT.Ln, bias=1.0).then_inc(ab_a, 1)
                go(bt.rearrange("p (t h) -> p t h", h=H), ab5[:, :, H:2 * H], ACT.Sigmoid).then_inc(ab_a, 1)
                act.wait_ge(ab_m, 1)
                go(eG, ps[:, 5, 0:40], ACT.Exp).then_inc(ab_a, 1)
                go(eR, ps[:, 5, 64:104], ACT.Exp).then_inc(ab_a, 1)
                go(eL, ps[:, 5, 128:168], ACT.Exp).then_inc(ab_a, 1)
                go(dsm[:, 8, :], ps[:, 5, 256:320], ACT.Exp).then_inc(ab_a, 1)
                nc.scalar.copy(dsm[:, 9, :], ps[:, 5, 320:384]).then_inc(ab_a, 1)

            def chunks():
                for c in range(TT):
                    n, t0 = chunk(c), P * c

                    def after(eng, *key):
                        s, at_ = {"pe": (g_pe, PE_AT), "dve": (g_dve, DVE_AT), "pool": (g_pool, POOL_AT)}[eng]
                        if key[0] >= 0:
                            act.wait_ge(s, at_[key])

                    for name, dst, bank, user in (("dr", DR, 4, "L"), ("dc", DC, 6, "o2")):
                        for g in G2:
                            if name == "dr" and c:
                                after("pool", c - 1, "L", LEVELS[c - 1][-1], g)
                            after("pe", c, name, g)
                            go(dst[0:n, 4 * g:4 * g + 4, 0:n],
                               ps[0:n, bank + g, 0:4 * n].rearrange("p (h j) -> p h j", h=4), ACT.Exp)\
                                .then_inc(g_act, 1)
                    for s in LEVELS[c][1:]:
                        for g in G2:
                            after("pe", c, "q1", s, g)
                            nc.scalar.copy(Q1[0:n, 4 * g:4 * g + 4, 0:n],
                                           ps[0:n, g, 0:4 * n].rearrange("p (h j) -> p h j", h=4)).then_inc(g_act, 1)
                    for g in G2:
                        after("pe", c, "qs", g)
                        for h in range(4 * g, 4 * g + 4):
                            i = (h % 4) * P
                            m = go(Q1[0:n, h, :], ps[0:n, 6 + g, i:i + P], ACT.Copy, scale=eG[0:n, H * c + h:H * c + h + 1])
                        m.then_inc(g_act, 1)
                    for g in G2:
                        after("pe", c, "vn", g)
                        nc.scalar.copy(vnb[0:n, 4 * g:4 * g + 4, :],
                                       ps[0:n, g, :].rearrange("p (h j) -> p h j", h=4)).then_inc(g_act, 1)
                    after("dve", c, "ms")
                    go(onr[0:n, H:2 * H], onr[0:n, 0:H], ACT.Sqrt, bias=epsc[0:n, :]).then_inc(g_act, 1)
                    for g in G2:
                        after("pe", c, "ot", g)
                        go(oaT[:, 4 * g:4 * g + 4, t0:t0 + n],
                           ps[:, 6 + g, 0:4 * n].rearrange("p (h j) -> p h j", h=4), ACT.Copy,
                           scale=cols[:, 24:25]).then_inc(g_act, 1)

            def sampled_delta():
                act.wait_ge(t_pe, 4)
                go(dsm[:, 7, :], ps[:, 3, 0:64], ACT.Identity, scale=1.0 / P, bias=epsc[:, :]).then_inc(t_act, 1)
                act.wait_ge(t_act, 1)
                go(dsm[:, 7, :], dsm[:, 7, :], ACT.Sqrt).then_inc(t_act, 1)
                act.wait_ge(t_dve, T_ON)
                go(oaT[:, :, LP:TOKENS].rearrange("p h b -> p b h"),
                   dsm[:, 5, :].rearrange("p (b h) -> p b h", h=H), ACT.Copy, scale=cols[:, 24:25]).then_inc(t_act, 1)

            act.wait_ge(const_ready, NCONST)
            act.wait_ge(eps_ready, 1)
            copy_x(0, hT0)

            def x_there(k):
                act.wait_ge(xt_a, k + 1)
                act.wait_ge(xt_d, k + 1)
            squares(0, hT0, sq, x_there, 0)
            root(0, rstd)
            read_tile(T_AB, abT[:, :], m=2 * H)
            for n in range(KT):
                read_tile(T_Q + n, qbT[:, n, :])
            put_q(0)
            for s in range(SEGS):
                if s == 5:
                    act.wait_ge(r_out, 16 * 5)
                for j in range(KT):
                    t, n = T_SEG + s * KT + j, (s - 2) * KT + j
                    if j == 0 and s in CHAIN_IN:
                        softplus_part(CHAIN_IN[s])
                    if j == 2 and s in CHAIN_IN:
                        weights(CHAIN_IN[s])
                    if j == 3 and s == 8:
                        softplus_part(DB - 1)
                    if j == 6 and s == 8:
                        weights(DB - 1)
                    if s in (0, 1):
                        read_tile(t, (kbT, vbT)[s][:, j, :])
                    elif s in (2, 3, 4):
                        if n == 0:
                            act.wait_ge(v_out, 16 * 6)
                            act.wait_ge(up_zero, 1)
                        if n >= 2:
                            act.wait_ge(cv_step, CW * (n - 1))
                            act.wait_ge(raw_c, n - 1)
                        read_tile(t, upad[:, n % 2, CW - 1:CW - 1 + TOKENS])
                        if n % 2 and n >= 3:
                            silu_conv(n - 3)
                            silu_conv(n - 2)
                    elif s == 5:
                        if j >= 2:
                            act.wait_ge(z_done, j - 1)
                        act.wait_ge(w_used, done(t))
                        go(halves(ztmp[:, j % 2, :]), pair(t), ACT.Silu).then_inc(act_read, 1)
                    elif s in (6, 8):
                        read_tile(t, (sgA if s == 6 else sgB)[:, j, :], ACT.Sigmoid)
                    if j == 1 and s in SUM_IN:
                        put_o(SUM_IN[s])
                    if j == 5 and s + 1 < DB:
                        put_q(s + 1)
                if s == 1:
                    softplus_part(V_ATT)
                    for t in range(TT):
                        token_bank(t, vtok[:, t, :], t)
                    weights(V_ATT)
                    put_o(0)
                    for t in range(TT):
                        if t >= 2:
                            act.wait_ge(k_out[t % 2], 16 * (t // 2))
                        token_bank(TT + t, ktok[:, t % 2, :], t)
                    attend()
                if s == 4:
                    silu_conv(NQKV - 2)
                    silu_conv(NQKV - 1)
                    put_o(3)
                    norm_qk()
                    decays()
                    norm_roots()
                    chunks()
                    sampled_delta()
            put_o(DB - 2)
            put_o(DB - 1)
            act.wait_ge(v_used, PAGES * DB)
            act.wait_ge(k_used, PAGES * DB)
            for n in range(KT):
                act_hi(act, n, m_hi[n], m_full[n])
                if n in (5, 6):
                    split_hi(act, T_O + n - 5)
            copy_x(1, hT)

            def h_there(base):
                def wait(k):
                    act.wait_ge(dve_read, base + k + 1)
                return wait
            for k in range(KT):
                split_hi(act, T_O + k + 2)
            squares(1, hT, sq1, h_there(READ_COUNT[T_O] - 1), 0)
            root(1, rstd1)
            for k in range(KT):
                act_hi(act, KT + k, x_hi[k], x_full[k])
            for n in range(FT + 1):
                if n < FT:
                    if n >= 2:
                        act.wait_ge(dve_read, READ_COUNT[T_FI + 2 * (n - 2) + 1])
                    split_hi(act, T_FI + 2 * n + 2)
                    read_tile(T_FI + 2 * n, gtmp[:, n % 2, :], ACT.Silu)
                    if n < FT - 1:
                        split_hi(act, T_FI + 2 * n + 3)
                if n >= 1:
                    act_hi(act, 2 * KT + n - 1, h_hi[n - 1], h_full[n - 1])
            split_hi(act, T_FO + 1)
            for n in range(KT - 2):
                split_hi(act, T_FO + n + 2)
            squares(2, hT, sq2, h_there(READ_COUNT[T_FO] - 1), 0)
            root(2, rstd2)
            for t in range(TT):
                token_bank(2 * TT + t, ytok[:, t, :], t)

        @block.vector
        def _(dve):
            v = nc.vector

            def copy_x(u, dst):
                for k in range(KT):
                    dve.wait_ge(xt_ready, KT * u + k + 1)
                    v.tensor_copy(dst[:, k, 512:TOKENS], ps[:, 2 * (k % 2) + 1, 0:LAST]).then_inc(xt_d, 1)

            def normalise(u, src, w0, rs):
                dve.wait_ge(sq_used, KT * (u + 1))
                v.tensor_scalar(halves(rs), ps[:, 4:6, 0:HALF], 1.0 / D, EPS, ALU.mult, ALU.add).then_inc(ms_ready, 1)
                dve.wait_ge(rt_ready, u + 1)
                v.reciprocal(rs, rs).then_inc(rc_ready, 1)
                dve.wait_ge(rc_ready, u + 1)
                for k in range(KT):
                    dst, full = (x_full[k], a_full) if u == 1 else (xn[:, k, :], xn_ready)
                    v.scalar_tensor_tensor(dst, src[:, k, :], cols[:, w0 + k:w0 + k + 1], rs,
                                           ALU.mult, ALU.mult).then_inc(full, 1)
                    if u == 1 and k >= 1:
                        act_lo(dve, KT + k - 1, x_hi[k - 1], x_full[k - 1], x_lo[k - 1])
                if u == 1:
                    act_lo(dve, 2 * KT - 1, x_hi[KT - 1], x_full[KT - 1], x_lo[KT - 1])

            def k_page(b, p):
                n = b * PAGES + p
                dve.wait_ge(k_in[n % RING], slot_value(n))
                if p == 0:
                    dve.wait_ge(qb_c, b + 1)
                    if b >= 3:
                        dve.wait_ge(d_w, b - 2)
                for h in range(H):
                    kh = kring[:, n % RING, h * P:h * P + P]
                    m = v.tensor_tensor_reduce(kh, kh, qbc[:, b % 2, h * P:h * P + P], 1.0, 0.0, ALU.mult,
                                               ALU.add, dz[:, b % 3, p * H + h:p * H + h + 1])
                m.then_inc(k_used, 1)
                if p == PAGES - 1:
                    scale_scores(b)

            def scale_scores(b):
                dve.wait_ge(k_used, PAGES * (b + 1))
                z = dz[:, b % 3, :].rearrange("p (a h) -> p a h", h=H)
                v.scalar_tensor_tensor(z, z, SCALE, sbb[:, :].unsqueeze(1).to_broadcast([P, PAGES, H]),
                                       ALU.mult, ALU.add).then_inc(dz_ready, 1)

            def chain_sp(b):
                dve.wait_ge(d_ln, b + 1)
                if b >= 1:
                    dve.wait_ge(d_cum, b)
                v.scalar_tensor_tensor(dsp[:, :], dz[:, b % 3, :], 0.0, de[:, :], ALU.max, ALU.add)\
                    .then_inc(d_sp, 1)
                dve.wait_ge(d_sp, b + 1)
                src = dsp[:, :]
                for i, step in enumerate((H, 2 * H, 4 * H, 8 * H)):
                    dst = dsuf[:, i % 2, :]
                    v.tensor_copy(dst[:, P - step:P], src[:, P - step:P])
                    v.tensor_tensor(dst[:, 0:P - step], src[:, 0:P - step], src[:, step:P], ALU.add).then_inc(d_suf, 1)
                    dve.wait_ge(d_suf, 4 * b + i + 1)
                    src = dst

            def chain_arg(b):
                dve.wait_ge(d_cum, b + 1)
                v.tensor_tensor(dz[:, b % 3, :], dz[:, b % 3, :], ps[:, 4, 0:P], ALU.subtract).then_inc(d_arg, 1)

            def v_page(b, p):
                n = b * PAGES + p
                dve.wait_ge(v_in[n % RING], slot_value(n))
                if p == 0:
                    dve.wait_ge(d_w, b + 1)
                    if b >= 2:
                        dve.wait_ge(v_sum, b - 1)
                else:
                    dve.wait_ge(v_used, n)
                for h in range(H):
                    vh, a = vring[:, n % RING, h * P:h * P + P], vacc[:, b % 2, h * P:h * P + P]
                    w = dw[:, b % 2, p * H + h:p * H + h + 1]
                    if p == 0:
                        m = v.tensor_scalar(a, vh, w, None, ALU.mult)
                    else:
                        m = v.scalar_tensor_tensor(a, vh, w, a, ALU.mult, ALU.add)
                m.then_inc(v_used, 1)

            def token_bank(i, dst, t):
                dve.wait_ge(tok_t, i + 1)
                n = rows_of(t)
                v.tensor_copy(dst[0:n, 512:D], ps[0:n, 2 * (i % 2) + 1, :]).then_inc(tok_d, 1)

            def attend():
                def first(h):
                    dve.wait_ge(s_z, h + 1)
                    if h >= 1:
                        dve.wait_ge(s_sp, h)
                    v.scalar_tensor_tensor(es, zs[:, h % 2, :], -1.0, zs[:, h % 2, :], ALU.mult, ALU.max).then_inc(s_abs, 1)
                    dve.wait_ge(s_ln, h + 1)
                    if h >= 2:
                        dve.wait_ge(s_c, h - 1)
                    v.scalar_tensor_tensor(sps[:, h % 2, :], zs[:, h % 2, :], 0.0, es, ALU.max, ALU.add)\
                        .then_inc(s_sp, 1)

                first(0)
                for h in range(H):
                    if h + 1 < H:
                        first(h + 1)
                    dve.wait_ge(s_c, h + 1)
                    for b in range(3):
                        w = SB_WIDTH[b]
                        zb = zs[:, h % 2, SB_FLAT[b]:SB_FLAT[b] + w]
                        m = v.tensor_tensor(zb, zb, ps[:, 3 + b, 0:w], ALU.subtract)
                    m.then_inc(s_arg, 1)
                    for p in (2 * h, 2 * h + 1):
                        k_page(K_ATT, p)
                        v_page(V_ATT, p)

            def conv(n):
                y = cT[:, n, 0:LP]
                dve.wait_ge(act_read, READ_COUNT[T_SEG + 2 * KT + n])
                for i in range(CW):
                    u, w = upad[:, n % 2, i:i + LP], convw[:, i, n:n + 1]
                    if i == 0:
                        v.tensor_scalar(y, u, w, None, ALU.mult).then_inc(cv_step, 1)
                    else:
                        dve.wait_ge(cv_step, CW * n + i)
                        v.scalar_tensor_tensor(y, u, w, y, ALU.mult, ALU.add).then_inc(cv_step, 1)

            def conv_sampled():
                y = cT[:, :, LP:TOKENS]
                dve.wait_ge(raw_c, NQKV)

                def w(i):
                    return per_head(convw[:, i, :], DB)
                v.tensor_tensor(y, rawt[:, :, 3:11], w(CW - 1), ALU.mult).then_inc(sc_step, 1)
                cb = cbuf[:, :, :].rearrange("p n (b i) -> p n b i", i=3)
                for i in range(3):
                    dve.wait_ge(sc_step, 1 + 2 * i)
                    v.tensor_tensor(cvt, cb[:, :, :, i], w(i), ALU.mult).then_inc(sc_step, 1)
                    dve.wait_ge(sc_step, 2 + 2 * i)
                    v.tensor_tensor(y, y, cvt, ALU.add).then_inc(sc_step, 1)

            def norm_qk():
                dve.wait_ge(v_used, PAGES * 4)
                v.memset(nr_q, 0.0).then_inc(n_dve, 1)
                dve.wait_ge(n_ss, 2 * H)
                dve.wait_ge(n_dve, 1)
                v.tensor_copy(nr_q[:, 0:64], ps[:, 3, 0:64]).then_inc(n_dve, 1)
                v.tensor_copy(nr_q[0:LAST, 64:80], ps[0:LAST, 3, 64:80]).then_inc(n_dve, 1)
                dve.wait_ge(n_act, 1)
                v.reciprocal(nr_s, nr_s).then_inc(n_dve, 1)
                dve.wait_ge(n_act, 2)
                v.reciprocal(nr_r, nr_t).then_inc(n_dve, 1)
                dve.wait_ge(n_dve, 5)
                rr = nr_r.rearrange("p (t n) -> p t n", t=TT)
                rs8 = nr_s.rearrange("p (n b) -> p n b", b=DB)
                v.scalar_tensor_tensor(cT[:, 0:H, LP:TOKENS], cT[:, 0:H, LP:TOKENS], SCALE, rs8[:, 0:H, :],
                                       ALU.mult, ALU.mult).then_inc(n_dve, 1)
                v.tensor_tensor(cT[:, H:2 * H, LP:TOKENS], cT[:, H:2 * H, LP:TOKENS], rs8[:, H:2 * H, :], ALU.mult)\
                    .then_inc(n_dve, 1)
                v.tensor_scalar(t5(rq), rr[:, :, 0:H], SCALE, None, ALU.mult).then_inc(n_dve, 1)
                v.tensor_tensor(t5(eR), t5(eR), rr[:, :, H:2 * H], ALU.mult).then_inc(n_dve, 1)
                v.tensor_tensor(t5(btk), t5(bt), rr[:, :, H:2 * H], ALU.mult).then_inc(n_dve, 1)
                dve.wait_ge(n_dve, 10)
                v.scalar_tensor_tensor(rq2, rq, 1.0 / P, rq, ALU.mult, ALU.mult).then_inc(n_dve, 1)
                v.scalar_tensor_tensor(nbG, btk, -1.0, eG, ALU.mult, ALU.mult).then_inc(n_dve, 1)
                dve.wait_ge(n_act, 3)
                v.tensor_scalar(lnk, lnk, -0.5, None, ALU.mult).then_inc(n_dve, 1)
                dve.wait_ge(n_dve, N_END)

            def t5(x):
                return x.rearrange("p (t h) -> p t h", h=H)

            def decays():
                v.memset(ab5[:, :, :], 0.0).then_inc(ab_d, 1)
                dve.wait_ge(ab_d, 1)
                dve.wait_ge(ab_t, 1)
                v.tensor_copy(ab5[:, 0:4, :], ps[:, 4, 0:64].rearrange("p (t h) -> p t h", t=4)).then_inc(ab_d, 1)
                v.tensor_copy(ab5[0:LAST, 4, :], ps[0:LAST, 4, 64:80]).then_inc(ab_d, 1)
                dve.wait_ge(ab_d, 3)
                v.tensor_tensor(t5(tmp1), ab5[:, :, 0:H], dtb[:, :].unsqueeze(1).to_broadcast([P, TT, H]), ALU.add)\
                    .then_inc(ab_d, 1)
                dve.wait_ge(ab_a, 4)
                dve.wait_ge(ab_d, 4)
                v.scalar_tensor_tensor(tmp1, tmp1, 0.0, tmp2, ALU.max, ALU.add).then_inc(ab_d, 1)
                dve.wait_ge(ab_d, 5)
                v.scalar_tensor_tensor(t5(gt), t5(tmp1), -1.0, eal[:, 0:H].unsqueeze(1).to_broadcast([P, TT, H]),
                                       ALU.mult, ALU.mult).then_inc(ab_d, 1)
                dve.wait_ge(ab_a, AB_END)

            def chunks():
                v.memset(S, 0.0).then_inc(g_dve0, 1)
                for c in range(TT):
                    n = chunk(c)

                    def after(eng, *key):
                        s, at_ = {"act": (g_act, ACT_AT), "pe": (g_pe, PE_AT), "pool": (g_pool, POOL_AT),
                                  "dve": (g_dve, DVE_AT)}[eng]
                        if key[0] >= 0:
                            dve.wait_ge(s, at_[key])

                    def hs(g):
                        return slice(4 * g, 4 * g + 4)

                    def bank(i, w, m=n):
                        return ps[0:m, i, 0:4 * w].rearrange("p (h j) -> p h j", h=4)

                    def one(x, h):
                        return x[0:n, H * c + h:H * c + h + 1]

                    for g in G2:
                        after("pe", c - 1, "kv", g)
                        after("pe", c, "tk", g)
                        v.tensor_tensor(krs[0:n, hs(g), :], bank(g, P),
                                        per_head(eR[0:n, H * c + 4 * g:H * c + 4 * g + 4], P), ALU.mult).then_inc(g_dve, 1)
                    for g in G2:
                        after("pe", c, "tv", g)
                        v.tensor_tensor(bvs[0:n, hs(g), :], bank(2 + g, P),
                                        per_head(bt[0:n, H * c + 4 * g:H * c + 4 * g + 4], P), ALU.mult).then_inc(g_dve, 1)
                    for g in G2:
                        after("pe", c, "kk", g)
                        after("pool", c, "dr", g)
                        for h in range(4 * g, 4 * g + 4):
                            i = (h % 4) * n
                            m = v.scalar_tensor_tensor(DR[0:n, h, 0:n], ps[0:n, g, i:i + n], one(btk, h), DR[0:n, h, 0:n],
                                                       ALU.mult, ALU.mult)
                        m.then_inc(g_dve, 1)
                    for g in G2:
                        after("pe", c, "kq", g)
                        after("pool", c, "dc", g)
                        v.tensor_tensor(DC[0:n, hs(g), 0:n], bank(2 + g, n), DC[0:n, hs(g), 0:n], ALU.mult).then_inc(g_dve, 1)
                    idb = ident[0:n, 0:n].unsqueeze(1).to_broadcast([n, 4, n])
                    for g in G2:
                        after("pe", c, "lt", g)
                        v.tensor_tensor(Um[0:n, hs(g), 0:n], idb, bank(4 + g, n), ALU.subtract).then_inc(g_dve, 1)
                        v.tensor_tensor(Tm[0:n, hs(g), 0:n], idb, Lm[0][0:n, hs(g), 0:n], ALU.subtract).then_inc(g_dve, 1)
                    for s in LEVELS[c][1:]:
                        w = n // 2
                        for g in G2:
                            after("pe", c, "up", s, g)
                            ue, te = odd(Um[0:n, hs(g), 0:n], s), even(Tm[0:n, hs(g), 0:n], s)

                            def upd(o):
                                return ps[0:n, 2 + g, o:o + 4 * w].rearrange("p (h b s) -> p h b s", h=4, s=s)
                            v.tensor_tensor(ue, ue, upd(0), ALU.subtract).then_inc(g_dve, 1)
                            if 2 * s < n:
                                v.tensor_tensor(te, te, upd(256), ALU.subtract).then_inc(g_dve, 1)
                    for g in G2:
                        after("pe", c, "ks", g)
                        for h in range(4 * g, 4 * g + 4):
                            i = (h % 4) * P
                            m = v.scalar_tensor_tensor(bvs[0:n, h, :], ps[0:n, 4 + g, i:i + P], one(nbG, h), bvs[0:n, h, :],
                                                       ALU.mult, ALU.add)
                        m.then_inc(g_dve, 1)
                    for g in G2:
                        after("pe", c, "o2", g)
                        after("act", c, "qs", g)
                        v.tensor_tensor(Q1[0:n, hs(g), :], Q1[0:n, hs(g), :], bank(2 + g, P), ALU.add).then_inc(g_dve, 1)
                    after("pool", c, "sq")
                    v.tensor_reduce(onr[0:n, 0:H], Lm[0][0:n, :, :], AX.X, ALU.add).then_inc(g_dve, 1)
                    after("dve", c, "ss")
                    v.tensor_tensor(onr[0:n, 0:H], onr[0:n, 0:H], rq2[0:n, H * c:H * c + H], ALU.mult).then_inc(g_dve, 1)
                    for g in G2:
                        after("pe", c, "kv", g)
                        for h in range(4 * g, 4 * g + 4):
                            i = (h % 4) * P
                            m = v.scalar_tensor_tensor(S[:, h, :], S[:, h, :], eL[:, H * c + h:H * c + h + 1],
                                                       ps[:, 4 + g, i:i + P], ALU.mult, ALU.add)
                        m.then_inc(g_dve, 1)
                    after("act", c, "rt")
                    v.reciprocal(onr[0:n, 2 * H:3 * H], onr[0:n, H:2 * H]).then_inc(g_dve, 1)
                    after("dve", c, "rc")
                    v.tensor_tensor(onr[0:n, 2 * H:3 * H], onr[0:n, 2 * H:3 * H], rq[0:n, H * c:H * c + H], ALU.mult)\
                        .then_inc(g_dve, 1)
                    after("dve", c, "rq")
                    v.tensor_tensor(Q1[0:n, :, :], Q1[0:n, :, :], per_head(onr[0:n, 2 * H:3 * H], P), ALU.mult)\
                        .then_inc(g_dve, 1)

            def sampled_delta():
                count = [0]

                def step(ins):
                    ins.then_inc(t_dve, 1)
                    count[0] += 1
                    dve.wait_ge(t_dve, count[0])

                def bh(x):
                    return x.rearrange("p (b h) -> p b h", h=H)

                def of(i):
                    return cT[:, H * i:H * i + H, LP:TOKENS].rearrange("p h b -> p b h")
                qk, kk, t1, vn, t2, o, osq, rs, eg, be = (dsm[:, i, :] for i in range(10))
                step(v.tensor_tensor(bh(qk), of(0), of(1), ALU.mult))
                step(v.tensor_copy(bh(kk), of(1)))
                dve.wait_ge(t_pe, 2)
                sqk = ps[:, 0, 0:P].rearrange("p (r two) -> p r two", two=2)
                step(v.tensor_tensor(t1, sqk[:, :, 1], eg, ALU.mult))
                step(v.tensor_tensor(bh(t1), of(2), bh(t1), ALU.subtract))
                step(v.tensor_tensor(vn, t1, be, ALU.mult))
                step(v.tensor_tensor(t2, sqk[:, :, 0], eg, ALU.mult))
                step(v.tensor_tensor(o, vn, ps[:, 1, 0:64], ALU.mult))
                step(v.tensor_tensor(o, o, t2, ALU.add))
                step(v.tensor_tensor(osq, o, o, ALU.mult))
                dve.wait_ge(t_pe, 3)
                step(v.tensor_copy(vrow[:, :], ps[0:64, 2, 0:P]))
                step(v.tensor_copy(krow[:, :], ps[0:64, 2, P:2 * P]))
                dve.wait_ge(t_act, 2)
                step(v.reciprocal(rs, rs))
                step(v.tensor_tensor(o, o, rs, ALU.mult))
                for j in range(4):
                    for i in range(4):
                        dve.wait_ge(t_pe, 5 + 4 * j + i)
                        for r4 in range(4):
                            r = 16 * j + 4 * i + r4
                            m = v.scalar_tensor_tensor(st[:, r, :], st[:, r, :], eg[:, r:r + 1],
                                                       ps[:, 4 + i, r4 * P:r4 * P + P], ALU.mult, ALU.add)
                        m.then_inc(t_dve, 1)

            v.memset(epsc[:, :], EPS).then_inc(eps_ready, 1)
            copy_x(0, hT0)
            dve.wait_ge(par_t, 1)
            v.tensor_copy(cols[:, 0:25], ps[:, 6, 0:25]).then_inc(par_c, 1)
            v.tensor_copy(convw[:, :, :], ps[:, 6, P:P + 96].rearrange("p (i n) -> p i n", i=CW)).then_inc(par_c, 1)
            dve.wait_ge(par_c, 2)
            dve.wait_ge(xt_a, KT)
            dve.wait_ge(xt_d, KT)
            normalise(0, hT0, 0, rstd)
            dve.wait_ge(par_t, 2)
            for i in range(2):
                v.tensor_copy(cbuf[:, 12 * i:12 * i + 12, :],
                              ps[:, 6 + i, 0:288].rearrange("p (n c) -> p n c", n=12)).then_inc(cb_c, 1)
            dve.wait_ge(xn_ready, KT)
            v.memset(R[:, 2 * A8:2 * A8 + P], 0.0).then_inc(kpad, 1)
            dve.wait_ge(qr_t, 1)
            v.tensor_copy(qrow[:, :].rearrange("p (a n) -> p a n", a=2), ps[0:DB, 6:8, :]).then_inc(qr_c, 1)
            for s in range(SEGS):
                if s in CHAIN_IN:
                    chain_sp(CHAIN_IN[s])
                if s == 2:
                    v.memset(upad[:, :, 0:CW - 1], 0.0).then_inc(up_zero, 1)
                for q in range(4):
                    if s in (2, 3, 4) and (s - 2) * KT + 2 * q >= 2:
                        conv((s - 2) * KT + 2 * q - 2)
                        conv((s - 2) * KT + 2 * q - 1)
                    if s == 7:
                        for j in (2 * q, 2 * q + 1):
                            dve.wait_ge(act_read, READ_COUNT[T_SEG + 6 * KT + j])
                            dve.wait_ge(w_used, done(T_SEG + s * KT + j))
                            v.tensor_tensor(halves(mT[:, j, :]), halves(sgA[:, j, :]), pair(T_SEG + s * KT + j), ALU.mult)\
                                .then_inc(dve_read, 1)
                    for b, p in pages_of(K_IN.get(s, ()), q, 4):
                        k_page(b, p)
                    if s in CHAIN_IN and q == 0:
                        chain_arg(CHAIN_IN[s])
                    if s == 8 and q == 2:
                        chain_sp(DB - 1)
                        chain_arg(DB - 1)
                    for b, p in pages_of(V_IN.get(s, ()), q, 4):
                        v_page(b, p)
                if s == 1:
                    chain_sp(V_ATT)
                    for t in range(TT):
                        token_bank(t, vtok[:, t, :], t)
                    chain_arg(V_ATT)
                    for t in range(TT):
                        if t >= 2:
                            dve.wait_ge(k_out[t % 2], 16 * (t // 2))
                        token_bank(TT + t, ktok[:, t % 2, :], t)
                    attend()
                    dve.wait_ge(s_av, H)
                    dve.wait_ge(v_out, 16 * 6)
                if s == 4:
                    conv(NQKV - 2)
                    conv(NQKV - 1)
                    conv_sampled()
                    for i in range(6):
                        dve.wait_ge(co_t, i + 1)
                        v.tensor_copy(convrow_sb[0:11, i * 512:i * 512 + 512], ps[0:11, i % 2, :]).then_inc(co_c, 1)
                    decays()
                    norm_qk()
                    chunks()
                    sampled_delta()
            for n in range(KT):
                dve.wait_ge(act_read, READ_COUNT[T_SEG + 8 * KT + n])
                dve.wait_ge(w_used, done(T_PB + n))
                v.tensor_tensor(halves(sgB[:, n, :]), halves(sgB[:, n, :]), pair(T_PB + n), ALU.mult).then_inc(dve_read, 1)
                dve.wait_ge(dve_read, READ_COUNT[T_PB + n])
                v.tensor_tensor(mT[:, n, :], mT[:, n, :], sgB[:, n, :], ALU.add).then_inc(a_full, 1)
                if n >= 1:
                    act_lo(dve, n - 1, m_hi[n - 1], m_full[n - 1], m_lo[n - 1])
                if n == KT - 1:
                    split_lo(dve, T_O)
            act_lo(dve, KT - 1, m_hi[KT - 1], m_full[KT - 1], m_lo[KT - 1])
            split_lo(dve, T_O + 1)
            copy_x(1, hT)
            dve.wait_ge(xt_a, 2 * KT)
            dve.wait_ge(xt_d, 2 * KT)
            for n in range(KT):
                split_lo(dve, T_O + n + 2)
                dve.wait_ge(w_used, done(T_O + n))
                v.tensor_tensor(halves(hT[:, n, :]), halves(hT[:, n, :]), pair(T_O + n), ALU.add).then_inc(dve_read, 1)
            dve.wait_ge(dve_read, READ_COUNT[T_O + KT - 1])
            normalise(1, hT, KT, rstd1)
            for n in range(FT + 1):
                if n < FT:
                    split_lo(dve, T_FI + 2 * n + 2)
                    if n < FT - 1:
                        split_lo(dve, T_FI + 2 * n + 3)
                if n >= 1:
                    act_lo(dve, 2 * KT + n - 1, h_hi[n - 1], h_full[n - 1], h_lo[n - 1])
                if n < FT:
                    dve.wait_ge(act_read, READ_COUNT[T_FI + 2 * n])
                    dve.wait_ge(w_used, done(T_FI + 2 * n + 1))
                    v.tensor_tensor(halves(h_full[n]), halves(gtmp[:, n % 2, :]), pair(T_FI + 2 * n + 1), ALU.mult)\
                        .then_inc(dve_read, 1)
            split_lo(dve, T_FO + 1)
            for n in range(KT):
                if n + 2 < KT:
                    split_lo(dve, T_FO + n + 2)
                dve.wait_ge(w_used, done(T_FO + n))
                v.tensor_tensor(halves(hT[:, n, :]), halves(hT[:, n, :]), pair(T_FO + n), ALU.add).then_inc(dve_read, 1)
            dve.wait_ge(dve_read, READ_COUNT[T_FO + KT - 1])
            normalise(2, hT, 2 * KT, rstd2)
            for t in range(TT):
                token_bank(2 * TT + t, ytok[:, t, :], t)

        @block.gpsimd
        def _(pool):
            g_ = nc.gpsimd

            def keep(out, in_, pattern, base, cm, op=ALU.is_ge, fill=0.0):
                return g_.affine_select(out=out, in_=in_, pattern=pattern, compare_op=op, fill=fill,
                                        base=base, channel_multiplier=cm)
            for m in (ident, zeros):
                g_.memset(m[:, :], 0.0).then_inc(const_step, 1)
            for m in (ones, tri_ge, tri_le, tri_gt):
                g_.memset(m[:, :], 1.0).then_inc(const_step, 1)
            g_.memset(lvl[:, :, :], 1.0).then_inc(const_step, 1)
            g_.memset(sel[:, :, :], 1.0).then_inc(const_step, 1)
            pool.wait_ge(const_step, 8)
            keep(ident[:, :], ident[:, :], [[-1, P]], 0, 1, ALU.not_equal, 1.0).then_inc(const_ready, 1)
            keep(tri_ge[:, :], tri_ge[:, :], [[-1, P]], 0, 1).then_inc(const_ready, 1)
            keep(tri_le[:, :], tri_le[:, :], [[1, P]], 0, -1).then_inc(const_ready, 1)
            keep(tri_gt[:, :], tri_gt[:, :], [[-1, P]], 0, 1, ALU.is_gt).then_inc(const_ready, 1)
            keep(sel[:, :, :], sel[:, :, :], [[-1, DB], [0, P]], 0, 1, ALU.is_equal).then_inc(const_ready, 1)
            for i in range(7):
                s = 1 << i
                v = lvl[:, i, :].rearrange("p (b two s) -> p b two s", two=2, s=s)
                nb = P // (2 * s)
                g_.memset(v[:, :, 1, :], 0.0).then_inc(const_step, 1)
                keep(v[:, :, 0, :], v[:, :, 0, :], [[-2 * s, nb], [0, s]], -s, 1).then_inc(const_step, 1)
            pool.wait_ge(const_step, 8 + 14)
            for i in range(7):
                s = 1 << i
                v = lvl[:, i, :].rearrange("p (b two s) -> p b two s", two=2, s=s)
                keep(v[:, :, 0, :], v[:, :, 0, :], [[2 * s, P // (2 * s)], [0, s]], 2 * s - 1, -1).then_inc(const_ready, 1)

            def causal(buf, fill, sig):
                for kt in range(TT):
                    n = chunk(kt)
                    f = sb_at(kt, P * kt)[2]
                    m = keep(buf[:, f:f + n], buf[:, f:f + n], [[1, n]], 0, -1, ALU.is_gt, fill)
                m.then_inc(sig, 1)

            pool.wait_ge(s_sp, 1)
            causal(sps[:, 0, :], 0.0, s_msp)
            for h in range(H):
                if h + 1 < H:
                    pool.wait_ge(s_sp, h + 2)
                    causal(sps[:, (h + 1) % 2, :], 0.0, s_msp)
                pool.wait_ge(s_arg, h + 1)
                causal(zs[:, h % 2, :], NEG, s_marg)
            for n in range(NQKV):
                pool.wait_ge(act_read, READ_COUNT[T_SEG + 2 * KT + n])
                g_.tensor_copy(rawt[:, n, :], upad[:, n % 2, CW - 1 + LP - 3:CW - 1 + TOKENS]).then_inc(raw_c, 1)
            pool.wait_ge(ab_d, AB_G)
            g_.tensor_copy(gP[:, 0:32], gt[:, 0:32]).then_inc(ab_p, 1)
            keep(gP[:, 32:40], gt[:, 32:40], [[0, H]], LASTP - 1, -1).then_inc(ab_p, 1)
            pool.wait_ge(ab_p, 2)

            def decay_columns(c):
                n, gm = chunk(c), gms[c % 2]
                g_.tensor_tensor(gm[0:n, :, 0:n], tri_gt[0:n, 0:n].unsqueeze(1).to_broadcast([n, H, n]),
                                 per_head(gP[0:n, H * c:H * c + H], n), ALU.mult).then_inc(g_pool, 1)
                g_.tensor_tensor(dg[0:n, :, 0:n], ident[0:n, 0:n].unsqueeze(1).to_broadcast([n, H, n]),
                                 per_head(lnk[0:n, H * c:H * c + H], n), ALU.mult).then_inc(g_pool, 1)
                pool.wait_ge(g_pool, POOL_AT[c, "gd"])
                g_.tensor_tensor(gm[0:n, :, 0:n], gm[0:n, :, 0:n], dg[0:n, :, 0:n], ALU.add).then_inc(g_pool, 1)

            pool.wait_ge(c_out, 16 * 3)
            pool.wait_ge(n_dve, N_END)
            decay_columns(0)
            for c in range(TT):
                n = chunk(c)

                def after(eng, *key):
                    s, at_ = {"act": (g_act, ACT_AT), "pe": (g_pe, PE_AT), "dve": (g_dve, DVE_AT)}[eng]
                    if key[0] >= 0:
                        pool.wait_ge(s, at_[key])

                def hs(g):
                    return slice(4 * g, 4 * g + 4)
                for g in G2:
                    after("act", c, "dr", g)
                    keep(DR[0:n, hs(g), 0:n], DR[0:n, hs(g), 0:n], [[0, 4], [-1, n]], 0, 1, ALU.is_gt).then_inc(g_pool, 1)
                for g in G2:
                    after("act", c, "dc", g)
                    keep(DC[0:n, hs(g), 0:n], DC[0:n, hs(g), 0:n], [[0, 4], [1, n]], 0, -1).then_inc(g_pool, 1)
                for j, s in enumerate(LEVELS[c]):
                    for g in G2:
                        if j == 0:
                            after("dve", c, "A", g)
                            if c:
                                after("dve", c - 1, "ss")
                        elif j == 2:
                            after("dve", c, "T1", g)
                            after("pe", c, "lt", g)
                        elif j >= 3:
                            after("pe", c, "q1", LEVELS[c][j - 2], g)
                        elif j == 1 and c:
                            after("pe", c - 1, "q1", LEVELS[c - 1][-1], g)
                        g_.tensor_tensor(Lm[j % 2][0:n, hs(g), 0:n], DR[0:n, hs(g), 0:n],
                                         lvl[0:n, j, 0:n].unsqueeze(1).to_broadcast([n, 4, n]), ALU.mult)\
                            .then_inc(g_pool, 1)
                if c + 1 < TT:
                    decay_columns(c + 1)
                after("dve", c, "o", 0)
                after("dve", c, "o", 1)
                g_.tensor_tensor(Lm[0][0:n, :, :], Q1[0:n, :, :], Q1[0:n, :, :], ALU.mult).then_inc(g_pool, 1)
            pool.wait_ge(t_dve, T_ROWS)
            for j in range(4):
                if j:
                    pool.wait_ge(t_pe, 4 + 4 * j)
                g_.tensor_tensor(ksel[:, :, :], krow[:, :].unsqueeze(1).to_broadcast([64, 16, P]),
                                 per_head(ident[64:P, 64 + 16 * j:64 + 16 * j + 16], P), ALU.mult).then_inc(t_pool, 1)
            pool.wait_ge(t_act, 3)
            for j in range(KT):
                pool.wait_ge(act_read, READ_COUNT[T_SEG + 5 * KT + j])
                g_.tensor_tensor(oaT[:, j, :], oaT[:, j, :], ztmp[:, j % 2, :], ALU.mult).then_inc(z_done, 1)


NPHYS = 160
NCONST = 12
AB_X, AB_G, AB_B, AB_END, AB_DEND = 4, 6, 5, 10, 6
N_ROWS, N_END = 3, 13
T_VN, T_OSQ, T_ROWS, T_ON, T_S0 = 5, 9, 11, 13, 13
T_PE_END = 20
_VIEWS = {
    "x_prompt": (SEQ, D), "x_sample": (DB, D), "cache_k": (NPHYS, PAGE, D), "cache_v": (NPHYS, PAGE, D),
    "state_rec": (DB, H, P, P), "state_conv": (DB * 3, 3 * D), "page_table": (1, DB * PAGES),
    "meta_tokens": (META, D), "norm_mix": (KT, P), "w_in": (D, 9232), "conv_w": (CW * NQKV, P),
    "a_log": (1, H), "dt_bias": (1, H), "gdn_norm": (1, P), "sb_bias": (1, H), "w_pa": (D, D), "w_pb": (D, D),
    "w_o": (D, D), "norm_ffn": (KT, P), "w_ffn_in": (D, 2 * D_FF), "w_ffn_out": (D_FF, D), "norm_final": (KT, P),
}
_OUTS = [("y_prompt", (SEQ, D), (1, SEQ, D)), ("y_sample", (DB, D), (DB, 1, D)),
         ("k_prompt", (LP, D), (1, 1, LP, H, P)), ("v_prompt", (LP, D), (1, 1, LP, H, P)),
         ("k_sample", (DB, D), (1, DB, 1, H, P)), ("v_sample", (DB, D), (1, DB, 1, H, P)),
         ("rec_prompt", (H, P, P), (1, 1, H, P, P)), ("rec_sample", (DB, H, P, P), (1, DB, H, P, P)),
         ("conv_prompt", (3, 3 * D), (1, 1, 3, 3 * D)), ("conv_sample", (DB, 3, 3 * D), (1, DB, 3, 3 * D))]


def kernel(**inputs):
    import numpy as _np
    import concourse.bacc as _bacc
    from concourse.bass_utils import run_bass_kernel_spmd as _run

    nc = _bacc.Bacc("TRN2", target_bir_lowering=False, num_devices=1)
    arrays, io = {}, {}
    for name, shape in _VIEWS.items():
        a = _np.ascontiguousarray(inputs[name]).reshape(shape)
        arrays[f"in_{name}"] = a
        io[name] = nc.dram_tensor(f"in_{name}", shape, mybir.dt.from_np(a.dtype), kind="ExternalInput").ap()
    io["state_conv3"] = io["state_conv"].rearrange("(b i) n -> b i n", i=3)
    for name, shape, _ in _OUTS:
        io[name] = nc.dram_tensor(f"out_{name}", shape, F32, kind="ExternalOutput").ap()
    build(nc, io)
    r = _run(nc, [arrays], core_ids=[0])
    return tuple(r.results[0][f"out_{name}"].reshape(whole) for name, _, whole in _OUTS)
```

```python
from contextlib import ExitStack

import concourse.bass as bass
from concourse import mybir

F32 = mybir.dt.float32
F32R = mybir.dt.float32r
I32 = mybir.dt.int32
ALU = mybir.AluOpType
ACT = mybir.ActivationFunctionType
AX = mybir.AxisListType

P = 128
D = 1024
KT = D // P
META, SEQ, DB = 16, 512, 8
LP = META + SEQ
TOKENS = LP + DB
HALF = TOKENS // 2
TT = 5
LAST = TOKENS - 4 * P
LASTP = LP - 4 * P
H = 8
PAGES, PAGE = 16, 128
CW = 4
D_FF = 2816
FT = D_FF // P
SCALE = float(P) ** -0.5
EPS = 1e-6
NQKV = 24
SEGS = 9
RING = 4
NEG = -1.0e30

C_QKV, C_Z, C_AB, C_Q, C_K, C_V, C_GA, C_GB = 0, 3072, 4096, 4112, 5136, 6160, 7184, 8208
SEG_W = [("w_in", C_K), ("w_in", C_V), ("w_in", C_QKV), ("w_in", C_QKV + D), ("w_in", C_QKV + 2 * D),
         ("w_in", C_Z), ("w_in", C_GA), ("w_pa", 0), ("w_in", C_GB)]

def weight_pieces():
    out = [("w_in", C_AB, 0, KT, 2 * H)]
    out += [("w_in", C_Q + P * n, 0, KT, P) for n in range(KT)]
    for name, col in SEG_W:
        out += [(name, col + P * n, 0, KT, P) for n in range(KT)]
    out += [("w_pb", P * n, 0, KT, P) for n in range(KT)]
    out += [("w_o", P * n, 0, KT, P) for n in range(KT)]
    for n in range(FT):
        out += [("w_ffn_in", P * n, 0, KT, P), ("w_ffn_in", D_FF + P * n, 0, KT, P)]
    for n in range(KT):
        out += [("w_ffn_out", P * n, 0, 8, P), ("w_ffn_out", P * n, 8, 16, P), ("w_ffn_out", P * n, 16, 22, P)]
    return out


T_AB, T_Q, T_SEG = 0, 1, 9
T_PB = T_SEG + SEGS * KT
T_O = T_PB + KT
T_FI = T_O + KT
T_FO = T_FI + 2 * FT
TILES = T_FO + KT


def reader(t):
    if T_SEG + 7 * KT <= t < T_SEG + 8 * KT or T_PB <= t < T_FI or t >= T_FO:
        return "dve"
    if T_FI <= t < T_FO:
        return "act" if (t - T_FI) % 2 == 0 else "dve"
    return "act"


READ_COUNT = []
for _t in range(TILES):
    READ_COUNT.append(sum(reader(u) == reader(_t) for u in range(_t + 1)))


def piece_of(t):
    return t if t < T_FO else T_FO + 3 * (t - T_FO)


SB_PIECES = [(0, 0, 512, 0, 0),
             (1, 128, 528, 1, 0), (0, 512, 528, 1, 400), (4, 512, 528, 1, 416),
             (2, 256, 528, 2, 0), (3, 384, 528, 2, 272)]
SB_WIDTH = [512, 432, 416]
SB_FLAT = [0, 512, 944]
SB_ALL = 1360


def sb_at(kt, q):
    for k, a, b, bank, col in SB_PIECES:
        if k == kt and a <= q < b:
            return bank, col + q - a, SB_FLAT[bank] + col + q - a


K_IN = {0: (0, 1), 3: (3,), 7: (7,)}
V_IN = {1: (0,), 2: (2,), 4: (3,)}
K_ATT, V_ATT = 2, 1
V_POOL = (4, 6)
POOL_PAGES = {(6, 1): 4, (6, 2): 2, (6, 3): 3, (7, 0): 3, (7, 1): 4,
              (7, 2): 3, (7, 3): 3, (8, 0): 4, (8, 1): 3, (8, 2): 3}
V_DVE = [b for b in range(DB) if b not in V_POOL]
SPREAD_AT = {(0, 1): 1, (1, 4): 2, (2, 4): 3, (3, 4): 4, (4, 4): 5, (6, 0): 6, (6, 6): 7}
PUT_Q_AT = {(0, 2): 1, (1, 5): 2, (2, 5): 3, (3, 5): 4, (4, 5): 5, (6, 1): 6, (6, 7): 7}
SOFT_AT = {(0, 5): 0, (1, 4): 1, (2, 0): 2, (4, 0): 3, (6, 0): 4, (6, 4): 5, (7, 1): 6, (8, 0): 7}
SUMS_AT = {(0, 6): 0, (1, 5): 1, (2, 0): 2, (4, 0): 3, (6, 0): 4, (6, 5): 5, (7, 2): 6, (8, 1): 7}
WEIGHT_AT = {(1, 1): 0, (1, 7): 1, (2, 1): 2, (4, 1): 3, (6, 1): 4, (6, 6): 5, (7, 4): 6, (8, 3): 7}
SUM_V_AT = {(2, 0): 1, (3, 0): 2, (7, 4): 4, (8, 3): 5}
PUT_O_AT = {(2, 1): 1, (3, 1): 2, (7, 5): 4, (8, 4): 5}
SP_AT = {(0, 3): 0, (1, 2): 1, (2, 0): 2, (4, 0): 3, (6, 0): 4, (6, 2): 5, (8, 0): 7}
ARG_AT = {(1, 0): 0, (1, 3): 1, (2, 0): 2, (4, 0): 3, (6, 0): 4, (6, 2): 5, (8, 1): 7}


def pages_of(seqs, part, parts):
    every = [(b, p) for b in seqs for p in range(PAGES)]
    n = len(every) // parts
    return every[n * part:n * part + n]


def k_pages(s, part, parts):
    if s in (5, 6):
        every = pages_of((4, 5, 6), s - 5, 2)
        n = len(every) // parts
        return every[n * part:n * part + n]
    return pages_of(K_IN.get(s, ()), part, parts)


def k_ahead(q, i):
    every = k_pages(5, 0, 1)
    return {(0, 0): every[0:4], (2, 0): every[4:12], (3, 0): every[12:24]}.get((q, i), [])


def v_pages(s, part, parts):
    if s == 7:
        return pages_of((5,), part, 2 * parts)
    if s == 8:
        first, n = ((0, 8), (8, 5), (13, 6), (19, 5))[part * 4 // parts]
        return (pages_of((5, 7), 0, 1)[8:])[first:first + n] if part * 4 % parts == 0 else []
    return pages_of(V_IN.get(s, ()), part, parts)


def v_number(b, p):
    return (V_POOL if b in V_POOL else V_DVE).index(b) * PAGES + p


def fr(v):
    return v.bitcast(F32R)


def build(nc, io):
    with ExitStack() as ctx:
        def sb(name, shape, dt=F32):
            return ctx.enter_context(nc.sbuf_tensor(name, shape, dt))

        def twins(name, shape):
            with nc.sbuf_tensor(name + "_split", shape, F32) as split:
                pass
            return sb(name, shape), split

        def sem(name):
            return ctx.enter_context(nc.semaphore(name))

        ps = ctx.enter_context(nc.psum_tensor("ps", [P, 8, 512], F32))

        xn, xn2 = twins("xn", [P, KT, TOKENS])
        obT, obT2 = twins("obT", [P, H, TOKENS])
        wring, wring2 = twins("wring", [P, RING, KT * P])
        kring, kring2 = twins("kring", [P, RING, D])
        vring, vring2 = twins("vring", [P, RING, D])
        qv, qv2 = twins("qv", [P, 4, D])
        qbc, qbc2 = qv[:, 0:2, :], qv2[:, 0:2, :]
        vacc, vacc2 = qv[:, 2:4, :], qv2[:, 2:4, :]
        rows, rows2 = twins("rows", [P, D])
        qrow = rows[0:DB, :]
        dz = sb("dz", [P, 3, P])
        de = sb("de", [P, P])
        dsp = sb("dsp", [P, P])
        dsuf = sb("dsuf", [P, 2, P])
        dw = sb("dw", [P, 2, P])
        ident = sb("ident", [P, P])
        ones = sb("ones", [P, P])
        tri_ge = sb("tri_ge", [P, P])
        tri_le = sb("tri_le", [P, P])
        tri_gt = sb("tri_gt", [P, P])
        lvl, lvl2 = twins("lvl", [P, 7, P])
        sel = sb("sel", [DB, DB, P])
        cols = sb("cols", [P, 32])
        convw = sb("convw", [P, CW, NQKV])
        alog = sb("alog", [P, H])
        dtb = sb("dtb", [P, H])
        sbb = sb("sbb", [P, H])
        ptab = sb("ptab", [1, DB * PAGES], I32)
        rawt = sb("rawt", [P, NQKV, 11])
        cbuf = sb("cbuf", [P, NQKV, 3 * DB])
        abT = rows[32:32 + 2 * H, 0:TOKENS]
        R, R2 = twins("R", [P, 21056])

        def at(o, *shape):
            n = 1
            for s in shape:
                n *= s
            v = R[:, o:o + n]
            if len(shape) == 2:
                v = v.rearrange("p (a b) -> p a b", a=shape[0])
            return v

        A8 = KT * TOKENS
        xs0 = at(0, TT, D)
        hT0 = at(5120, KT, TOKENS)
        cst = at(9408, 3 * D)
        sq = at(12480, 2, TOKENS)
        rstd = at(13552, TOKENS)
        prow = at(14088, P)
        crow = at(14216, P)
        qbT = at(0, H, TOKENS)
        kbT = at(A8, H, TOKENS)
        kbflat = R[:, A8:2 * A8 + P]
        vtok = at(2 * A8 + P, TT, D)
        SBT = 2 * A8 + P + TT * D
        vbT = at(SBT, H, TOKENS)
        ktok = at(21056 - TT * D, TT, D)
        zs = [at(SBT, SB_ALL), at(SBT + SB_ALL, SB_ALL),
              qv[:, 1:3, :].rearrange("p a n -> p (a n)")[:, 0:SB_ALL]]
        sps = at(SBT + 2 * SB_ALL, 2, SB_ALL)
        es = at(SBT + 4 * SB_ALL, SB_ALL)
        cT = at(0, NQKV, TOKENS)
        oaT = at(0, H, TOKENS)
        G0 = 3 * A8
        upad = at(G0, 2, 3 + TOKENS)
        krs, bvs, gmA, DR, DC, Tm, Q1 = (at(G0 + i * 1024, H, P) for i in range(7))
        gms = [gmA, kring[:, 0, :].rearrange("p (h j) -> p h j", h=H)]
        vnb = kring[:, 1, :].rearrange("p (h j) -> p h j", h=H)
        Lm = [kring[:, 2 + i, :].rearrange("p (h j) -> p h j", h=H) for i in range(2)]
        vflat = vring[:, 2:4, :].rearrange("p a n -> p (a n)")
        SQB = 7
        sqg = kring[:, :, :].rearrange("p a n -> p (a n)")[:, 0:SQB * TOKENS].rearrange("p (a t) -> p a t", a=SQB)
        dg = vflat[:, 0:D].rearrange("p (h j) -> p h j", h=H)
        ztmp = vflat[:, 0:2 * TOKENS].rearrange("p (a t) -> p a t", a=2)
        nrm = vflat[:, 1088:1088 + 11 * 80].rearrange("p (a t) -> p a t", a=11)
        Um = vacc[:, 0, :].rearrange("p (h j) -> p h j", h=H)
        S = vacc[:, 1, :].rearrange("p (h j) -> p h j", h=H)
        cvt = at(G0 + 6 * 1024, NQKV, DB)
        st = at(G0, 64, P)
        ksel = vring[64:P, 0:2, :].rearrange("p a (r j) -> p (a r) j", r=8)
        sgA = at(A8, KT, TOKENS)
        sgB = at(2 * A8, KT, TOKENS)
        mT = at(3 * A8, KT, TOKENS)
        hT = at(0, KT, TOKENS)
        xs1, xs1_end = at(A8, TT - 1, D), at(4 * A8 + 2 * TOKENS, D)
        prings = [at(2 * A8, 4, D), at(4 * A8, 3, D)]
        hid = at(A8, FT, TOKENS)
        gtmp = at(A8 + FT * TOKENS, 2, TOKENS)
        sq1 = at(3 * A8 + TT * D, 2, TOKENS)
        rstd1 = at(3 * A8 + TT * D + 2 * TOKENS, TOKENS)
        ytok = at(A8, TT, D)
        whi, wlo = vring2, wring2

        def flat(buf):
            return buf[:, :, :].rearrange("p a n -> p (a n)")

        def cut(buf, n, o=0):
            return [buf[:, o + i * TOKENS:o + (i + 1) * TOKENS] for i in range(n)]

        def low_parts(ob, r, k, q, va, lv, ro):
            return (cut(r, KT, 3 * A8), cut(flat(ob), KT),
                    cut(flat(k), 7) + cut(r, 7, A8 + (FT + 2) * TOKENS) + cut(flat(q), 3) + cut(flat(va), 3)
                    + cut(flat(lv), 1) + cut(ro, 1))
        m_full, x_full, h_full = low_parts(obT, R, kring, qbc, vacc, lvl, rows)
        m_lo, x_lo, h_lo = low_parts(obT2, R2, kring2, qbc2, vacc2, lvl2, rows2)
        m_hi = cut(flat(kring2), 7) + cut(flat(qbc2), 1)
        x_hi = cut(flat(xn2), KT)
        h_hi = cut(R2, FT, A8)
        sq2, rstd2 = obT[:, 0:2, :], obT[:, 2, :]
        small = sb("small", [P, 11, 40])
        gt, bt, gP, eG, eR, eL, nbG, tmp1, tmp2, eal = (small[:, i, :] for i in range(10))
        onr = small[:, 10, :]
        srow = sb("srow", [1, P])
        dsm = sb("dsm", [P, 10, 64])
        krow, vrow = rows[64:P, 0:P], rows[64:P, P:2 * P]

        nr_q, nr_t, nr_r = (nrm[:, i, :] for i in range(3))
        rq, rq2, lnk, btk = (nrm[:, 3 + i // 2, 40 * (i % 2):40 * (i % 2) + 40] for i in range(4))
        nr_s = vflat[:, 1088 + 400:1088 + 400 + P]
        epsc = sb("epsc", [P, 1])
        pick = sb("pick", [P, 4 * H - 1])
        ab5 = sb("ab5", [P, TT, 2 * H])
        convrow_sb = R[:, G0 + 2 * 1024:G0 + 5 * 1024]
        g_dve0, eps_ready, kpad, pick_ready = sem("g_dve0"), sem("eps_ready"), sem("kpad"), sem("pick_ready")

        def convrows(a, b):
            return convrow_sb[a:b, :]

        const_step, const_ready = sem("const_step"), sem("const_ready")
        x_in = [sem("x_in0"), sem("x_in1")]
        par_in, pt_in, cst_in = sem("par_in"), sem("pt_in"), sem("cst_in")
        w_in_slot = [sem(f"w_in_slot{i}") for i in range(RING)]
        k_in = [sem(f"k_in{i}") for i in range(RING)]
        v_in = [sem(f"v_in{i}") for i in range(RING)]
        w_used = sem("w_used")
        act_read = sem("act_read")
        dve_read = sem("dve_read")
        k_used, v_used = sem("k_used"), sem("v_used")
        xt_ready, xt_a, xt_d = sem("xt_ready"), sem("xt_a"), sem("xt_d")
        sq_ready, sq_used = sem("sq_ready"), sem("sq_used")
        ms_ready, rt_ready, rc_ready, xn_ready = sem("ms_ready"), sem("rt_ready"), sem("rc_ready"), sem("xn_ready")
        par_t, par_c, cb_c = sem("par_t"), sem("par_c"), sem("cb_c")
        qr_t, qr_c, qb_t, qb_c = sem("qr_t"), sem("qr_c"), sem("qb_t"), sem("qb_c")
        dz_ready = sem("dz_ready")
        d_abs, d_exp, d_ln, d_sp, d_suf = sem("d_abs"), sem("d_exp"), sem("d_ln"), sem("d_sp"), sem("d_suf")
        d_cum, d_arg, d_w = sem("d_cum"), sem("d_arg"), sem("d_w")
        v_sum, ob_s = sem("v_sum"), sem("ob_s")
        tok_t, tok_a, tok_d = sem("tok_t"), sem("tok_a"), sem("tok_d")
        k_out, v_out, c_out, r_out, y_out = [sem("k_out0"), sem("k_out1")], sem("v_out"), sem("c_out"), sem("r_out"), sem("y_out")
        s_s, s_z, s_abs, s_exp, s_ln, s_sp = (sem(n) for n in ("s_s", "s_z", "s_abs", "s_exp", "s_ln", "s_sp"))
        s_msp, s_c, s_arg, s_marg, s_w, s_av, s_o = (sem(n) for n in ("s_msp", "s_c", "s_arg", "s_marg", "s_w", "s_av", "s_o"))
        up_zero, cv_step, cs_done, raw_c = sem("up_zero"), sem("cv_step"), sem("cs_done"), sem("raw_c")
        sc_step = sem("sc_step")
        n_sq, n_ss, n_act, n_dve, n_tt = (sem(n) for n in ("n_sq", "n_ss", "n_act", "n_dve", "n_tt"))
        nrow = rows[64:64 + 2 * H, 0:TOKENS]
        co_t, co_c = sem("co_t"), sem("co_c")
        ab_t, ab_d, ab_a, ab_p, ab_row, ab_m = (sem(n) for n in ("ab_t", "ab_d", "ab_a", "ab_p", "ab_row", "ab_m"))
        g_pe, g_act, g_dve, g_pool = (sem(n) for n in ("g_pe", "g_act", "g_dve", "g_pool"))
        t_in = [sem(f"t_in{i}") for i in range(4)]
        t_pe, t_dve, t_act, t_pool = (sem(n) for n in ("t_pe", "t_dve", "t_act", "t_pool"))
        z_done, zs_done = sem("z_done"), sem("zs_done")
        zs_cp, p_mul = sem("zs_cp"), sem("p_mul")
        p_in, p_used = [[sem(f"p_in{k}_{i}") for i in range(4 - k)] for k in range(2)], sem("p_used")
        zsv = vflat[:, 2 * D - H * DB:2 * D].rearrange("p (h b) -> p h b", h=H)
        w_hi, w_lo = sem("w_hi"), sem("w_lo")
        a_full, a_hi, a_lo = sem("a_full"), sem("a_hi"), sem("a_lo")

        def slot_value(n):
            return 16 * (n // RING + 1)

        pieces = weight_pieces()

        def done(t):
            return piece_of(t) + (3 if t >= T_FO else 1)

        def wait_read(eng, t):
            eng.wait_ge(act_read if reader(t) == "act" else dve_read, READ_COUNT[t])

        def w_load(sp, p):
            name, col, k0, k1, n = pieces[p]
            if p >= RING:
                sp.wait_ge(w_used, p - RING + 1)
            dst = wring[:, p % RING, :].rearrange("p (k n) -> p k n", k=KT)[:, 0:k1 - k0, 0:n]
            src = io[name][k0 * P:k1 * P, col:col + n].rearrange("(k p) n -> p k n", p=P)
            sp.dma_start(dst, src).then_inc(w_in_slot[p % RING], 16)

        def split_hi(act, t):
            for p in range(piece_of(t), done(t)):
                n = (pieces[p][3] - pieces[p][2]) * P
                act.wait_ge(w_in_slot[p % RING], slot_value(p))
                nc.scalar.activation(fr(whi[:, p % RING, 0:n]), wring[:, p % RING, 0:n], ACT.Copy).then_inc(w_hi, 1)

        def split_lo(dve, t):
            for p in range(piece_of(t), done(t)):
                n = (pieces[p][3] - pieces[p][2]) * P
                dve.wait_ge(w_hi, p - piece_of(T_O) + 1)
                nc.vector.tensor_tensor(fr(wlo[:, p % RING, 0:n]), wring[:, p % RING, 0:n], whi[:, p % RING, 0:n],
                                        ALU.subtract).then_inc(w_lo, 1)

        def act_hi(act, i, dst, src):
            if i < 2 * KT:
                act.wait_ge(a_full, i + 1)
            else:
                act.wait_ge(dve_read, READ_COUNT[T_FI + 2 * (i - 2 * KT) + 1])
            nc.scalar.activation(fr(dst), src, ACT.Copy).then_inc(a_hi, 1)

        def act_lo(dve, i, hi, full, lo):
            dve.wait_ge(a_hi, i + 1)
            nc.vector.tensor_tensor(fr(lo), full, hi, ALU.subtract).then_inc(a_lo, 1)

        def w_block(p, k):
            return wring[:, p % RING, :].rearrange("p (k n) -> p k n", k=KT)[:, k, 0:pieces[p][4]]

        def pair(t, m=P):
            return ps[0:m, 2 * (t % 2):2 * (t % 2) + 2, 0:HALF]

        def halves(v):
            return v.rearrange("p (a b) -> p a b", a=2)

        def per_head(v, n):
            return v.unsqueeze(2).to_broadcast([v.shape[0], v.shape[1], n])

        def rows_of(t):
            return LAST if t == 4 else P

        def chunk(c):
            return LASTP if c == 4 else P

        LEVELS = {c: [s for s in (1, 2, 4, 8, 16, 32, 64) if s < chunk(c)] for c in range(TT)}
        G2 = (0, 1)

        def order(first, body, nxt, last):
            keys = [(0,) + k for k in first(0)]
            for c in range(TT):
                keys += [(c,) + k for k in body(c)]
                keys += [(c + 1,) + k for k in nxt(c + 1)] if c + 1 < TT else []
                keys += [(c,) + k for k in last(c)]
            return {k: i + 1 for i, k in enumerate(keys)}

        def pe_head(c):
            return [(n, g) for n in ("tk", "tv", "dr", "dc", "kk", "kq") for g in G2]

        def act_head(c):
            return [(n, g) for n in ("dr", "dc") for g in G2]

        def dve_head(c):
            return [(n, g) for n in ("kr", "bv") for g in G2]

        PE_AT = order(pe_head,
                      lambda c: [("lt", g) for g in G2]
                      + [(n, s, g) for s in LEVELS[c][1:] for n in ("q1", "up") for g in G2]
                      + [(n, g) for n in ("ks", "qs", "vn", "o2", "kv") for g in G2],
                      pe_head, lambda c: [("ot", g) for g in G2])
        ACT_AT = order(act_head,
                       lambda c: [("q1", s, g) for s in LEVELS[c][1:] for g in G2]
                       + [("qs", 0), ("qs", 1), ("vn", 0), ("vn", 1)],
                       act_head, lambda c: [("rt",), ("ot", 0), ("ot", 1)])
        DVE_AT = order(dve_head,
                       lambda c: [("A", 0), ("A", 1), ("qk", 0), ("qk", 1)]
                       + [(n, g) for g in G2 for n in ("U1", "T1")]
                       + [(n, s, g) for s in LEVELS[c][1:] for g in G2
                          for n in (("U", "T") if s != LEVELS[c][-1] else ("U",))]
                       + [("R", 0), ("R", 1), ("o", 0), ("o", 1), ("S", 0), ("S", 1), ("ss",), ("ms",)],
                       dve_head, lambda c: [("rc",), ("rq",), ("on",)])
        pool_steps = [(0, n) for n in ("gt", "gd", "gm")]
        for c in range(TT):
            pool_steps += [(c, n, g) for n in ("dr", "dc") for g in G2]
            pool_steps += [(c, "L", s, g) for s in LEVELS[c] for g in G2]
            if c + 1 < TT:
                pool_steps += [(c + 1, n) for n in ("gt", "gd", "gm")]
            pool_steps.append((c, "sq"))
        POOL_AT = {key: i + 1 for i, key in enumerate(pool_steps)}

        def even(v, s):
            return v.rearrange("p h (b two s) -> p h b two s", two=2, s=s)[:, :, :, 0, :]

        def odd(v, s):
            return v.rearrange("p h (b two s) -> p h b two s", two=2, s=s)[:, :, :, 1, :]

        block = ctx.enter_context(nc.Block())

        @block.sync
        def _(sp):
            def load_x(u, xs, end):
                sp.dma_start(xs[0:META, 0, :], io["meta_tokens"]).then_inc(x_in[u], 16)
                sp.dma_start(xs[META:P, 0, :], io["x_prompt"][0:P - META, :]).then_inc(x_in[u], 16)
                sp.dma_start(xs[:, 1:4, :], io["x_prompt"][P - META:4 * P - META, :]
                             .rearrange("(t p) d -> p t d", p=P)).then_inc(x_in[u], 16)
                sp.dma_start(end[0:LASTP, :], io["x_prompt"][4 * P - META:SEQ, :]).then_inc(x_in[u], 16)
                sp.dma_start(end[LASTP:LAST, :], io["x_sample"]).then_inc(x_in[u], 16)

            load_x(0, xs0, xs0[:, 4, :])
            sp.dma_start(prow[0:KT, :], io["norm_mix"]).then_inc(par_in, 16)
            sp.dma_start(prow[KT:2 * KT, :], io["norm_ffn"]).then_inc(par_in, 16)
            sp.dma_start(prow[2 * KT:3 * KT, :], io["norm_final"]).then_inc(par_in, 16)
            sp.dma_start(prow[3 * KT:3 * KT + 1, :], io["gdn_norm"]).then_inc(par_in, 16)
            sp.dma_start(crow[0:CW * NQKV, :], io["conv_w"]).then_inc(par_in, 16)
            sp.dma_start(alog[:, :], io["a_log"].to_broadcast([P, H])).then_inc(par_in, 16)
            sp.dma_start(dtb[:, :], io["dt_bias"].to_broadcast([P, H])).then_inc(par_in, 16)
            sp.dma_start(sbb[:, :], io["sb_bias"].to_broadcast([P, H])).then_inc(par_in, 16)
            sp.dma_start(ptab[:, :], io["page_table"]).then_inc(pt_in, 16)
            sp.dma_start(cst[0:3 * DB, :], io["state_conv"]).then_inc(cst_in, 16)
            sp.dma_start(io["conv_sample"][:, 0:2, :], io["state_conv3"][:, 1:3, :]).then_inc(c_out, 16)
            for p in range(T_SEG):
                w_load(sp, p)
            sp.wait_ge(pt_in, 16)

            def page(ring, landed, used, cache, b, p):
                n = v_number(b, p) if ring is vring else b * PAGES + p
                if n >= RING:
                    sp.wait_ge(used, n - RING + 1)
                row = sp.value_load(ptab[0:1, b * PAGES + p:b * PAGES + p + 1], min_val=0, max_val=NPHYS - 1)
                sp.dma_start(ring[:, n % RING:n % RING + 1, :],
                             cache[bass.ds(row, 1), :, :].rearrange("a p n -> p a n"))\
                  .then_inc(landed[n % RING], 16)

            pool_pages = [(b, p) for b in V_POOL for p in range(PAGES)]

            def pool_page(i):
                b, p = pool_pages[i]
                k, n = i // PAGES, 4 - i // PAGES
                if p >= n:
                    sp.wait_ge(p_used, i - n + 1)
                elif k == 0:
                    sp.wait_ge(t_dve, T_VN)
                else:
                    sp.wait_ge(r_out, 16 * 5)
                row = sp.value_load(ptab[0:1, b * PAGES + p:b * PAGES + p + 1], min_val=0, max_val=NPHYS - 1)
                sp.dma_start(prings[k][:, p % n:p % n + 1, :],
                             io["cache_v"][bass.ds(row, 1), :, :].rearrange("a p n -> p a n")).then_inc(p_in[k][p % n], 16)

            def store_kv():
                for name, src, s_out in (("v", vtok, (v_out, v_out)), ("k", ktok, k_out)):
                    for t in range(TT):
                        i = t if name == "v" else TT + t
                        sp.wait_ge(tok_a, i + 1)
                        sp.wait_ge(tok_d, i + 1)
                        v = src[:, t, :]
                        n = LASTP if t == 4 else P
                        sp.dma_start(io[name + "_prompt"][t * P:t * P + n, :], v[0:n, :]).then_inc(s_out[t % 2], 16)
                        if t == 4:
                            sp.dma_start(io[name + "_sample"], v[LASTP:LAST, :]).then_inc(s_out[0], 16)

            def gdn_dma():
                sp.wait_ge(ab_d, AB_G)
                sp.wait_ge(ab_a, AB_B)
                sp.dma_start(srow[0:1, 0:64],
                             gt[LASTP:LAST, 32:40]).then_inc(ab_row, 16)
                sp.dma_start(srow[0:1, 64:128],
                             bt[LASTP:LAST, 32:40]).then_inc(ab_row, 16)
                sp.wait_ge(co_c, 6)
                sp.dma_start(io["conv_prompt"], convrows(0, 3)).then_inc(c_out, 16)
                sp.dma_start(io["conv_sample"][:, 2, :], convrows(3, 11)).then_inc(c_out, 16)
                sp.wait_ge(g_dve, DVE_AT[4, "S", 1])
                sp.dma_start(io["rec_prompt"].rearrange("h k v -> k h v"), S).then_inc(r_out, 16)
                sp.wait_ge(r_out, 16)
                sp.wait_ge(g_act, ACT_AT[4, "ot", 1])
                for j in range(4):
                    sp.dma_start(st[:, 16 * j:16 * j + 16, :],
                                 io["state_rec"][2 * j:2 * j + 2].rearrange("b h k v -> k (b h) v"))\
                      .then_inc(t_in[j], 16)

            def store_states(j):
                sp.wait_ge(t_dve, T_S0 + 4 * j + 4)
                sp.dma_start(io["rec_sample"][2 * j:2 * j + 2].rearrange("b h k v -> k (b h) v"),
                             st[:, 16 * j:16 * j + 16, :]).then_inc(r_out, 16)

            fetched = 0
            for s in range(SEGS):
                for q in range(4):
                    for t in range(4) if s == 0 and q == 0 else range(2 * q + 2, 2 * q + 4):
                        w_load(sp, T_SEG + s * KT + t)
                    if s == 6 and q == 0:
                        for j in range(4):
                            store_states(j)
                    if s == 7 and q == 0:
                        sp.wait_ge(zs_done, 1)
                    for _ in range(POOL_PAGES.get((s, q), 0)):
                        pool_page(fetched)
                        fetched += 1
                    for i in range(2):
                        for b, p in (k_ahead(q, i) if s == 5 else k_pages(s, 2 * q + i, 8)):
                            page(kring, k_in, k_used, io["cache_k"], b, p)
                        for b, p in v_pages(s, 2 * q + i, 8):
                            page(vring, v_in, v_used, io["cache_v"], b, p)
                if s == 1:
                    for i in range(8):
                        for p in (2 * i, 2 * i + 1):
                            page(kring, k_in, k_used, io["cache_k"], K_ATT, p)
                            page(vring, v_in, v_used, io["cache_v"], V_ATT, p)
                        if i == 1:
                            store_kv()
                if s == 4:
                    gdn_dma()
            for p in range(T_PB + 2, T_O):
                w_load(sp, p)
            sp.wait_ge(r_out, 16 * 5)
            wait_read(sp, T_SEG + 8 * KT - 1)
            sp.wait_ge(p_used, PAGES * len(V_POOL))
            load_x(1, xs1, xs1_end)
            for p in range(T_O, len(pieces)):
                w_load(sp, p)
            for t in range(TT):
                sp.wait_ge(tok_a, 2 * TT + t + 1)
                sp.wait_ge(tok_d, 2 * TT + t + 1)
                if t == 0:
                    sp.dma_start(io["y_prompt"][0:P - META, :], ytok[META:P, 0, :]).then_inc(y_out, 16)
                elif t < 4:
                    sp.dma_start(io["y_prompt"][t * P - META:(t + 1) * P - META, :], ytok[:, t, :]).then_inc(y_out, 16)
                else:
                    sp.dma_start(io["y_prompt"][4 * P - META:SEQ, :], ytok[0:LASTP, 4, :]).then_inc(y_out, 16)
                    sp.dma_start(io["y_sample"], ytok[LASTP:LAST, 4, :]).then_inc(y_out, 16)
            sp.wait_ge(y_out, 16 * 6)
            sp.wait_ge(k_out[0], 16 * 4)
            sp.wait_ge(k_out[1], 16 * 2)
            sp.wait_ge(v_out, 16 * 6)
            sp.wait_ge(c_out, 16 * 3)
            sp.wait_ge(r_out, 16 * 5)

        @block.tensor
        def _(pe):
            mm, tr = nc.tensor.matmul, nc.tensor.transpose

            def transpose_x(u, xs, end):
                pe.wait_ge(x_in[u], 80)
                for k in range(KT):
                    if k >= 2:
                        pe.wait_ge(xt_a, KT * u + k - 1)
                        pe.wait_ge(xt_d, KT * u + k - 1)
                    b = 2 * (k % 2)
                    for t in range(4):
                        tr(ps[:, b, t * P:t * P + P], xs[:, t, k * P:k * P + P], ident[:, :])
                    tr(ps[:, b + 1, 0:LAST], end[0:LAST, k * P:k * P + P], ident[0:LAST, 0:LAST])\
                        .then_inc(xt_ready, 1)

            def square_sums(u):
                for k in range(KT):
                    pe.wait_ge(sq_ready, KT * u + k + 1)
                    sq_u = (sq, sq1, sq2)[u]
                    for i in range(2):
                        m = mm(ps[:, 4 + i, 0:HALF], ones[:, :], sq_u[:, k % 2, i * HALF:i * HALF + HALF],
                               start=(k == 0), stop=(k == KT - 1))
                    m.then_inc(sq_used, 1)

            def tile(t, src, ready=False):
                if t >= 2:
                    wait_read(pe, t - 2)
                m, k, n_k = pieces[piece_of(t)][4], 0, FT if t >= T_FO else KT
                for p in range(piece_of(t), done(t)):
                    pe.wait_ge(w_in_slot[p % RING], slot_value(p))
                    for kk in range(pieces[p][3] - pieces[p][2]):
                        if ready:
                            pe.wait_ge(xn_ready, kk + 1)
                        for i in range(2):
                            last = mm(ps[0:m, 2 * (t % 2) + i, 0:HALF], w_block(p, kk),
                                      src[:, k, i * HALF:i * HALF + HALF], start=(k == 0), stop=(k == n_k - 1))
                        k += 1
                    last.then_inc(w_used, 1)

            def tile_split(t, hi, lo, ready=None):
                if t >= 2:
                    wait_read(pe, t - 2)
                k, n_k = 0, FT if t >= T_FO else KT
                for p in range(piece_of(t), done(t)):
                    pe.wait_ge(w_lo, p - piece_of(T_O) + 1)
                    for kk in range(pieces[p][3] - pieces[p][2]):
                        w_h, w_l = (b[:, p % RING, kk * P:kk * P + P] for b in (whi, wlo))
                        if ready is not None:
                            pe.wait_ge(a_lo, ready + k + 1)
                        for w, x in ((w_h, hi), (w_h, lo), (w_l, hi)):
                            for i in range(2):
                                last = mm(ps[:, 2 * (t % 2) + i, 0:HALF], fr(w),
                                          fr(x[k][:, i * HALF:i * HALF + HALF]),
                                          start=(k == 0 and w is w_h and x is hi),
                                          stop=(k == n_k - 1 and w is w_l))
                        k += 1
                    last.then_inc(w_used, 1)

            def spread_q(b):
                if b >= 1:
                    pe.wait_ge(qb_c, b)
                for i in range(2):
                    m = mm(ps[:, 6 + i, :], sel[:, b, :], qrow[:, 512 * i:512 * i + 512], start=True, stop=True)
                m.then_inc(qb_t, 1)

            def cumulate(b):
                pe.wait_ge(d_suf, 4 * (b + 1))
                if b >= 1:
                    pe.wait_ge(d_arg, b)
                mm(ps[:, 4, 0:P], tri_ge[:, :], dsp[:, :], start=True, stop=False)
                mm(ps[:, 4, 0:P - H], ones[:, :], dsuf[:, 1, H:P], start=False, stop=True).then_inc(d_cum, 1)

            def sum_v(b):
                pe.wait_ge(p_used if b in V_POOL else v_used, v_number(b, PAGES))
                if b >= 1:
                    pe.wait_ge(ob_s, b)
                for h in range(H):
                    m = mm(ps[:, 5, h:h + 1], vacc[:, b % 2, h * P:h * P + P], ones[:, 0:1], start=True, stop=True)
                m.then_inc(v_sum, 1)

            def to_tokens(i, src, t):
                if i >= 2:
                    pe.wait_ge(tok_a, i - 1)
                    pe.wait_ge(tok_d, i - 1)
                n = rows_of(t)
                for h in range(H):
                    if i == 2 * TT:
                        pe.wait_ge(xn_ready, KT + h + 1)
                    m = tr(ps[0:n, 2 * (i % 2) + h // 4, (h % 4) * P:(h % 4) * P + P],
                           src[:, h, t * P:t * P + n], ident[:, :])
                m.then_inc(tok_t, 1)

            def attend():
                def scores(h):
                    if h == 0:
                        pe.wait_ge(tok_a, 2 * TT)
                        pe.wait_ge(tok_d, 2 * TT)
                    else:
                        pe.wait_ge(s_z, h)
                    for kt, a, b, bank, col in SB_PIECES:
                        o = h * TOKENS + kt * P
                        m = mm(ps[:, bank, col:col + b - a], kbflat[:, o:o + P], qbT[:, h, a:b],
                               start=True, stop=True)
                    m.then_inc(s_s, 1)

                def later_sums(h):
                    pe.wait_ge(s_msp, h + 1)
                    if h >= 1:
                        pe.wait_ge(s_arg, h)
                    for kt, a, b, bank, col in SB_PIECES:
                        parts = [(tri_ge, kt, a)] + [(ones, k2, max(a, P * k2)) for k2 in range(kt + 1, TT)
                                                     if P * k2 < b]
                        for j, (lhs, k2, q) in enumerate(parts):
                            f = sb_at(k2, q)[2]
                            m = mm(ps[:, 3 + bank, col + q - a:col + b - a], lhs[:, :],
                                   sps[:, h % 2, f:f + b - q], start=(j == 0), stop=(j == len(parts) - 1))
                    m.then_inc(s_c, 1)

                def values(h):
                    pe.wait_ge(s_w, h + 1)
                    if h >= 1:
                        pe.wait_ge(s_o, h)
                    else:
                        pe.wait_ge(qb_c, 3)
                    for bank, a, b in ((6, 0, 512), (7, 512, LP)):
                        ks = [k for k in range(TT) if P * k < b]
                        for k in ks:
                            q, n = max(a, P * k), chunk(k)
                            f = sb_at(k, q)[2]
                            m = mm(ps[:, bank, q - a:b - a], vtok[0:n, k, h * P:h * P + P],
                                   zs[h % 3][0:n, f:f + b - q], start=(k == 0), stop=(k == ks[-1]))
                    m.then_inc(s_av, 1)

                scores(0)
                scores(1)
                for h in range(H):
                    later_sums(h)
                    if h + 2 < H:
                        scores(h + 2)
                    values(h)
                pe.wait_ge(s_z, H)
                pe.wait_ge(s_arg, H)
                pe.wait_ge(s_o, H)

            def conv_rows():
                pe.wait_ge(raw_c, NQKV)
                for n in range(NQKV):
                    i = n // 4
                    if n % 4 == 0 and i >= 2:
                        pe.wait_ge(co_c, i - 1)
                    m = tr(ps[0:11, i % 2, (n % 4) * P:(n % 4) * P + P], rawt[:, n, :], ident[:, :])
                    if n % 4 == 3:
                        m.then_inc(co_t, 1)
                pe.wait_ge(co_c, 6)

            def norm_qk():
                for n in range(2 * H):
                    pe.wait_ge(n_sq, n + 1)
                    for i in range(2):
                        m = mm(ps[0:2 * H, 2 + i, 0:HALF], pick[:, 2 * H - 1 - n:4 * H - 1 - n],
                               sqg[:, n % SQB, i * HALF:i * HALF + HALF], start=(n == 0), stop=(n == 2 * H - 1))
                    mm(ps[:, 6, DB * n:DB * n + DB], ones[:, :], sqg[:, n % SQB, LP:TOKENS], start=True, stop=True)\
                        .then_inc(n_ss, 1)
                pe.wait_ge(n_act, 1)
                for t in range(TT):
                    n = rows_of(t)
                    m = tr(ps[0:n, 7, 16 * t:16 * t + 16], nrow[:, t * P:t * P + n],
                           ident[64:64 + 2 * H, 64:64 + 2 * H])
                m.then_inc(n_tt, 1)

            def decay_rows():
                for t in range(TT):
                    n = rows_of(t)
                    m = tr(ps[0:n, 4, 16 * t:16 * t + 16], abT[:, t * P:t * P + n], ident[32:48, 32:48])
                m.then_inc(ab_t, 1)

            def decays():
                pe.wait_ge(ab_p, 2)
                mm(ps[:, 5, 0:40], tri_le[:, :], gP, start=True, stop=True)
                mm(ps[:, 5, 64:104], tri_gt[:, :], gP, start=True, stop=True)
                mm(ps[:, 5, 128:168], ones[:, :], gP, start=True, stop=True)
                pe.wait_ge(ab_row, 32)
                mm(ps[:, 5, 256:384], ones[0:1, :], srow[0:1, :], start=True, stop=True).then_inc(ab_m, 1)

            def chunks():
                pe.wait_ge(ab_a, AB_END)
                pe.wait_ge(ab_d, AB_DEND)
                pe.wait_ge(n_dve, N_END)
                def part(c, which):
                    n, t0 = chunk(c), P * c
                    gm = gms[c % 2]

                    def after(eng, *key):
                        s, at_ = {"act": (g_act, ACT_AT), "dve": (g_dve, DVE_AT), "pool": (g_pool, POOL_AT)}[eng]
                        if key[0] >= 0:
                            pe.wait_ge(s, at_[key])

                    def heads(g):
                        return range(4 * g, 4 * g + 4)

                    def col(h):
                        return (h % 4) * P

                    if which == "head":
                        for g in G2:
                            after("act", c - 1, "vn", g)
                            for h in heads(g):
                                m = tr(ps[0:n, g, col(h):col(h) + P], cT[:, H + h, t0:t0 + n], ident[:, :])
                            m.then_inc(g_pe, 1)
                        for g in G2:
                            after("dve", c - 1, "o", g)
                            for h in heads(g):
                                m = tr(ps[0:n, 2 + g, col(h):col(h) + P], cT[:, 2 * H + h, t0:t0 + n], ident[:, :])
                            m.then_inc(g_pe, 1)
                        after("pool", c, "gm")
                        for g in G2:
                            after("dve", c - 1, "S", g)
                            mm(ps[0:n, 4 + g, 0:4 * n], tri_le[0:n, 0:n], gm[0:n, 4 * g:4 * g + 4, 0:n],
                               start=True, stop=True).then_inc(g_pe, 1)
                        for g in G2:
                            after("act", c - 1, "qs", g)
                            for h in heads(g):
                                m = mm(ps[0:n, 6 + g, (h % 4) * n:(h % 4) * n + n], gm[0:n, h, 0:n],
                                       tri_le[0:n, 0:n], start=True, stop=True)
                            m.then_inc(g_pe, 1)
                        for g in G2:
                            after("dve", c, "kr", g)
                            for h in heads(g):
                                m = mm(ps[0:n, g, (h % 4) * n:(h % 4) * n + n], cT[:, H + h, t0:t0 + n],
                                       cT[:, H + h, t0:t0 + n], start=True, stop=True)
                            m.then_inc(g_pe, 1)
                        for g in G2:
                            after("dve", c, "bv", g)
                            for h in heads(g):
                                m = mm(ps[0:n, 2 + g, (h % 4) * n:(h % 4) * n + n], cT[:, H + h, t0:t0 + n],
                                       cT[:, h, t0:t0 + n], start=True, stop=True)
                            m.then_inc(g_pe, 1)
                    if which == "body":
                        for g in G2:
                            after("pool", c, "L", 1, g)
                            after("act", c, "dr", g)
                            for h in heads(g):
                                m = tr(ps[0:n, 4 + g, (h % 4) * n:(h % 4) * n + n], Lm[0][0:n, h, 0:n], ident[0:n, 0:n])
                            m.then_inc(g_pe, 1)
                        for j, s in enumerate(LEVELS[c][1:]):
                            w = n // 2
                            for g in G2:
                                after("pool", c, "L", s, g)
                                if j == 0:
                                    after("dve", c, "U1", g)
                                    after("dve", c, "A", g)
                                else:
                                    after("dve", c, "U", s // 2, g)
                                for h in heads(g):
                                    m = mm(ps[0:n, g, (h % 4) * n:(h % 4) * n + n], Lm[(j + 1) % 2][0:n, h, 0:n],
                                           Um[0:n, h, 0:n], start=True, stop=True)
                                m.then_inc(g_pe, 1)
                            for g in G2:
                                after("act", c, "q1", s, g)
                                if j == 0:
                                    after("dve", c, "qk", g)
                                    after("dve", c, "T1", g)
                                else:
                                    after("dve", c, "T", s // 2, g)
                                for h in heads(g):
                                    m = mm(ps[0:n, 2 + g, (h % 4) * w:(h % 4) * w + w], Tm[0:n, h, 0:n],
                                           odd(Q1[0:n, h:h + 1, 0:n], s)[:, 0], start=True, stop=True)
                                if 2 * s < n:
                                    for h in heads(g):
                                        m = mm(ps[0:n, 2 + g, 256 + (h % 4) * w:256 + (h % 4) * w + w], Q1[0:n, h, 0:n],
                                               even(Tm[0:n, h:h + 1, 0:n], s)[:, 0], start=True, stop=True)
                                m.then_inc(g_pe, 1)
                        last = LEVELS[c][-1]
                        for g in G2:
                            if c:
                                after("dve", c - 1, "S", g)
                            else:
                                pe.wait_ge(g_dve0, 1)
                            after("dve", c, "U1", g)
                            for h in heads(g):
                                m = mm(ps[0:n, 4 + g, col(h):col(h) + P], cT[:, H + h, t0:t0 + n], S[:, h, :],
                                       start=True, stop=True)
                            m.then_inc(g_pe, 1)
                        for g in G2:
                            after("act", c, "dc", g)
                            after("act", c - 1, "ot", g)
                            for h in heads(g):
                                m = mm(ps[0:n, 6 + g, col(h):col(h) + P], cT[:, h, t0:t0 + n], S[:, h, :],
                                       start=True, stop=True)
                            m.then_inc(g_pe, 1)
                        for g in G2:
                            after("dve", c, "R", g)
                            after("dve", c, "U", last, g)
                            for h in heads(g):
                                m = mm(ps[0:n, g, col(h):col(h) + P], Um[0:n, h, 0:n], bvs[0:n, h, :],
                                       start=True, stop=True)
                            m.then_inc(g_pe, 1)
                        for g in G2:
                            after("act", c, "vn", g)
                            for h in heads(g):
                                m = mm(ps[0:n, 2 + g, col(h):col(h) + P], DC[0:n, h, 0:n], vnb[0:n, h, :],
                                       start=True, stop=True)
                            m.then_inc(g_pe, 1)
                        for g in G2:
                            for h in heads(g):
                                m = mm(ps[:, 4 + g, col(h):col(h) + P], krs[0:n, h, :], vnb[0:n, h, :],
                                       start=True, stop=True)
                            m.then_inc(g_pe, 1)
                    if which == "out":
                        after("dve", c, "on")
                        for g in G2:
                            after("act", c, "qs", g)
                            if c + 1 < TT:
                                after("act", c + 1, "dc", g)
                            for h in heads(g):
                                m = tr(ps[:, 6 + g, (h % 4) * n:(h % 4) * n + n], Q1[0:n, h, :], ident[0:n, 0:n])
                            m.then_inc(g_pe, 1)

                part(0, "head")
                for c in range(TT):
                    part(c, "body")
                    if c + 1 < TT:
                        part(c + 1, "head")
                    part(c, "out")
                pe.wait_ge(g_act, ACT_AT[4, "ot", 1])
                pe.wait_ge(g_dve, DVE_AT[4, "on"])

            def sampled_step(j):
                if j == 1:
                    pe.wait_ge(t_dve, 1)
                    pe.wait_ge(g_act, ACT_AT[4, "ot", 1])
                    for r in range(64):
                        b, h = r // H, r % H
                        if r % 16 == 0:
                            pe.wait_ge(t_in[r // 16], 16)
                        m = mm(ps[:, 4, 2 * r:2 * r + 2], st[:, r, :], cT[:, h:h + H + 1:H, LP + b],
                               start=True, stop=True)
                    m.then_inc(t_pe, 1)
                    mm(ps[:, 5, 0:64], ones[:, :], dsm[:, 0, :], start=True, stop=True).then_inc(t_pe, 1)
                if j == 2:
                    pe.wait_ge(t_dve, T_VN)
                    tr(ps[0:64, 6, 0:P], dsm[:, 3, :], ident[:, :])
                    tr(ps[0:64, 6, P:2 * P], dsm[:, 1, :], ident[:, :]).then_inc(t_pe, 1)
                    pe.wait_ge(t_dve, T_OSQ)
                    mm(ps[:, 7, 0:64], ones[:, :], dsm[:, 6, :], start=True, stop=True).then_inc(t_pe, 1)
                if j >= 4:
                    j -= 4
                    pe.wait_ge(t_act, 2)
                    pe.wait_ge(t_pool, j + 1)
                    pe.wait_ge(t_dve, T_ROWS)
                    for i in range(4):
                        if j:
                            pe.wait_ge(t_dve, T_S0 + 4 * (j - 1) + i + 1)
                        for r4 in range(4):
                            r = 4 * i + r4
                            m = mm(ps[:, 4 + i, r4 * P:r4 * P + P], ksel[:, r, :], vrow[:, :],
                                   start=True, stop=True)
                        m.then_inc(t_pe, 1)

            pe.wait_ge(const_ready, NCONST)
            transpose_x(0, xs0, xs0[:, 4, :])
            pe.wait_ge(par_in, 16 * 8)
            tr(ps[:, 6, 0:25], prow[0:25, :], ident[0:25, 0:25])
            tr(ps[:, 6, P:P + 96], crow[0:96, :], ident[0:96, 0:96]).then_inc(par_t, 1)
            square_sums(0)
            pe.wait_ge(par_c, 2)
            pe.wait_ge(cst_in, 16)
            for n in range(NQKV):
                m = tr(ps[:, 6 + n // 12, 24 * (n % 12):24 * (n % 12) + 24], cst[0:24, n * P:n * P + P],
                       ident[0:24, 0:24])
            m.then_inc(par_t, 1)
            for t in range(T_SEG):
                tile(t, xn, t == 0)
            wait_read(pe, T_SEG - 1)
            pe.wait_ge(cb_c, 2)
            for h in range(H):
                m = tr(ps[0:DB, 6 + h // 4, (h % 4) * P:(h % 4) * P + P], qbT[:, h, LP:TOKENS], ident[:, :])
            m.then_inc(qr_t, 1)
            pe.wait_ge(qr_c, 1)
            spread_q(0)
            for s in range(SEGS):
                src = oaT if s == 7 else xn
                if s == 7:
                    pe.wait_ge(z_done, KT)
                    pe.wait_ge(zs_done, 1)
                if s == 6:
                    pe.wait_ge(t_dve, T_S0 + 16)
                for j in range(KT):
                    tile(T_SEG + s * KT + j, src)
                    if s == 5:
                        sampled_step(j)
                    if (s, j) in SUM_V_AT:
                        sum_v(SUM_V_AT[s, j])
                    if (s, j) in SUMS_AT:
                        cumulate(SUMS_AT[s, j])
                    if (s, j) in SPREAD_AT:
                        spread_q(SPREAD_AT[s, j])
                if s == 1:
                    wait_read(pe, T_SEG + 2 * KT - 2)
                    wait_read(pe, T_SEG + 2 * KT - 1)
                    for t in range(TT):
                        to_tokens(t, vbT, t)
                    sum_v(0)
                    for t in range(TT):
                        to_tokens(TT + t, kbT, t)
                    pe.wait_ge(d_arg, 2)
                    pe.wait_ge(ob_s, 1)
                    attend()
                if s == 4:
                    wait_read(pe, T_SEG + 5 * KT - 2)
                    wait_read(pe, T_SEG + 5 * KT - 1)
                    pe.wait_ge(d_arg, 4)
                    decay_rows()
                    sum_v(3)
                    pe.wait_ge(qb_c, 6)
                    conv_rows()
                    pe.wait_ge(ob_s, 4)
                    norm_qk()
                    decays()
                    chunks()
            sum_v(DB - 2)
            sum_v(DB - 1)
            pe.wait_ge(ob_s, DB)
            for n in range(KT):
                tile(T_PB + n, obT)
            wait_read(pe, T_PB + 6)
            wait_read(pe, T_PB + 7)
            transpose_x(1, xs1, xs1_end)
            pe.wait_ge(xt_a, 2 * KT)
            pe.wait_ge(xt_d, 2 * KT)
            for n in range(KT):
                tile_split(T_O + n, m_hi, m_lo, None if n else 0)
            square_sums(1)
            for n in range(2 * FT):
                tile_split(T_FI + n, x_hi, x_lo, None if n else KT)
            pe.wait_ge(a_lo, 2 * KT + FT)
            for n in range(KT):
                tile_split(T_FO + n, h_hi, h_lo)
            square_sums(2)
            wait_read(pe, TILES - 2)
            wait_read(pe, TILES - 1)
            for t in range(TT):
                to_tokens(2 * TT + t, xn, t)

        @block.scalar
        def _(act):
            go = nc.scalar.activation

            def copy_x(u, dst):
                for k in range(KT):
                    act.wait_ge(xt_ready, KT * u + k + 1)
                    nc.scalar.copy(dst[:, k, 0:512], ps[:, 2 * (k % 2), :]).then_inc(xt_a, 1)

            def squares(u, src, dst, ready, value):
                for k in range(KT):
                    ready(k)
                    if KT * u + k >= 2:
                        act.wait_ge(sq_used, KT * u + k - 1)
                    go(dst[:, k % 2, :], src[:, k, :], ACT.Square).then_inc(sq_ready, 1)

            def root(u, buf):
                act.wait_ge(ms_ready, u + 1)
                go(buf, buf, ACT.Sqrt).then_inc(rt_ready, 1)

            def read_tile(t, dst, func=ACT.Copy, m=P):
                act.wait_ge(w_used, done(t))
                go(halves(dst), pair(t, m), func).then_inc(act_read, 1)

            def put_q(b):
                act.wait_ge(qb_t, b + 1)
                if b >= 2:
                    act.wait_ge(k_used, PAGES * (b - 1))
                nc.scalar.copy(qbc[:, b % 2, :].rearrange("p (a n) -> p a n", a=2), ps[:, 6:8, :]).then_inc(qb_c, 1)

            def softplus_part(b):
                act.wait_ge(dz_ready, b + 1)
                if b >= 1:
                    act.wait_ge(d_sp, b)
                go(de[:, :], dz[:, b % 3, :], ACT.Abs).then_inc(d_abs, 1)
                act.wait_ge(d_abs, b + 1)
                go(de[:, :], de[:, :], ACT.Exp, scale=-1.0).then_inc(d_exp, 1)
                act.wait_ge(d_exp, b + 1)
                go(de[:, :], de[:, :], ACT.Ln, bias=1.0).then_inc(d_ln, 1)

            def weights(b):
                act.wait_ge(d_arg, b + 1)
                if b >= 2:
                    act.wait_ge(p_used if b - 2 in V_POOL else v_used, v_number(b - 2, PAGES))
                go(dw[:, b % 2, :], dz[:, b % 3, :], ACT.Exp).then_inc(d_w, 1)

            def put_o(b):
                act.wait_ge(v_sum, b + 1)
                nc.scalar.copy(obT[:, :, LP + b], ps[:, 5, 0:H]).then_inc(ob_s, 1)

            def token_bank(i, dst, t):
                act.wait_ge(tok_t, i + 1)
                n = rows_of(t)
                nc.scalar.copy(dst[0:n, 0:512], ps[0:n, 2 * (i % 2), :]).then_inc(tok_a, 1)

            def attend():
                def first(h):
                    act.wait_ge(s_s, h + 1)
                    if h == 0:
                        act.wait_ge(tok_d, 2 * TT)
                    if h == 2:
                        act.wait_ge(v_sum, 1)
                        act.wait_ge(k_used, 2 * PAGES)
                    if h >= 3:
                        act.wait_ge(s_av, h - 2)
                    for b in range(3):
                        w = SB_WIDTH[b]
                        m = go(zs[h % 3][:, SB_FLAT[b]:SB_FLAT[b] + w], ps[:, b, 0:w], ACT.Identity,
                               bias=sbb[:, h:h + 1], scale=SCALE)
                    m.then_inc(s_z, 1)
                    act.wait_ge(s_abs, h + 1)
                    go(es, es, ACT.Exp, scale=-1.0).then_inc(s_exp, 1)
                    act.wait_ge(s_exp, h + 1)
                    go(es, es, ACT.Ln, bias=1.0).then_inc(s_ln, 1)

                first(0)
                first(1)
                for h in range(H):
                    act.wait_ge(s_marg, h + 1)
                    go(zs[h % 3], zs[h % 3], ACT.Exp).then_inc(s_w, 1)
                    if h + 2 < H:
                        first(h + 2)
                    act.wait_ge(s_av, h + 1)
                    nc.scalar.copy(obT[:, h, 0:512], ps[:, 6, :])
                    nc.scalar.copy(obT[:, h, 512:LP], ps[:, 7, 0:LP - 512]).then_inc(s_o, 1)

            def silu_conv(n):
                act.wait_ge(cv_step, CW * (n + 1))
                go(cT[:, n, 0:LP], cT[:, n, 0:LP], ACT.Silu).then_inc(cs_done, 1)

            def norm_qk():
                act.wait_ge(sc_step, 7)
                go(cT[:, :, LP:TOKENS], cT[:, :, LP:TOKENS], ACT.Silu).then_inc(cs_done, 1)
                act.wait_ge(cs_done, NQKV + 1)
                act.wait_ge(k_used, PAGES * 4)
                for n in range(2 * H):
                    if n >= SQB:
                        act.wait_ge(n_ss, n - SQB + 1)
                    go(sqg[:, n % SQB, :], cT[:, n, :], ACT.Square).then_inc(n_sq, 1)
                act.wait_ge(n_ss, 2 * H)
                nc.scalar.copy(halves(nrow), ps[0:2 * H, 2:4, 0:HALF]).then_inc(n_act, 1)

            def norm_roots():
                go(nr_s, ps[:, 6, 0:P], ACT.Sqrt, bias=epsc[:, :]).then_inc(n_act, 1)
                act.wait_ge(n_dve, N_ROWS)
                go(nr_t, nr_q, ACT.Sqrt, bias=epsc[:, :]).then_inc(n_act, 1)
                go(lnk.rearrange("p (t h) -> p t h", h=H), nr_q.rearrange("p (t n) -> p t n", t=TT)[:, :, H:2 * H],
                   ACT.Ln, bias=epsc[:, :]).then_inc(n_act, 1)

            def decays():
                act.wait_ge(par_in, 16 * 8)
                go(eal[:, 0:H], alog[:, :], ACT.Exp).then_inc(ab_a, 1)
                act.wait_ge(ab_d, AB_X)
                go(tmp2, tmp1, ACT.Abs).then_inc(ab_a, 1)
                act.wait_ge(ab_a, 2)
                go(tmp2, tmp2, ACT.Exp, scale=-1.0).then_inc(ab_a, 1)
                act.wait_ge(ab_a, 3)
                go(tmp2, tmp2, ACT.Ln, bias=1.0).then_inc(ab_a, 1)
                go(bt.rearrange("p (t h) -> p t h", h=H), ab5[:, :, H:2 * H], ACT.Sigmoid).then_inc(ab_a, 1)

            def exp_decays():
                act.wait_ge(ab_m, 1)
                go(eG, ps[:, 5, 0:40], ACT.Exp).then_inc(ab_a, 1)
                go(eR, ps[:, 5, 64:104], ACT.Exp).then_inc(ab_a, 1)
                go(eL, ps[:, 5, 128:168], ACT.Exp).then_inc(ab_a, 1)
                go(dsm[:, 8, :], ps[:, 5, 256:320], ACT.Exp).then_inc(ab_a, 1)
                nc.scalar.copy(dsm[:, 9, :], ps[:, 5, 320:384]).then_inc(ab_a, 1)

            def chunks():
                def part(c, which):
                    n, t0 = chunk(c), P * c

                    def after(eng, *key):
                        s, at_ = {"pe": (g_pe, PE_AT), "dve": (g_dve, DVE_AT), "pool": (g_pool, POOL_AT)}[eng]
                        if key[0] >= 0:
                            act.wait_ge(s, at_[key])

                    if which == "head":
                        for name, dst, bank, user in (("dr", DR, 4, "L"), ("dc", DC, 6, "o2")):
                            for g in G2:
                                if name == "dr" and c:
                                    after("pool", c - 1, "L", LEVELS[c - 1][-1], g)
                                after("pe", c, name, g)
                                go(dst[0:n, 4 * g:4 * g + 4, 0:n],
                                   ps[0:n, bank + g, 0:4 * n].rearrange("p (h j) -> p h j", h=4), ACT.Exp)\
                                    .then_inc(g_act, 1)
                    if which == "body":
                        for s in LEVELS[c][1:]:
                            for g in G2:
                                after("pe", c, "q1", s, g)
                                nc.scalar.copy(Q1[0:n, 4 * g:4 * g + 4, 0:n],
                                               ps[0:n, g, 0:4 * n].rearrange("p (h j) -> p h j", h=4)).then_inc(g_act, 1)
                        for g in G2:
                            after("pe", c, "qs", g)
                            for h in range(4 * g, 4 * g + 4):
                                i = (h % 4) * P
                                m = go(Q1[0:n, h, :], ps[0:n, 6 + g, i:i + P], ACT.Copy, scale=eG[0:n, H * c + h:H * c + h + 1])
                            m.then_inc(g_act, 1)
                        for g in G2:
                            after("pe", c, "vn", g)
                            nc.scalar.copy(vnb[0:n, 4 * g:4 * g + 4, :],
                                           ps[0:n, g, :].rearrange("p (h j) -> p h j", h=4)).then_inc(g_act, 1)
                    if which == "out":
                        after("dve", c, "ms")
                        go(onr[0:n, H:2 * H], onr[0:n, 0:H], ACT.Sqrt, bias=epsc[0:n, :]).then_inc(g_act, 1)
                        for g in G2:
                            after("pe", c, "ot", g)
                            go(oaT[:, 4 * g:4 * g + 4, t0:t0 + n],
                               ps[:, 6 + g, 0:4 * n].rearrange("p (h j) -> p h j", h=4), ACT.Copy,
                               scale=cols[:, 24:25]).then_inc(g_act, 1)

                part(0, "head")
                for c in range(TT):
                    part(c, "body")
                    if c + 1 < TT:
                        part(c + 1, "head")
                    part(c, "out")

            def sampled_root():
                act.wait_ge(t_pe, 4)
                go(dsm[:, 7, :], ps[:, 7, 0:64], ACT.Identity, scale=1.0 / P, bias=epsc[:, :]).then_inc(t_act, 1)
                act.wait_ge(t_act, 1)
                go(dsm[:, 7, :], dsm[:, 7, :], ACT.Sqrt).then_inc(t_act, 1)

            def sampled_out():
                act.wait_ge(t_dve, T_ON)
                go(oaT[:, :, LP:TOKENS].rearrange("p h b -> p b h"),
                   dsm[:, 5, :].rearrange("p (b h) -> p b h", h=H), ACT.Copy, scale=cols[:, 24:25]).then_inc(t_act, 1)

            act.wait_ge(const_ready, NCONST)
            act.wait_ge(eps_ready, 1)
            copy_x(0, hT0)

            def x_there(k):
                act.wait_ge(xt_a, k + 1)
                act.wait_ge(xt_d, k + 1)
            squares(0, hT0, sq, x_there, 0)
            root(0, rstd)
            read_tile(T_AB, abT[:, :], m=2 * H)
            for n in range(KT):
                read_tile(T_Q + n, qbT[:, n, :])
            put_q(0)
            for s in range(SEGS):
                for j in range(KT):
                    t, n = T_SEG + s * KT + j, (s - 2) * KT + j
                    if (s, j) in SOFT_AT:
                        softplus_part(SOFT_AT[s, j])
                    if (s, j) in WEIGHT_AT:
                        weights(WEIGHT_AT[s, j])
                    if s in (0, 1):
                        read_tile(t, (kbT, vbT)[s][:, j, :])
                    elif s in (2, 3, 4):
                        if n == 0:
                            act.wait_ge(v_out, 16 * 6)
                            act.wait_ge(up_zero, 1)
                        if n >= 2:
                            act.wait_ge(cv_step, CW * (n - 1))
                            act.wait_ge(raw_c, n - 1)
                        read_tile(t, upad[:, n % 2, CW - 1:CW - 1 + TOKENS])
                        if n % 2 and n >= 3:
                            silu_conv(n - 3)
                            silu_conv(n - 2)
                    elif s == 5:
                        if j >= 2:
                            act.wait_ge(z_done, j - 1)
                        act.wait_ge(w_used, done(t))
                        go(halves(ztmp[:, j % 2, :]), pair(t), ACT.Silu).then_inc(act_read, 1)
                    elif s in (6, 8):
                        read_tile(t, (sgA if s == 6 else sgB)[:, j, :], ACT.Sigmoid)
                    if s == 5 and j == 3:
                        sampled_root()
                    if s == 5 and j == 5:
                        sampled_out()
                    if (s, j) in PUT_O_AT:
                        put_o(PUT_O_AT[s, j])
                    if (s, j) in PUT_Q_AT:
                        put_q(PUT_Q_AT[s, j])
                if s == 1:
                    for t in range(TT):
                        token_bank(t, vtok[:, t, :], t)
                    put_o(0)
                    for t in range(TT):
                        token_bank(TT + t, ktok[:, t, :], t)
                    attend()
                if s == 4:
                    silu_conv(NQKV - 2)
                    silu_conv(NQKV - 1)
                    decays()
                    put_o(3)
                    norm_qk()
                    exp_decays()
                    norm_roots()
                    chunks()
            put_o(DB - 2)
            put_o(DB - 1)
            act.wait_ge(v_used, PAGES * len(V_DVE))
            act.wait_ge(k_used, PAGES * DB)
            for n in range(KT):
                act_hi(act, n, m_hi[n], m_full[n])
                if n in (5, 6):
                    split_hi(act, T_O + n - 5)
            copy_x(1, hT)

            def h_there(base):
                def wait(k):
                    act.wait_ge(dve_read, base + k + 1)
                return wait
            for k in range(KT):
                split_hi(act, T_O + k + 2)
            squares(1, hT, sq1, h_there(READ_COUNT[T_O] - 1), 0)
            root(1, rstd1)
            for k in range(KT):
                act_hi(act, KT + k, x_hi[k], x_full[k])
            for n in range(FT + 1):
                if n < FT:
                    if n >= 2:
                        act.wait_ge(dve_read, READ_COUNT[T_FI + 2 * (n - 2) + 1])
                    split_hi(act, T_FI + 2 * n + 2)
                    read_tile(T_FI + 2 * n, gtmp[:, n % 2, :], ACT.Silu)
                    if n < FT - 1:
                        split_hi(act, T_FI + 2 * n + 3)
                if n >= 1:
                    act_hi(act, 2 * KT + n - 1, h_hi[n - 1], h_full[n - 1])
            split_hi(act, T_FO + 1)
            for n in range(KT - 2):
                split_hi(act, T_FO + n + 2)
            squares(2, hT, sq2, h_there(READ_COUNT[T_FO] - 1), 0)
            root(2, rstd2)
            for t in range(TT):
                token_bank(2 * TT + t, ytok[:, t, :], t)

        @block.vector
        def _(dve):
            v = nc.vector

            def copy_x(u, dst):
                for k in range(KT):
                    dve.wait_ge(xt_ready, KT * u + k + 1)
                    v.tensor_copy(dst[:, k, 512:TOKENS], ps[:, 2 * (k % 2) + 1, 0:LAST]).then_inc(xt_d, 1)

            def normalise(u, src, w0, rs):
                dve.wait_ge(sq_used, KT * (u + 1))
                v.tensor_scalar(halves(rs), ps[:, 4:6, 0:HALF], 1.0 / D, EPS, ALU.mult, ALU.add).then_inc(ms_ready, 1)
                dve.wait_ge(rt_ready, u + 1)
                v.reciprocal(rs, rs).then_inc(rc_ready, 1)
                dve.wait_ge(rc_ready, u + 1)
                for k in range(KT):
                    dst, full = (x_full[k], a_full) if u == 1 else (xn[:, k, :], xn_ready)
                    v.scalar_tensor_tensor(dst, src[:, k, :], cols[:, w0 + k:w0 + k + 1], rs,
                                           ALU.mult, ALU.mult).then_inc(full, 1)
                    if u == 1 and k >= 1:
                        act_lo(dve, KT + k - 1, x_hi[k - 1], x_full[k - 1], x_lo[k - 1])
                if u == 1:
                    act_lo(dve, 2 * KT - 1, x_hi[KT - 1], x_full[KT - 1], x_lo[KT - 1])

            def k_page(b, p):
                n = b * PAGES + p
                dve.wait_ge(k_in[n % RING], slot_value(n))
                if p == 0:
                    dve.wait_ge(qb_c, b + 1)
                    if b >= 3:
                        dve.wait_ge(d_w, b - 2)
                for h in range(H):
                    kh = kring[:, n % RING, h * P:h * P + P]
                    m = v.tensor_tensor_reduce(kh, kh, qbc[:, b % 2, h * P:h * P + P], 1.0, 0.0, ALU.mult,
                                               ALU.add, dz[:, b % 3, p * H + h:p * H + h + 1])
                m.then_inc(k_used, 1)
                if p == PAGES - 1:
                    scale_scores(b)

            def scale_scores(b):
                dve.wait_ge(k_used, PAGES * (b + 1))
                z = dz[:, b % 3, :].rearrange("p (a h) -> p a h", h=H)
                v.scalar_tensor_tensor(z, z, SCALE, sbb[:, :].unsqueeze(1).to_broadcast([P, PAGES, H]),
                                       ALU.mult, ALU.add).then_inc(dz_ready, 1)

            def chain_sp(b):
                dve.wait_ge(d_ln, b + 1)
                if b >= 1:
                    dve.wait_ge(d_cum, b)
                v.scalar_tensor_tensor(dsp[:, :], dz[:, b % 3, :], 0.0, de[:, :], ALU.max, ALU.add)\
                    .then_inc(d_sp, 1)
                dve.wait_ge(d_sp, b + 1)
                src = dsp[:, :]
                for i, step in enumerate((H, 2 * H, 4 * H, 8 * H)):
                    dst = dsuf[:, i % 2, :]
                    v.tensor_copy(dst[:, P - step:P], src[:, P - step:P])
                    v.tensor_tensor(dst[:, 0:P - step], src[:, 0:P - step], src[:, step:P], ALU.add).then_inc(d_suf, 1)
                    dve.wait_ge(d_suf, 4 * b + i + 1)
                    src = dst

            def chain_arg(b):
                dve.wait_ge(d_cum, b + 1)
                v.tensor_tensor(dz[:, b % 3, :], dz[:, b % 3, :], ps[:, 4, 0:P], ALU.subtract).then_inc(d_arg, 1)

            def v_page(b, p):
                n = v_number(b, p)
                dve.wait_ge(v_in[n % RING], slot_value(n))
                if p == 0:
                    dve.wait_ge(d_w, b + 1)
                    if b >= 2:
                        dve.wait_ge(v_sum, b - 1)
                else:
                    dve.wait_ge(v_used, n)
                for h in range(H):
                    vh, a = vring[:, n % RING, h * P:h * P + P], vacc[:, b % 2, h * P:h * P + P]
                    w = dw[:, b % 2, p * H + h:p * H + h + 1]
                    if p == 0:
                        m = v.tensor_scalar(a, vh, w, None, ALU.mult)
                    else:
                        m = v.scalar_tensor_tensor(a, vh, w, a, ALU.mult, ALU.add)
                m.then_inc(v_used, 1)

            def token_bank(i, dst, t):
                dve.wait_ge(tok_t, i + 1)
                n = rows_of(t)
                v.tensor_copy(dst[0:n, 512:D], ps[0:n, 2 * (i % 2) + 1, :]).then_inc(tok_d, 1)

            def attend():
                def magnitude(h):
                    dve.wait_ge(s_z, h + 1)
                    if h == 0:
                        dve.wait_ge(k_out[0], 16 * 4)
                        dve.wait_ge(k_out[1], 16 * 2)
                    if h >= 1:
                        dve.wait_ge(s_sp, h)
                    v.scalar_tensor_tensor(es, zs[h % 3], -1.0, zs[h % 3], ALU.mult, ALU.max).then_inc(s_abs, 1)

                def softplus(h):
                    dve.wait_ge(s_ln, h + 1)
                    if h >= 2:
                        dve.wait_ge(s_c, h - 1)
                    v.scalar_tensor_tensor(sps[:, h % 2, :], zs[h % 3], 0.0, es, ALU.max, ALU.add)\
                        .then_inc(s_sp, 1)

                for h in (0, 1):
                    magnitude(h)
                    softplus(h)
                for h in range(H):
                    dve.wait_ge(s_c, h + 1)
                    for b in range(3):
                        w = SB_WIDTH[b]
                        zb = zs[h % 3][:, SB_FLAT[b]:SB_FLAT[b] + w]
                        m = v.tensor_tensor(zb, zb, ps[:, 3 + b, 0:w], ALU.subtract)
                    m.then_inc(s_arg, 1)
                    for p in (2 * h, 2 * h + 1):
                        k_page(K_ATT, p)
                    if h + 2 < H:
                        magnitude(h + 2)
                    for p in (2 * h, 2 * h + 1):
                        v_page(V_ATT, p)
                    if h + 2 < H:
                        softplus(h + 2)

            def conv(n):
                y = cT[:, n, 0:LP]
                dve.wait_ge(act_read, READ_COUNT[T_SEG + 2 * KT + n])
                for i in range(CW):
                    u, w = upad[:, n % 2, i:i + LP], convw[:, i, n:n + 1]
                    if i == 0:
                        v.tensor_scalar(y, u, w, None, ALU.mult).then_inc(cv_step, 1)
                    else:
                        dve.wait_ge(cv_step, CW * n + i)
                        v.scalar_tensor_tensor(y, u, w, y, ALU.mult, ALU.add).then_inc(cv_step, 1)

            def conv_sampled():
                y = cT[:, :, LP:TOKENS]
                dve.wait_ge(raw_c, NQKV)

                def w(i):
                    return per_head(convw[:, i, :], DB)
                v.tensor_tensor(y, rawt[:, :, 3:11], w(CW - 1), ALU.mult).then_inc(sc_step, 1)
                cb = cbuf[:, :, :].rearrange("p n (b i) -> p n b i", i=3)
                for i in range(3):
                    dve.wait_ge(sc_step, 1 + 2 * i)
                    v.tensor_tensor(cvt, cb[:, :, :, i], w(i), ALU.mult).then_inc(sc_step, 1)
                    dve.wait_ge(sc_step, 2 + 2 * i)
                    v.tensor_tensor(y, y, cvt, ALU.add).then_inc(sc_step, 1)

            def norm_qk():
                dve.wait_ge(v_used, PAGES * 4)
                v.memset(nr_q, 0.0).then_inc(n_dve, 1)
                dve.wait_ge(n_tt, 1)
                dve.wait_ge(n_dve, 1)
                v.tensor_copy(nr_q[:, 0:64], ps[:, 7, 0:64]).then_inc(n_dve, 1)
                v.tensor_copy(nr_q[0:LAST, 64:80], ps[0:LAST, 7, 64:80]).then_inc(n_dve, 1)
                dve.wait_ge(n_act, 2)
                v.reciprocal(nr_s, nr_s).then_inc(n_dve, 1)
                dve.wait_ge(ab_a, AB_END)
                dve.wait_ge(n_act, 3)
                v.reciprocal(nr_r, nr_t).then_inc(n_dve, 1)
                dve.wait_ge(n_dve, 5)
                rr = nr_r.rearrange("p (t n) -> p t n", t=TT)
                rs8 = nr_s.rearrange("p (n b) -> p n b", b=DB)
                v.scalar_tensor_tensor(cT[:, 0:H, LP:TOKENS], cT[:, 0:H, LP:TOKENS], SCALE, rs8[:, 0:H, :],
                                       ALU.mult, ALU.mult).then_inc(n_dve, 1)
                v.tensor_tensor(cT[:, H:2 * H, LP:TOKENS], cT[:, H:2 * H, LP:TOKENS], rs8[:, H:2 * H, :], ALU.mult)\
                    .then_inc(n_dve, 1)
                v.tensor_scalar(t5(rq), rr[:, :, 0:H], SCALE, None, ALU.mult).then_inc(n_dve, 1)
                v.tensor_tensor(t5(eR), t5(eR), rr[:, :, H:2 * H], ALU.mult).then_inc(n_dve, 1)
                v.tensor_tensor(t5(btk), t5(bt), rr[:, :, H:2 * H], ALU.mult).then_inc(n_dve, 1)
                dve.wait_ge(n_dve, 10)
                v.scalar_tensor_tensor(rq2, rq, 1.0 / P, rq, ALU.mult, ALU.mult).then_inc(n_dve, 1)
                v.scalar_tensor_tensor(nbG, btk, -1.0, eG, ALU.mult, ALU.mult).then_inc(n_dve, 1)
                dve.wait_ge(n_act, 4)
                v.tensor_scalar(lnk, lnk, -0.5, None, ALU.mult).then_inc(n_dve, 1)
                dve.wait_ge(n_dve, N_END)

            def t5(x):
                return x.rearrange("p (t h) -> p t h", h=H)

            def decays():
                v.memset(ab5[:, :, :], 0.0).then_inc(ab_d, 1)
                dve.wait_ge(ab_d, 1)
                dve.wait_ge(ab_t, 1)
                v.tensor_copy(ab5[:, 0:4, :], ps[:, 4, 0:64].rearrange("p (t h) -> p t h", t=4)).then_inc(ab_d, 1)
                v.tensor_copy(ab5[0:LAST, 4, :], ps[0:LAST, 4, 64:80]).then_inc(ab_d, 1)
                dve.wait_ge(ab_d, 3)
                v.tensor_tensor(t5(tmp1), ab5[:, :, 0:H], dtb[:, :].unsqueeze(1).to_broadcast([P, TT, H]), ALU.add)\
                    .then_inc(ab_d, 1)

            def log_decays():
                dve.wait_ge(ab_a, 4)
                dve.wait_ge(ab_d, 4)
                v.scalar_tensor_tensor(tmp1, tmp1, 0.0, tmp2, ALU.max, ALU.add).then_inc(ab_d, 1)
                dve.wait_ge(ab_d, 5)
                v.scalar_tensor_tensor(t5(gt), t5(tmp1), -1.0, eal[:, 0:H].unsqueeze(1).to_broadcast([P, TT, H]),
                                       ALU.mult, ALU.mult).then_inc(ab_d, 1)

            def chunks():
                v.memset(S, 0.0).then_inc(g_dve0, 1)
                def part(c, which):
                    n = chunk(c)

                    def after(eng, *key):
                        s, at_ = {"act": (g_act, ACT_AT), "pe": (g_pe, PE_AT), "pool": (g_pool, POOL_AT),
                                  "dve": (g_dve, DVE_AT)}[eng]
                        if key[0] >= 0:
                            dve.wait_ge(s, at_[key])

                    def hs(g):
                        return slice(4 * g, 4 * g + 4)

                    def bank(i, w, m=n):
                        return ps[0:m, i, 0:4 * w].rearrange("p (h j) -> p h j", h=4)

                    def one(x, h):
                        return x[0:n, H * c + h:H * c + h + 1]

                    if which == "head":
                        for g in G2:
                            after("pe", c - 1, "kv", g)
                            after("pe", c, "tk", g)
                            v.tensor_tensor(krs[0:n, hs(g), :], bank(g, P),
                                            per_head(eR[0:n, H * c + 4 * g:H * c + 4 * g + 4], P), ALU.mult).then_inc(g_dve, 1)
                        for g in G2:
                            after("pe", c, "tv", g)
                            v.tensor_tensor(bvs[0:n, hs(g), :], bank(2 + g, P),
                                            per_head(bt[0:n, H * c + 4 * g:H * c + 4 * g + 4], P), ALU.mult).then_inc(g_dve, 1)
                    if which == "body":
                        for g in G2:
                            after("pe", c, "kk", g)
                            after("pool", c, "dr", g)
                            for h in range(4 * g, 4 * g + 4):
                                i = (h % 4) * n
                                m = v.scalar_tensor_tensor(DR[0:n, h, 0:n], ps[0:n, g, i:i + n], one(btk, h), DR[0:n, h, 0:n],
                                                           ALU.mult, ALU.mult)
                            m.then_inc(g_dve, 1)
                        for g in G2:
                            after("pe", c, "kq", g)
                            after("pool", c, "dc", g)
                            v.tensor_tensor(DC[0:n, hs(g), 0:n], bank(2 + g, n), DC[0:n, hs(g), 0:n], ALU.mult).then_inc(g_dve, 1)
                        idb = ident[0:n, 0:n].unsqueeze(1).to_broadcast([n, 4, n])
                        for g in G2:
                            after("pe", c, "lt", g)
                            v.tensor_tensor(Um[0:n, hs(g), 0:n], idb, bank(4 + g, n), ALU.subtract).then_inc(g_dve, 1)
                            v.tensor_tensor(Tm[0:n, hs(g), 0:n], idb, Lm[0][0:n, hs(g), 0:n], ALU.subtract).then_inc(g_dve, 1)
                        for s in LEVELS[c][1:]:
                            w = n // 2
                            for g in G2:
                                after("pe", c, "up", s, g)
                                ue, te = odd(Um[0:n, hs(g), 0:n], s), even(Tm[0:n, hs(g), 0:n], s)

                                def upd(o):
                                    return ps[0:n, 2 + g, o:o + 4 * w].rearrange("p (h b s) -> p h b s", h=4, s=s)
                                v.tensor_tensor(ue, ue, upd(0), ALU.subtract).then_inc(g_dve, 1)
                                if 2 * s < n:
                                    v.tensor_tensor(te, te, upd(256), ALU.subtract).then_inc(g_dve, 1)
                        for g in G2:
                            after("pe", c, "ks", g)
                            for h in range(4 * g, 4 * g + 4):
                                i = (h % 4) * P
                                m = v.scalar_tensor_tensor(bvs[0:n, h, :], ps[0:n, 4 + g, i:i + P], one(nbG, h), bvs[0:n, h, :],
                                                           ALU.mult, ALU.add)
                            m.then_inc(g_dve, 1)
                        for g in G2:
                            after("pe", c, "o2", g)
                            after("act", c, "qs", g)
                            v.tensor_tensor(Q1[0:n, hs(g), :], Q1[0:n, hs(g), :], bank(2 + g, P), ALU.add).then_inc(g_dve, 1)
                        for g in G2:
                            after("pe", c, "kv", g)
                            for h in range(4 * g, 4 * g + 4):
                                i = (h % 4) * P
                                m = v.scalar_tensor_tensor(S[:, h, :], S[:, h, :], eL[:, H * c + h:H * c + h + 1],
                                                           ps[:, 4 + g, i:i + P], ALU.mult, ALU.add)
                            m.then_inc(g_dve, 1)
                        after("pool", c, "sq")
                        v.tensor_reduce(onr[0:n, 0:H], Lm[0][0:n, :, :], AX.X, ALU.add).then_inc(g_dve, 1)
                        after("dve", c, "ss")
                        v.tensor_tensor(onr[0:n, 0:H], onr[0:n, 0:H], rq2[0:n, H * c:H * c + H], ALU.mult).then_inc(g_dve, 1)
                    if which == "out":
                        after("act", c, "rt")
                        v.reciprocal(onr[0:n, 2 * H:3 * H], onr[0:n, H:2 * H]).then_inc(g_dve, 1)
                        after("dve", c, "rc")
                        v.tensor_tensor(onr[0:n, 2 * H:3 * H], onr[0:n, 2 * H:3 * H], rq[0:n, H * c:H * c + H], ALU.mult)\
                            .then_inc(g_dve, 1)
                        after("dve", c, "rq")
                        v.tensor_tensor(Q1[0:n, :, :], Q1[0:n, :, :], per_head(onr[0:n, 2 * H:3 * H], P), ALU.mult)\
                            .then_inc(g_dve, 1)

                part(0, "head")
                for c in range(TT):
                    part(c, "body")
                    if c + 1 < TT:
                        part(c + 1, "head")
                    part(c, "out")

            def sampled_delta():
                count = [0]

                def step(ins):
                    ins.then_inc(t_dve, 1)
                    count[0] += 1
                    dve.wait_ge(t_dve, count[0])

                def bh(x):
                    return x.rearrange("p (b h) -> p b h", h=H)

                def of(i):
                    return cT[:, H * i:H * i + H, LP:TOKENS].rearrange("p h b -> p b h")
                qk, kk, t1, vn, t2, o, osq, rs, eg, be = (dsm[:, i, :] for i in range(10))
                step(v.tensor_tensor(bh(qk), of(0), of(1), ALU.mult))
                step(v.tensor_copy(bh(kk), of(1)))
                dve.wait_ge(t_pe, 2)
                sqk = ps[:, 4, 0:P].rearrange("p (r two) -> p r two", two=2)
                step(v.tensor_tensor(t1, sqk[:, :, 1], eg, ALU.mult))
                step(v.tensor_tensor(bh(t1), of(2), bh(t1), ALU.subtract))
                step(v.tensor_tensor(vn, t1, be, ALU.mult))
                step(v.tensor_tensor(t2, sqk[:, :, 0], eg, ALU.mult))
                step(v.tensor_tensor(o, vn, ps[:, 5, 0:64], ALU.mult))
                step(v.tensor_tensor(o, o, t2, ALU.add))
                step(v.tensor_tensor(osq, o, o, ALU.mult))
                dve.wait_ge(t_pe, 3)
                step(v.tensor_copy(vrow[:, :], ps[0:64, 6, 0:P]))
                step(v.tensor_copy(krow[:, :], ps[0:64, 6, P:2 * P]))
                dve.wait_ge(t_act, 2)
                step(v.reciprocal(rs, rs))
                step(v.tensor_tensor(o, o, rs, ALU.mult))
                for j in range(4):
                    for i in range(4):
                        dve.wait_ge(t_pe, 5 + 4 * j + i)
                        for r4 in range(4):
                            r = 16 * j + 4 * i + r4
                            m = v.scalar_tensor_tensor(st[:, r, :], st[:, r, :], eg[:, r:r + 1],
                                                       ps[:, 4 + i, r4 * P:r4 * P + P], ALU.mult, ALU.add)
                        m.then_inc(t_dve, 1)
                    for b, p in k_pages(5, j, 4):
                        k_page(b, p)

            v.memset(epsc[:, :], EPS).then_inc(eps_ready, 1)
            v.memset(pick[:, :], 0.0).then_inc(pick_ready, 1)
            dve.wait_ge(pick_ready, 1)
            v.memset(pick[:, 2 * H - 1:2 * H], 1.0).then_inc(pick_ready, 1)
            copy_x(0, hT0)
            dve.wait_ge(par_t, 1)
            v.tensor_copy(cols[:, 0:25], ps[:, 6, 0:25]).then_inc(par_c, 1)
            v.tensor_copy(convw[:, :, :], ps[:, 6, P:P + 96].rearrange("p (i n) -> p i n", i=CW)).then_inc(par_c, 1)
            dve.wait_ge(par_c, 2)
            dve.wait_ge(xt_a, KT)
            dve.wait_ge(xt_d, KT)
            normalise(0, hT0, 0, rstd)
            dve.wait_ge(par_t, 2)
            for i in range(2):
                v.tensor_copy(cbuf[:, 12 * i:12 * i + 12, :],
                              ps[:, 6 + i, 0:288].rearrange("p (n c) -> p n c", n=12)).then_inc(cb_c, 1)
            dve.wait_ge(xn_ready, KT)
            v.memset(R[:, 2 * A8:2 * A8 + P], 0.0).then_inc(kpad, 1)
            dve.wait_ge(qr_t, 1)
            v.tensor_copy(qrow[:, :].rearrange("p (a n) -> p a n", a=2), ps[0:DB, 6:8, :]).then_inc(qr_c, 1)
            for s in range(SEGS):
                if s == 2:
                    v.memset(upad[:, :, 0:CW - 1], 0.0).then_inc(up_zero, 1)
                for q in range(4):
                    if (s, q) in SP_AT:
                        chain_sp(SP_AT[s, q])
                    if s in (2, 3, 4) and (s - 2) * KT + 2 * q >= 2:
                        conv((s - 2) * KT + 2 * q - 2)
                        conv((s - 2) * KT + 2 * q - 1)
                    if s == 7:
                        for j in (2 * q, 2 * q + 1):
                            dve.wait_ge(act_read, READ_COUNT[T_SEG + 6 * KT + j])
                            dve.wait_ge(w_used, done(T_SEG + s * KT + j))
                            v.tensor_tensor(halves(mT[:, j, :]), halves(sgA[:, j, :]), pair(T_SEG + s * KT + j), ALU.mult)\
                                .then_inc(dve_read, 1)
                            if j == 2:
                                chain_sp(6)
                            if j == 4:
                                chain_arg(6)
                            for b, p in k_pages(s, j, 8):
                                k_page(b, p)
                            for b, p in v_pages(s, j, 8):
                                v_page(b, p)
                        continue
                    if s == 5:
                        continue
                    for b, p in k_pages(s, q, 4):
                        k_page(b, p)
                    if (s, q) in ARG_AT:
                        chain_arg(ARG_AT[s, q])
                    for b, p in v_pages(s, q, 4):
                        v_page(b, p)
                if s == 1:
                    for t in range(TT):
                        token_bank(t, vtok[:, t, :], t)
                    for t in range(TT):
                        token_bank(TT + t, ktok[:, t, :], t)
                    attend()
                    dve.wait_ge(s_av, H)
                    dve.wait_ge(v_out, 16 * 6)
                if s == 4:
                    conv(NQKV - 2)
                    conv(NQKV - 1)
                    decays()
                    conv_sampled()
                    for i in range(6):
                        dve.wait_ge(co_t, i + 1)
                        v.tensor_copy(convrow_sb[0:11, i * 512:i * 512 + 512], ps[0:11, i % 2, :]).then_inc(co_c, 1)
                    log_decays()
                    norm_qk()
                    chunks()
                    sampled_delta()
            for n in range(KT):
                dve.wait_ge(act_read, READ_COUNT[T_SEG + 8 * KT + n])
                dve.wait_ge(w_used, done(T_PB + n))
                v.tensor_tensor(halves(sgB[:, n, :]), halves(sgB[:, n, :]), pair(T_PB + n), ALU.mult).then_inc(dve_read, 1)
                dve.wait_ge(dve_read, READ_COUNT[T_PB + n])
                v.tensor_tensor(mT[:, n, :], mT[:, n, :], sgB[:, n, :], ALU.add).then_inc(a_full, 1)
                if n >= 1:
                    act_lo(dve, n - 1, m_hi[n - 1], m_full[n - 1], m_lo[n - 1])
                if n == KT - 1:
                    split_lo(dve, T_O)
            act_lo(dve, KT - 1, m_hi[KT - 1], m_full[KT - 1], m_lo[KT - 1])
            split_lo(dve, T_O + 1)
            copy_x(1, hT)
            dve.wait_ge(xt_a, 2 * KT)
            dve.wait_ge(xt_d, 2 * KT)
            for n in range(KT):
                split_lo(dve, T_O + n + 2)
                dve.wait_ge(w_used, done(T_O + n))
                v.tensor_tensor(halves(hT[:, n, :]), halves(hT[:, n, :]), pair(T_O + n), ALU.add).then_inc(dve_read, 1)
            dve.wait_ge(dve_read, READ_COUNT[T_O + KT - 1])
            normalise(1, hT, KT, rstd1)
            for n in range(FT + 1):
                if n < FT:
                    split_lo(dve, T_FI + 2 * n + 2)
                    if n < FT - 1:
                        split_lo(dve, T_FI + 2 * n + 3)
                if n >= 1:
                    act_lo(dve, 2 * KT + n - 1, h_hi[n - 1], h_full[n - 1], h_lo[n - 1])
                if n < FT:
                    dve.wait_ge(act_read, READ_COUNT[T_FI + 2 * n])
                    dve.wait_ge(w_used, done(T_FI + 2 * n + 1))
                    v.tensor_tensor(halves(h_full[n]), halves(gtmp[:, n % 2, :]), pair(T_FI + 2 * n + 1), ALU.mult)\
                        .then_inc(dve_read, 1)
            split_lo(dve, T_FO + 1)
            for n in range(KT):
                dve.wait_ge(w_used, done(T_FO + n))
                v.tensor_tensor(halves(hT[:, n, :]), halves(hT[:, n, :]), pair(T_FO + n), ALU.add).then_inc(dve_read, 1)
                if n + 2 < KT:
                    split_lo(dve, T_FO + n + 2)
            dve.wait_ge(dve_read, READ_COUNT[T_FO + KT - 1])
            normalise(2, hT, 2 * KT, rstd2)
            for t in range(TT):
                token_bank(2 * TT + t, ytok[:, t, :], t)

        @block.gpsimd
        def _(pool):
            g_ = nc.gpsimd

            def keep(out, in_, pattern, base, cm, op=ALU.is_ge, fill=0.0):
                return g_.affine_select(out=out, in_=in_, pattern=pattern, compare_op=op, fill=fill,
                                        base=base, channel_multiplier=cm)
            for m in (ident,):
                g_.memset(m[:, :], 0.0).then_inc(const_step, 1)
            for m in (ones, tri_ge, tri_le, tri_gt):
                g_.memset(m[:, :], 1.0).then_inc(const_step, 1)
            g_.memset(lvl[:, :, :], 1.0).then_inc(const_step, 1)
            g_.memset(sel[:, :, :], 1.0).then_inc(const_step, 1)
            pool.wait_ge(const_step, 7)
            keep(ident[:, :], ident[:, :], [[-1, P]], 0, 1, ALU.not_equal, 1.0).then_inc(const_ready, 1)
            keep(tri_ge[:, :], tri_ge[:, :], [[-1, P]], 0, 1).then_inc(const_ready, 1)
            keep(tri_le[:, :], tri_le[:, :], [[1, P]], 0, -1).then_inc(const_ready, 1)
            keep(tri_gt[:, :], tri_gt[:, :], [[-1, P]], 0, 1, ALU.is_gt).then_inc(const_ready, 1)
            keep(sel[:, :, :], sel[:, :, :], [[-1, DB], [0, P]], 0, 1, ALU.is_equal).then_inc(const_ready, 1)
            for i in range(7):
                s = 1 << i
                v = lvl[:, i, :].rearrange("p (b two s) -> p b two s", two=2, s=s)
                nb = P // (2 * s)
                g_.memset(v[:, :, 1, :], 0.0).then_inc(const_step, 1)
                keep(v[:, :, 0, :], v[:, :, 0, :], [[-2 * s, nb], [0, s]], -s, 1).then_inc(const_step, 1)
            pool.wait_ge(const_step, 7 + 14)
            for i in range(7):
                s = 1 << i
                v = lvl[:, i, :].rearrange("p (b two s) -> p b two s", two=2, s=s)
                keep(v[:, :, 0, :], v[:, :, 0, :], [[2 * s, P // (2 * s)], [0, s]], 2 * s - 1, -1).then_inc(const_ready, 1)

            def causal(buf, fill, sig):
                for kt in range(TT):
                    n = chunk(kt)
                    f = sb_at(kt, P * kt)[2]
                    m = keep(buf[:, f:f + n], buf[:, f:f + n], [[1, n]], 0, -1, ALU.is_gt, fill)
                m.then_inc(sig, 1)

            for h in range(-2, H):
                if h >= 0:
                    pool.wait_ge(s_arg, h + 1)
                    causal(zs[h % 3], NEG, s_marg)
                if h + 2 < H:
                    pool.wait_ge(s_sp, h + 3)
                    causal(sps[:, h % 2, :], 0.0, s_msp)
            for n in range(NQKV):
                pool.wait_ge(act_read, READ_COUNT[T_SEG + 2 * KT + n])
                g_.tensor_copy(rawt[:, n, :], upad[:, n % 2, CW - 1 + LP - 3:CW - 1 + TOKENS]).then_inc(raw_c, 1)
            pool.wait_ge(ab_d, AB_G)
            g_.tensor_copy(gP[:, 0:32], gt[:, 0:32]).then_inc(ab_p, 1)
            keep(gP[:, 32:40], gt[:, 32:40], [[0, H]], LASTP - 1, -1).then_inc(ab_p, 1)
            pool.wait_ge(ab_p, 2)

            def decay_columns(c):
                n, gm = chunk(c), gms[c % 2]
                g_.tensor_tensor(gm[0:n, :, 0:n], tri_gt[0:n, 0:n].unsqueeze(1).to_broadcast([n, H, n]),
                                 per_head(gP[0:n, H * c:H * c + H], n), ALU.mult).then_inc(g_pool, 1)
                g_.tensor_tensor(dg[0:n, :, 0:n], ident[0:n, 0:n].unsqueeze(1).to_broadcast([n, H, n]),
                                 per_head(lnk[0:n, H * c:H * c + H], n), ALU.mult).then_inc(g_pool, 1)
                pool.wait_ge(g_pool, POOL_AT[c, "gd"])
                g_.tensor_tensor(gm[0:n, :, 0:n], gm[0:n, :, 0:n], dg[0:n, :, 0:n], ALU.add).then_inc(g_pool, 1)

            pool.wait_ge(c_out, 16 * 3)
            pool.wait_ge(n_dve, N_END)
            decay_columns(0)
            for c in range(TT):
                n = chunk(c)

                def after(eng, *key):
                    s, at_ = {"act": (g_act, ACT_AT), "pe": (g_pe, PE_AT), "dve": (g_dve, DVE_AT)}[eng]
                    if key[0] >= 0:
                        pool.wait_ge(s, at_[key])

                def hs(g):
                    return slice(4 * g, 4 * g + 4)
                for g in G2:
                    after("act", c, "dr", g)
                    keep(DR[0:n, hs(g), 0:n], DR[0:n, hs(g), 0:n], [[0, 4], [-1, n]], 0, 1, ALU.is_gt).then_inc(g_pool, 1)
                for g in G2:
                    after("act", c, "dc", g)
                    keep(DC[0:n, hs(g), 0:n], DC[0:n, hs(g), 0:n], [[0, 4], [1, n]], 0, -1).then_inc(g_pool, 1)
                for j, s in enumerate(LEVELS[c]):
                    for g in G2:
                        if j == 0:
                            after("dve", c, "A", g)
                            if c:
                                after("dve", c - 1, "ss")
                        elif j == 2:
                            after("dve", c, "T1", g)
                            after("pe", c, "lt", g)
                        elif j >= 3:
                            after("pe", c, "q1", LEVELS[c][j - 2], g)
                        elif j == 1 and c:
                            after("pe", c - 1, "q1", LEVELS[c - 1][-1], g)
                        g_.tensor_tensor(Lm[j % 2][0:n, hs(g), 0:n], DR[0:n, hs(g), 0:n],
                                         lvl[0:n, j, 0:n].unsqueeze(1).to_broadcast([n, 4, n]), ALU.mult)\
                            .then_inc(g_pool, 1)
                if c + 1 < TT:
                    decay_columns(c + 1)
                after("dve", c, "o", 0)
                after("dve", c, "o", 1)
                g_.tensor_tensor(Lm[0][0:n, :, :], Q1[0:n, :, :], Q1[0:n, :, :], ALU.mult).then_inc(g_pool, 1)
            def masked_rows(j):
                pool.wait_ge(t_dve, T_ROWS)
                if j:
                    pool.wait_ge(t_pe, 4 + 4 * j)
                g_.tensor_tensor(ksel[:, :, :], krow[:, :].unsqueeze(1).to_broadcast([64, 16, P]),
                                 per_head(ident[64:P, 64 + 16 * j:64 + 16 * j + 16], P), ALU.mult).then_inc(t_pool, 1)
            for j in range(KT):
                pool.wait_ge(act_read, READ_COUNT[T_SEG + 5 * KT + j])
                g_.tensor_copy(zsv[:, j, :], ztmp[:, j % 2, LP:TOKENS]).then_inc(zs_cp, 1)
                g_.tensor_tensor(oaT[:, j, 0:LP], oaT[:, j, 0:LP], ztmp[:, j % 2, 0:LP], ALU.mult).then_inc(z_done, 1)
                if 3 <= j < 7:
                    pool.wait_ge(z_done, j + 1)
                    masked_rows(j - 3)
                    pool.wait_ge(t_pool, j - 2)
            pool.wait_ge(t_act, 3)
            pool.wait_ge(zs_cp, KT)
            g_.tensor_tensor(oaT[:, :, LP:TOKENS], oaT[:, :, LP:TOKENS], zsv[:, :, :], ALU.mult).then_inc(zs_done, 1)

            for k, b in enumerate(V_POOL):
                acc = vacc[:, b % 2, :].rearrange("p (h j) -> p h j", h=H)
                for p in range(PAGES):
                    n = 4 - k
                    page = prings[k][:, p % n, :].rearrange("p (h j) -> p h j", h=H)
                    w = per_head(dw[:, b % 2, p * H:p * H + H], P)
                    pool.wait_ge(p_in[k][p % n], 16 * (p // n + 1))
                    if p == 0:
                        pool.wait_ge(d_w, b + 1)
                        if k == 1:
                            pool.wait_ge(v_sum, b - 1)
                        g_.tensor_tensor(acc, page, w, ALU.mult).then_inc(p_used, 1)
                    else:
                        g_.tensor_tensor(page, page, w, ALU.mult).then_inc(p_mul, 1)
                        pool.wait_ge(p_mul, k * (PAGES - 1) + p)
                        pool.wait_ge(p_used, k * PAGES + p)
                        g_.tensor_tensor(acc, acc, page, ALU.add).then_inc(p_used, 1)


NPHYS = 160
NCONST = 12
AB_X, AB_G, AB_B, AB_END, AB_DEND = 4, 6, 5, 10, 6
N_ROWS, N_END = 3, 13
T_VN, T_OSQ, T_ROWS, T_ON, T_S0 = 5, 9, 11, 13, 13
T_PE_END = 20
_VIEWS = {
    "x_prompt": (SEQ, D), "x_sample": (DB, D), "cache_k": (NPHYS, PAGE, D), "cache_v": (NPHYS, PAGE, D),
    "state_rec": (DB, H, P, P), "state_conv": (DB * 3, 3 * D), "page_table": (1, DB * PAGES),
    "meta_tokens": (META, D), "norm_mix": (KT, P), "w_in": (D, 9232), "conv_w": (CW * NQKV, P),
    "a_log": (1, H), "dt_bias": (1, H), "gdn_norm": (1, P), "sb_bias": (1, H), "w_pa": (D, D), "w_pb": (D, D),
    "w_o": (D, D), "norm_ffn": (KT, P), "w_ffn_in": (D, 2 * D_FF), "w_ffn_out": (D_FF, D), "norm_final": (KT, P),
}
_OUTS = [("y_prompt", (SEQ, D), (1, SEQ, D)), ("y_sample", (DB, D), (DB, 1, D)),
         ("k_prompt", (LP, D), (1, 1, LP, H, P)), ("v_prompt", (LP, D), (1, 1, LP, H, P)),
         ("k_sample", (DB, D), (1, DB, 1, H, P)), ("v_sample", (DB, D), (1, DB, 1, H, P)),
         ("rec_prompt", (H, P, P), (1, 1, H, P, P)), ("rec_sample", (DB, H, P, P), (1, DB, H, P, P)),
         ("conv_prompt", (3, 3 * D), (1, 1, 3, 3 * D)), ("conv_sample", (DB, 3, 3 * D), (1, DB, 3, 3 * D))]


def kernel(**inputs):
    import numpy as _np
    import concourse.bacc as _bacc
    from concourse.bass_utils import run_bass_kernel_spmd as _run

    nc = _bacc.Bacc("TRN2", target_bir_lowering=False, num_devices=1)
    arrays, io = {}, {}
    for name, shape in _VIEWS.items():
        a = _np.ascontiguousarray(inputs[name]).reshape(shape)
        arrays[f"in_{name}"] = a
        io[name] = nc.dram_tensor(f"in_{name}", shape, mybir.dt.from_np(a.dtype), kind="ExternalInput").ap()
    io["state_conv3"] = io["state_conv"].rearrange("(b i) n -> b i n", i=3)
    for name, shape, _ in _OUTS:
        io[name] = nc.dram_tensor(f"out_{name}", shape, F32, kind="ExternalOutput").ap()
    build(nc, io)
    r = _run(nc, [arrays], core_ids=[0])
    return tuple(r.results[0][f"out_{name}"].reshape(whole) for name, _, whole in _OUTS)
```
